# Optimizing a Trainium2 kernel written in Bass

```python
import math
import jax, jax.numpy as jnp
from jax import lax
import numpy as np
import jax
import jax.numpy as jnp

D_MODEL = 1024
BATCH = 1
SEQ = 256
DEPTH = 2

N_MIXERS = 3
N_HEADS = 8
HEAD_DIM = D_MODEL // N_HEADS
ROT_DIM = HEAD_DIM // 4
ROPE_THETA = 500000.0
MOBA_BLOCK = 256
MOBA_TOPK = 3
Q_CHUNK = 16
POOL_WINDOWS = (2, 4, 8, 16)
N_POOL_GROUPS = len(POOL_WINDOWS)
POOL_GROUP_DIM = D_MODEL // N_POOL_GROUPS
CONV_WIDTH = 3
D_FF = 4 * D_MODEL
NORM_EPS = 1e-6
NEG_INF = -1e30


def rms_norm(x, g):
    xf = x.astype(jnp.float32)
    y = xf * lax.rsqrt(jnp.mean(xf * xf, axis=-1, keepdims=True) + NORM_EPS)
    return (y * g.astype(jnp.float32)).astype(x.dtype)

def rope_tables(positions):
    inv_freq = ROPE_THETA ** (-jnp.arange(0, ROT_DIM, 2, dtype=jnp.float32) / ROT_DIM)
    ang = positions.astype(jnp.float32)[..., None] * inv_freq
    return jnp.cos(ang)[:, None], jnp.sin(ang)[:, None]

def apply_partial_rope(t, cos, sin):
    half = ROT_DIM // 2
    rot = t[..., :ROT_DIM].astype(jnp.float32)
    x1, x2 = rot[..., :half], rot[..., half:]
    rotated = jnp.concatenate([x1 * cos - x2 * sin, x2 * cos + x1 * sin], axis=-1)
    return jnp.concatenate([rotated.astype(t.dtype), t[..., ROT_DIM:]], axis=-1)

def moba_attention(xn, w_qkv, w_o, cos, sin):
    b, s, _ = xn.shape
    qkv = (xn @ w_qkv).reshape(b, s, 3, N_HEADS, HEAD_DIM)
    q, k, v = [jnp.transpose(qkv[:, :, i], (0, 2, 1, 3)) for i in range(3)]
    q = apply_partial_rope(q, cos, sin)
    k = apply_partial_rope(k, cos, sin)

    n_blocks = -(-s // MOBA_BLOCK)
    top_k = min(MOBA_TOPK, n_blocks)
    pad = n_blocks * MOBA_BLOCK - s
    kp = jnp.pad(k, ((0, 0), (0, 0), (0, pad), (0, 0)))
    vp = jnp.pad(v, ((0, 0), (0, 0), (0, pad), (0, 0)))
    kb = kp.reshape(b, N_HEADS, n_blocks, MOBA_BLOCK, HEAD_DIM)
    vb = vp.reshape(b, N_HEADS, n_blocks, MOBA_BLOCK, HEAD_DIM)
    k_mean = jnp.mean(kb.astype(jnp.float32), axis=3)

    scale = 1.0 / math.sqrt(HEAD_DIM)
    bi = jnp.arange(b)[:, None, None, None]
    hi = jnp.arange(N_HEADS)[None, :, None, None]
    blk_ids = jnp.arange(n_blocks)

    def chunk(c):
        start = c * Q_CHUNK
        qc = lax.dynamic_slice_in_dim(q, start, Q_CHUNK, axis=2)
        qpos = start + jnp.arange(Q_CHUNK)
        qblk = start // MOBA_BLOCK
        gate = jnp.einsum('bhqd,bhnd->bhqn', qc.astype(jnp.float32), k_mean)
        gate = jnp.where(blk_ids < qblk, gate, NEG_INF)
        _, sel = lax.top_k(gate, top_k)
        sel_valid = sel < qblk
        k_sel = kb[bi, hi, sel]
        v_sel = vb[bi, hi, sel]
        s_sel = jnp.einsum('bhqd,bhqnkd->bhqnk', qc, k_sel).astype(jnp.float32) * scale
        s_sel = jnp.where(sel_valid[..., None], s_sel, NEG_INF)
        s_sel = s_sel.reshape(b, N_HEADS, Q_CHUNK, top_k * MOBA_BLOCK)
        k_own = lax.dynamic_slice_in_dim(kp, qblk * MOBA_BLOCK, MOBA_BLOCK, axis=2)
        v_own = lax.dynamic_slice_in_dim(vp, qblk * MOBA_BLOCK, MOBA_BLOCK, axis=2)
        s_own = jnp.einsum('bhqd,bhkd->bhqk', qc, k_own).astype(jnp.float32) * scale
        kpos = qblk * MOBA_BLOCK + jnp.arange(MOBA_BLOCK)
        s_own = jnp.where(kpos[None, :] <= qpos[:, None], s_own, NEG_INF)
        p = jax.nn.softmax(jnp.concatenate([s_sel, s_own], axis=-1), axis=-1)
        p_sel = p[..., :top_k * MOBA_BLOCK].reshape(
            b, N_HEADS, Q_CHUNK, top_k, MOBA_BLOCK).astype(v.dtype)
        p_own = p[..., top_k * MOBA_BLOCK:].astype(v.dtype)
        return (jnp.einsum('bhqnk,bhqnkd->bhqd', p_sel, v_sel)
                + jnp.einsum('bhqk,bhkd->bhqd', p_own, v_own))

    outs = lax.map(chunk, jnp.arange(s // Q_CHUNK))
    out = jnp.transpose(outs, (1, 0, 3, 2, 4)).reshape(b, s, D_MODEL)
    return out @ w_o

def pool_mixer(xn, w_groups, ls_scale):
    b, s, _ = xn.shape
    xf = xn.astype(jnp.float32).reshape(b, s, N_POOL_GROUPS, POOL_GROUP_DIM)
    cs = jnp.concatenate([jnp.zeros((b, 1, N_POOL_GROUPS, POOL_GROUP_DIM), jnp.float32),
                          jnp.cumsum(xf, axis=1)], axis=1)
    t = jnp.arange(s)
    pooled = []
    for g, w in enumerate(POOL_WINDOWS):
        c = cs[:, :, g]
        lower = jnp.pad(c[:, :s - w + 1], ((0, 0), (w - 1, 0), (0, 0)))
        count = jnp.minimum(t + 1, w).astype(jnp.float32)[None, :, None]
        pooled.append((c[:, 1:] - lower) / count)
    pooled = jnp.stack(pooled, axis=2) - xf
    y = jnp.einsum('bsgc,gcd->bsgd', pooled.astype(xn.dtype), w_groups)
    return y.reshape(b, s, D_MODEL) * ls_scale

def short_conv_mixer(xn, w_in, conv_w, w_out):
    u = xn @ w_in
    gate_b, gate_c, h = jnp.split(u, 3, axis=-1)
    z = gate_c * h
    zc = lax.conv_general_dilated(
        z, conv_w[:, None, :].astype(z.dtype), window_strides=(1,),
        padding=[(CONV_WIDTH - 1, 0)], dimension_numbers=('NWC', 'WIO', 'NWC'),
        feature_group_count=D_MODEL)
    return (gate_b * zc) @ w_out

def squared_relu_mlp(x, w_up, w_down):
    h = jax.nn.relu(x @ w_up)
    return (h * h) @ w_down

def first_inputs(seed: int = 0) -> dict:
    key = jax.random.key(seed)
    ks = jax.random.split(key, 16)
    n_attn = len(range(0, DEPTH, N_MIXERS))
    n_pool = len(range(1, DEPTH, N_MIXERS))
    n_conv = len(range(2, DEPTH, N_MIXERS))
    f32 = jnp.float32

    def nrm(k, shape, fan_in):
        return jax.random.normal(k, shape, f32) * (fan_in ** -0.5)

    x = jax.random.normal(ks[0], (BATCH, SEQ, D_MODEL), f32)
    positions = jnp.broadcast_to(jnp.arange(SEQ, dtype=jnp.int32), (BATCH, SEQ))
    norm_mix = 1.0 + 0.02 * jax.random.normal(ks[1], (DEPTH, D_MODEL), f32)
    norm_mlp = 1.0 + 0.02 * jax.random.normal(ks[2], (DEPTH, D_MODEL), f32)
    attn_w_qkv = nrm(ks[3], (n_attn, D_MODEL, 3 * D_MODEL), D_MODEL)
    attn_w_o = nrm(ks[4], (n_attn, D_MODEL, D_MODEL), D_MODEL)
    pool_w = nrm(ks[5], (n_pool, N_POOL_GROUPS, POOL_GROUP_DIM, POOL_GROUP_DIM), POOL_GROUP_DIM)
    pool_scale = 1.0 + 0.1 * jax.random.normal(ks[6], (n_pool, D_MODEL), f32)
    conv_w_in = nrm(ks[7], (n_conv, D_MODEL, 3 * D_MODEL), D_MODEL)
    conv_w = nrm(ks[8], (n_conv, CONV_WIDTH, D_MODEL), CONV_WIDTH)
    conv_w_out = nrm(ks[9], (n_conv, D_MODEL, D_MODEL), D_MODEL)
    mlp_w_up = nrm(ks[10], (DEPTH, D_MODEL, D_FF), D_MODEL)
    mlp_w_down = nrm(ks[11], (DEPTH, D_FF, D_MODEL), D_FF)
    norm_final = 1.0 + 0.02 * jax.random.normal(ks[12], (D_MODEL,), f32)
    return {"x": x, "positions": positions, "norm_mix": norm_mix, "norm_mlp": norm_mlp,
            "attn_w_qkv": attn_w_qkv, "attn_w_o": attn_w_o,
            "pool_w": pool_w, "pool_scale": pool_scale,
            "conv_w_in": conv_w_in, "conv_w": conv_w, "conv_w_out": conv_w_out,
            "mlp_w_up": mlp_w_up, "mlp_w_down": mlp_w_down, "norm_final": norm_final}

def first_block(x, positions, norm_mix, norm_mlp, attn_w_qkv, attn_w_o, pool_w, pool_scale,
              conv_w_in, conv_w, conv_w_out, mlp_w_up, mlp_w_down, norm_final):
    cos, sin = rope_tables(positions)
    i_attn = i_pool = i_conv = 0
    for i in range(DEPTH):
        xn = rms_norm(x, norm_mix[i])
        kind = i % N_MIXERS
        if kind == 0:
            y = moba_attention(xn, attn_w_qkv[i_attn], attn_w_o[i_attn], cos, sin)
            i_attn += 1
        elif kind == 1:
            y = pool_mixer(xn, pool_w[i_pool], pool_scale[i_pool])
            i_pool += 1
        else:
            y = short_conv_mixer(xn, conv_w_in[i_conv], conv_w[i_conv], conv_w_out[i_conv])
            i_conv += 1
        x = x + y
        x = x + squared_relu_mlp(rms_norm(x, norm_mlp[i]), mlp_w_up[i], mlp_w_down[i])
    return rms_norm(x, norm_final)


DEPTH_2 = 1

N_MEM = 256
SSD_EXPAND = 2
D_INNER = SSD_EXPAND * D_MODEL
SSD_HEAD_DIM = 64
SSD_HEADS = D_INNER // SSD_HEAD_DIM
SSD_GROUPS = 4
SSD_STATE = 128
CONV_WIDTH_2 = 4
SSD_CHUNK = 128
XBC_DIM = D_INNER + 2 * SSD_GROUPS * SSD_STATE
MLA_HEADS = 16
QK_NOPE_DIM = 64
QK_ROPE_DIM = 32
QK_HEAD_DIM = QK_NOPE_DIM + QK_ROPE_DIM
V_HEAD_DIM = 64
Q_LORA_RANK = 384
KV_LORA_RANK = 256
ROPE_THETA_2 = 10000.0
Q_BLOCK = 128
XA_HEADS = 4
XA_HEAD_DIM = D_MODEL // XA_HEADS
N_EXPERT_GROUPS = 4
EXPERTS_PER_GROUP = 8
N_EXPERTS = N_EXPERT_GROUPS * EXPERTS_PER_GROUP
TOP_K = 2
D_EXPERT = 256
RMS_EPS = 1e-6

IN_SPLITS = (D_INNER, XBC_DIM, SSD_HEADS, Q_LORA_RANK, KV_LORA_RANK, QK_ROPE_DIM, D_MODEL, D_MODEL)
IN_PROJ_DIM = D_INNER + XBC_DIM + SSD_HEADS + Q_LORA_RANK + KV_LORA_RANK + QK_ROPE_DIM + 2 * D_MODEL


def rms_norm_2(x, gain):
    xf = x.astype(jnp.float32)
    xf = xf * lax.rsqrt(jnp.mean(xf * xf, axis=-1, keepdims=True) + RMS_EPS)
    return xf.astype(x.dtype) * gain

def split_cols(x, sizes):
    offs = np.cumsum(np.array(sizes))[:-1].tolist()
    return jnp.split(x, offs, axis=-1)

def causal_depthwise_conv(x, w, b):
    k, c = w.shape
    y = lax.conv_general_dilated(x, w[:, None, :], window_strides=(1,), padding=[(k - 1, 0)],
                                 dimension_numbers=('NWC', 'WIO', 'NWC'), feature_group_count=c)
    return y + b

def apply_rope(x, positions):
    half = x.shape[-1] // 2
    inv_freq = ROPE_THETA_2 ** (-jnp.arange(half, dtype=jnp.float32) / half)
    ang = positions.astype(jnp.float32)[..., None] * inv_freq
    cos = jnp.cos(ang)[:, :, None, :]
    sin = jnp.sin(ang)[:, :, None, :]
    xf = x.astype(jnp.float32)
    x1, x2 = xf[..., :half], xf[..., half:]
    return jnp.concatenate([x1 * cos - x2 * sin, x2 * cos + x1 * sin], axis=-1).astype(x.dtype)

def ssd_chunked_scan(xh, dt, a, bm, cm):
    b, s, h, p = xh.shape
    g, n = bm.shape[2], bm.shape[3]
    r = h // g
    nc, l = s // SSD_CHUNK, SSD_CHUNK
    x_dt = (xh.astype(jnp.float32) * dt[..., None]).reshape(b, nc, l, g, r, p)
    a_dt = (dt * a).reshape(b, nc, l, g, r).transpose(0, 3, 4, 1, 2)
    bc = bm.astype(jnp.float32).reshape(b, nc, l, g, n)
    cc = cm.astype(jnp.float32).reshape(b, nc, l, g, n)
    a_cum = jnp.cumsum(a_dt, axis=-1)
    causal = jnp.tril(jnp.ones((l, l), dtype=bool))
    seg = a_cum[..., :, None] - a_cum[..., None, :]
    decay_in = jnp.exp(jnp.where(causal, seg, -jnp.inf))
    cb = jnp.einsum('bclgn,bcsgn->bcgls', cc, bc)
    y_diag = jnp.einsum('bcgls,bgrcls,bcsgrp->bclgrp', cb, decay_in, x_dt)
    decay_to_end = jnp.exp(a_cum[..., -1:] - a_cum)
    chunk_states = jnp.einsum('bclgn,bgrcl,bclgrp->bcgrpn', bc, decay_to_end, x_dt)
    chunk_decay = jnp.exp(a_cum[..., -1])

    def step(state, inp):
        st, dec = inp
        return state * dec[..., None, None] + st, state

    init = jnp.zeros((b, g, r, p, n), jnp.float32)
    _, prev_states = lax.scan(step, init, (jnp.moveaxis(chunk_states, 1, 0), jnp.moveaxis(chunk_decay, -1, 0)))
    prev_states = jnp.moveaxis(prev_states, 0, 1)
    y_off = jnp.einsum('bclgn,bcgrpn,bgrcl->bclgrp', cc, prev_states, jnp.exp(a_cum))
    return (y_diag + y_off).reshape(b, s, h, p)

def ssd_branch(z, xbc, dt_raw, conv_w, conv_b, dt_bias, a_log, d_skip, ssd_norm):
    b, s, _ = z.shape
    xbc = jax.nn.silu(causal_depthwise_conv(xbc, conv_w, conv_b))
    xs, bm, cm = split_cols(xbc, (D_INNER, SSD_GROUPS * SSD_STATE, SSD_GROUPS * SSD_STATE))
    xh = xs.reshape(b, s, SSD_HEADS, SSD_HEAD_DIM)
    bm = bm.reshape(b, s, SSD_GROUPS, SSD_STATE)
    cm = cm.reshape(b, s, SSD_GROUPS, SSD_STATE)
    dt = jax.nn.softplus(dt_raw.astype(jnp.float32) + dt_bias.astype(jnp.float32))
    a = -jnp.exp(a_log.astype(jnp.float32))
    y = ssd_chunked_scan(xh, dt, a, bm, cm)
    y = y + d_skip.astype(jnp.float32)[:, None] * xh.astype(jnp.float32)
    y = y.reshape(b, s, D_INNER) * jax.nn.silu(z.astype(jnp.float32))
    y = y.reshape(b, s, SSD_GROUPS, D_INNER // SSD_GROUPS)
    y = y * lax.rsqrt(jnp.mean(y * y, axis=-1, keepdims=True) + RMS_EPS)
    return y.reshape(b, s, D_INNER).astype(z.dtype) * ssd_norm

def causal_block_attention(q, k, v, scale):
    b, s, h, dq = q.shape
    nb = s // Q_BLOCK
    qb = jnp.moveaxis(q.reshape(b, nb, Q_BLOCK, h, dq), 1, 0)
    kpos = jnp.arange(s)

    def one_block(args):
        i, qi = args
        sc = jnp.einsum('bqhd,bkhd->bhqk', qi, k).astype(jnp.float32) * scale
        qpos = i * Q_BLOCK + jnp.arange(Q_BLOCK)
        sc = jnp.where(kpos[None, :] <= qpos[:, None], sc, -jnp.inf)
        pr = jax.nn.softmax(sc, axis=-1).astype(v.dtype)
        return jnp.einsum('bhqk,bkhd->bqhd', pr, v)

    out = lax.map(one_block, (jnp.arange(nb), qb))
    return jnp.moveaxis(out, 0, 1).reshape(b, s, h, v.shape[-1])

def mla_branch(q_a, c_kv, k_rope, positions, q_a_norm, w_q_b, kv_a_norm, w_kv_b):
    b, s, _ = q_a.shape
    q = (rms_norm_2(q_a, q_a_norm) @ w_q_b).reshape(b, s, MLA_HEADS, QK_HEAD_DIM)
    kv = (rms_norm_2(c_kv, kv_a_norm) @ w_kv_b).reshape(b, s, MLA_HEADS, QK_NOPE_DIM + V_HEAD_DIM)
    q_nope, q_pe = q[..., :QK_NOPE_DIM], q[..., QK_NOPE_DIM:]
    k_nope, v = kv[..., :QK_NOPE_DIM], kv[..., QK_NOPE_DIM:]
    q_pe = apply_rope(q_pe, positions)
    k_pe = apply_rope(k_rope[:, :, None, :], positions)
    q = jnp.concatenate([q_nope, q_pe], axis=-1)
    k = jnp.concatenate([k_nope, jnp.broadcast_to(k_pe, (b, s, MLA_HEADS, QK_ROPE_DIM))], axis=-1)
    o = causal_block_attention(q, k, v, QK_HEAD_DIM ** -0.5)
    return o.reshape(b, s, MLA_HEADS * V_HEAD_DIM)

def memory_cross_attention(h, mem, w_xq, w_xkv, w_xo):
    b, s, _ = h.shape
    m = mem.shape[1]
    q = (h @ w_xq).reshape(b, s, XA_HEADS, XA_HEAD_DIM)
    k, v = jnp.split(mem @ w_xkv, 2, axis=-1)
    k = k.reshape(b, m, XA_HEADS, XA_HEAD_DIM)
    v = v.reshape(b, m, XA_HEADS, XA_HEAD_DIM)
    sc = jnp.einsum('bshd,bmhd->bhsm', q, k).astype(jnp.float32) * XA_HEAD_DIM ** -0.5
    pr = jax.nn.softmax(sc, axis=-1).astype(v.dtype)
    o = jnp.einsum('bhsm,bmhd->bshd', pr, v).reshape(b, s, XA_HEADS * XA_HEAD_DIM)
    return o @ w_xo

def hierarchical_moe(h, w_rg, b_rg, w_re, b_re, w_gate, w_up, w_down):
    b, s, d = h.shape
    t = h.reshape(b * s, d)
    g_logits = (t @ w_rg).astype(jnp.float32) + b_rg
    g_prob = jax.nn.softmax(g_logits, axis=-1)
    g_sel = jnp.argmax(g_logits, axis=-1)
    g_w = jnp.take_along_axis(g_prob, g_sel[:, None], axis=1)
    e_logits = ((t @ w_re).astype(jnp.float32) + b_re).reshape(-1, N_EXPERT_GROUPS, EXPERTS_PER_GROUP)
    e_in = jnp.take_along_axis(e_logits, g_sel[:, None, None], axis=1)[:, 0]
    top_v, top_i = lax.top_k(e_in, TOP_K)
    w_top = jax.nn.softmax(top_v, axis=-1) * g_w
    expert_id = g_sel[:, None] * EXPERTS_PER_GROUP + top_i
    combine = jnp.sum(jax.nn.one_hot(expert_id, N_EXPERTS, dtype=jnp.float32) * w_top[..., None], axis=1).astype(t.dtype)
    hg = jnp.einsum('td,edf->tef', t, w_gate)
    hu = jnp.einsum('td,edf->tef', t, w_up)
    act = jax.nn.silu(hg) * hu * combine[:, :, None]
    y = jnp.einsum('tef,efd->td', act, w_down)
    return y.reshape(b, s, d)

def second_inputs(seed: int = 0) -> dict:
    key = jax.random.key(seed)
    ks = iter(jax.random.split(key, 48))
    f32 = jnp.float32
    L = DEPTH_2

    def nrm(shape, fan_in):
        return jax.random.normal(next(ks), shape, f32) * fan_in ** -0.5

    def gain(shape):
        return 1.0 + 0.02 * jax.random.normal(next(ks), shape, f32)

    x = jax.random.normal(next(ks), (BATCH, SEQ, D_MODEL), f32)
    mem = jax.random.normal(next(ks), (BATCH, N_MEM, D_MODEL), f32)
    offset = jax.random.randint(next(ks), (BATCH, 1), 0, 1024, dtype=jnp.int32)
    positions = (offset + jnp.arange(SEQ, dtype=jnp.int32)[None, :]).astype(jnp.int32)
    dt0 = jnp.exp(jax.random.uniform(next(ks), (L, SSD_HEADS), f32, math.log(1e-3), math.log(1e-1)))
    dt_bias = dt0 + jnp.log(-jnp.expm1(-dt0))
    a_log = jnp.log(jax.random.uniform(next(ks), (L, SSD_HEADS), f32, 1.0, 16.0))
    return {
        'x': x,
        'mem': mem,
        'positions': positions,
        'norm_mix': gain((L, D_MODEL)),
        'w_in': nrm((L, D_MODEL, IN_PROJ_DIM), D_MODEL),
        'conv_w': nrm((L, CONV_WIDTH_2, XBC_DIM), CONV_WIDTH_2),
        'conv_b': 0.02 * jax.random.normal(next(ks), (L, XBC_DIM), f32),
        'dt_bias': dt_bias,
        'a_log': a_log,
        'd_skip': 1.0 + 0.1 * jax.random.normal(next(ks), (L, SSD_HEADS), f32),
        'ssd_norm': gain((L, D_INNER)),
        'w_ssd_out': nrm((L, D_INNER, D_MODEL), D_INNER),
        'q_a_norm': gain((L, Q_LORA_RANK)),
        'w_q_b': nrm((L, Q_LORA_RANK, MLA_HEADS * QK_HEAD_DIM), Q_LORA_RANK),
        'kv_a_norm': gain((L, KV_LORA_RANK)),
        'w_kv_b': nrm((L, KV_LORA_RANK, MLA_HEADS * (QK_NOPE_DIM + V_HEAD_DIM)), KV_LORA_RANK),
        'w_mla_out': nrm((L, MLA_HEADS * V_HEAD_DIM, D_MODEL), MLA_HEADS * V_HEAD_DIM),
        'w_o': nrm((L, D_MODEL, D_MODEL), D_MODEL),
        'norm_xattn': gain((L, D_MODEL)),
        'norm_mem': gain((L, D_MODEL)),
        'w_xq': nrm((L, D_MODEL, XA_HEADS * XA_HEAD_DIM), D_MODEL),
        'w_xkv': nrm((L, D_MODEL, 2 * XA_HEADS * XA_HEAD_DIM), D_MODEL),
        'w_xo': nrm((L, XA_HEADS * XA_HEAD_DIM, D_MODEL), XA_HEADS * XA_HEAD_DIM),
        'norm_moe': gain((L, D_MODEL)),
        'w_router_group': nrm((L, D_MODEL, N_EXPERT_GROUPS), D_MODEL),
        'b_router_group': 0.01 * jax.random.normal(next(ks), (L, N_EXPERT_GROUPS), f32),
        'w_router_expert': nrm((L, D_MODEL, N_EXPERTS), D_MODEL),
        'b_router_expert': 0.01 * jax.random.normal(next(ks), (L, N_EXPERTS), f32),
        'w_exp_gate': nrm((L, N_EXPERTS, D_MODEL, D_EXPERT), D_MODEL),
        'w_exp_up': nrm((L, N_EXPERTS, D_MODEL, D_EXPERT), D_MODEL),
        'w_exp_down': nrm((L, N_EXPERTS, D_EXPERT, D_MODEL), D_EXPERT),
        'norm_final': gain((D_MODEL,)),
    }

def second_block(x, mem, positions, norm_mix, w_in, conv_w, conv_b, dt_bias, a_log, d_skip, ssd_norm, w_ssd_out,
              q_a_norm, w_q_b, kv_a_norm, w_kv_b, w_mla_out, w_o, norm_xattn, norm_mem, w_xq, w_xkv, w_xo,
              norm_moe, w_router_group, b_router_group, w_router_expert, b_router_expert,
              w_exp_gate, w_exp_up, w_exp_down, norm_final):
    h = x
    for i in range(DEPTH_2):
        u = rms_norm_2(h, norm_mix[i])
        z, xbc, dt_raw, q_a, c_kv, k_rope, gate_ssd, gate_mla = split_cols(u @ w_in[i], IN_SPLITS)
        y_ssd = ssd_branch(z, xbc, dt_raw, conv_w[i], conv_b[i], dt_bias[i], a_log[i], d_skip[i], ssd_norm[i]) @ w_ssd_out[i]
        y_mla = mla_branch(q_a, c_kv, k_rope, positions, q_a_norm[i], w_q_b[i], kv_a_norm[i], w_kv_b[i]) @ w_mla_out[i]
        merged = jax.nn.sigmoid(gate_ssd) * y_ssd + jax.nn.sigmoid(gate_mla) * y_mla
        h = h + merged @ w_o[i]
        h = h + memory_cross_attention(rms_norm_2(h, norm_xattn[i]), rms_norm_2(mem, norm_mem[i]), w_xq[i], w_xkv[i], w_xo[i])
        h = h + hierarchical_moe(rms_norm_2(h, norm_moe[i]), w_router_group[i], b_router_group[i],
                                 w_router_expert[i], b_router_expert[i], w_exp_gate[i], w_exp_up[i], w_exp_down[i])
    return rms_norm_2(h, norm_final)


def setup_inputs(seed=0):
    out = dict(first_inputs(seed))
    for name, value in second_inputs(seed + 1).items():
        if name != "x":
            out[name + "_2"] = value
    return out


def reference(
    x, positions, norm_mix, norm_mlp, attn_w_qkv, attn_w_o, pool_w, pool_scale, conv_w_in,
    conv_w, conv_w_out, mlp_w_up, mlp_w_down, norm_final, mem_2, positions_2, norm_mix_2,
    w_in_2, conv_w_2, conv_b_2, dt_bias_2, a_log_2, d_skip_2, ssd_norm_2, w_ssd_out_2,
    q_a_norm_2, w_q_b_2, kv_a_norm_2, w_kv_b_2, w_mla_out_2, w_o_2, norm_xattn_2, norm_mem_2,
    w_xq_2, w_xkv_2, w_xo_2, norm_moe_2, w_router_group_2, b_router_group_2, w_router_expert_2,
    b_router_expert_2, w_exp_gate_2, w_exp_up_2, w_exp_down_2, norm_final_2,
):
    x = first_block(
        x, positions, norm_mix, norm_mlp, attn_w_qkv, attn_w_o, pool_w, pool_scale, conv_w_in,
        conv_w, conv_w_out, mlp_w_up, mlp_w_down, norm_final,
    )
    return second_block(
        x, mem_2, positions_2, norm_mix_2, w_in_2, conv_w_2, conv_b_2, dt_bias_2, a_log_2,
        d_skip_2, ssd_norm_2, w_ssd_out_2, q_a_norm_2, w_q_b_2, kv_a_norm_2, w_kv_b_2,
        w_mla_out_2, w_o_2, norm_xattn_2, norm_mem_2, w_xq_2, w_xkv_2, w_xo_2, norm_moe_2,
        w_router_group_2, b_router_group_2, w_router_expert_2, b_router_expert_2, w_exp_gate_2,
        w_exp_up_2, w_exp_down_2, norm_final_2,
    )


_drawn_inputs = setup_inputs


def setup_inputs(seed=0):
    import zlib

    import numpy as np

    out = dict(_drawn_inputs(seed))
    spreads = {}
    factors = {'conv_b_2': 2.972,
     'ssd_norm_2': 3.568,
     'q_a_norm_2': 5.51,
     'kv_a_norm_2': 8.0,
     'norm_xattn_2': 8.0,
     'norm_mem_2': 8.0,
     'norm_moe_2': 3.189,
     'b_router_group_2': 6.037,
     'b_router_expert_2': 7.08,
     'norm_final_2': 2.809}
    for name, (base, spread) in spreads.items():
        noise = np.random.default_rng([zlib.crc32(name.encode()), seed]).standard_normal(out[name].shape)
        drawn = base * np.exp(spread * noise) if base else spread * noise
        out[name] = jnp.asarray(drawn.astype(out[name].dtype))
    for name, factor in factors.items():
        out[name] = (out[name] * factor).astype(out[name].dtype)
    return out
```

```python
import math
from contextlib import ExitStack

import numpy as np

import concourse.bass as bass
from concourse import mybir

F32 = mybir.dt.float32
BF16 = mybir.dt.bfloat16
I32 = mybir.dt.int32
ALU = mybir.AluOpType
ACT = mybir.ActivationFunctionType
AX_X = mybir.AxisListType.X

P = 128
TOK = 256
TB = TOK // P
D = 1024
KT = D // P
EPS = 1e-6
NEG = -1e30

H1 = 8
ROT = 32
DFF = 4096
FC = DFF // TOK
WINDOWS = (2, 4, 8, 16)

DIN = 2048
ZT = DIN // P
NG, NST = 4, 128
SH = 32
HPG = SH // NG
CONV = 4
XBC = DIN + 2 * NG * NST
MH, QK, NOPE, VH = 16, 96, 64, 64
QLR, KLR = 384, 256
XH = 4
EG, EPG = 4, 8
NE = EG * EPG
DE = 256
O_Z, O_XBC, O_DT = 0, DIN, DIN + XBC
O_QA = O_DT + SH
O_KV = O_QA + QLR
O_KR = O_KV + KLR
O_GS = O_KR + ROT
O_GM = O_GS + D

SLOTS = 8
SLOT = 2048

C_ID, C_ONE, C_MASK, C_CAP, C_ROT, C_INVF, C_IOTA, C_N = 0, 128, 256, 640, 768, 800, 801, 812

ROWS_A = [("norm_mix", 16), ("norm_mlp", 16), ("pool_scale", 8), ("norm_final", 8), ("norm_mix_2", 8),
          ("norm_xattn_2", 8), ("norm_mem_2", 8), ("norm_moe_2", 8), ("norm_final_2", 8),
          ("q_a_norm_2", 3), ("kv_a_norm_2", 2), ("ssd_norm_2", 16)]
ROWS_B = [("conv_w_2", CONV * XBC // P), ("conv_b_2", XBC // P)]
COL = {}
for _first, _rows in ((0, ROWS_A), (P, ROWS_B)):
    for _name, _n in _rows:
        COL[_name] = _first
        _first += _n
N_A = sum(n for _, n in ROWS_A)
N_B = sum(n for _, n in ROWS_B)

A_QK, A_V1, A_O1, A_BAND = 0, 4096, 6144, 8192
A_POOLZ = 0
A_ZS, A_XS, A_BC, A_XN, A_GATE = 0, 4096, 8192, 10240, 14336
A_QA, A_KV, A_E, A_EA, A_XW, A_ST, A_BN = 18432, 19200, 19712, 21760, 22784, 23296, 23808
A_CONV = 19712
A_QH, A_KH, A_VH, A_OM = 4096, 8192, 12288, 0
A_XQ, A_XK, A_XV, A_XO = 0, 2048, 4096, 6144
A_COMB, A_RT = 0, 8192
A_HID = 19712
A_SG = A_HID + 1024
A_OUT = 14336
A_P, A_PT, A_MEM = 19712, 21248, 8192
ARENA = 23936


def const_array():
    c = np.zeros((P, C_N), np.float32)
    c[:, C_ID:C_ID + P] = np.eye(P)
    c[:, C_ONE:C_ONE + P] = 1.0
    i = np.arange(P)
    tri = np.where(i[None, :] <= i[:, None], 0.0, NEG)
    c[:, C_MASK:C_MASK + P] = tri
    c[:, C_MASK + 2 * P:C_MASK + 3 * P] = tri
    c[:, C_CAP:C_CAP + P] = np.where(i[None, :] >= i[:, None], 0.0, NEG)
    h = ROT // 2
    for base in (0, 64):
        for j in range(h):
            c[base + j + h, C_ROT + j] = -1.0
            c[base + j, C_ROT + j + h] = 1.0
    f = np.float32
    f1 = f(500000.0) ** (-np.arange(0, ROT, 2, dtype=f) / f(ROT))
    f2 = f(10000.0) ** (-np.arange(h, dtype=f) / f(h))
    for base, fr in ((0, f1), (64, f2)):
        c[base:base + ROT, C_INVF] = np.tile(fr.astype(f), 2)
    c[:, C_IOTA:C_IOTA + EPG] = np.arange(EPG)
    return c


def band_array():
    b = np.zeros((TOK, len(WINDOWS), TOK), np.float32)
    for g, w in enumerate(WINDOWS):
        for t in range(TOK):
            lo = max(0, t - w + 1)
            b[lo:t + 1, g, t] = np.float32(1.0) / np.float32(t + 1 - lo)
            b[t, g, t] -= np.float32(1.0)
    return b


class Counts:

    def __init__(self):
        self.loads, self.fills, self.tenants = {}, {}, {}
        self.slot_loads = [0] * SLOTS
        self.bank_fills = [0] * 8
        self.next_slot = 0
        self.downs = 0

    def load(self, key, freed_by, slot=None):
        slot = self.next_slot % SLOTS if slot is None else slot
        self.slot_loads[slot] += 1
        self.loads[key] = (slot, self.slot_loads[slot], self.tenants.get(slot))
        self.tenants[slot] = freed_by
        self.next_slot = slot + 1

    def fill(self, bank, *key):
        self.bank_fills[bank] += 1
        self.fills[key] = (bank, self.bank_fills[bank])

    def fill_each(self, stage, n, banks):
        for j in range(n):
            self.fill(banks[j % len(banks)], stage, j)

    def attention(self, first, heads, pair):
        for i in range(heads + 3):
            if i < heads:
                self.fill(i % 2, "S", first + i)
            if 2 <= i < heads + 2:
                self.fill(2 + i % 2, "T", first + i - 2)
            if i >= 3 and (i - 3) % pair == 0:
                self.fill(4 + (i - 3) // pair % 2, "O", first + i - 3)

    def mlp(self, i):
        self.fill(0, "norm", 2 * i + 1)
        stage, u = f"mlp{i}", self.bank_fills[0:2]
        self.fills[stage, "first"] = (tuple(u), self.downs)
        self.bank_fills[0] += FC // 2
        self.bank_fills[1] += FC // 2
        self.fill_each(stage + "y", 4, (4, 5, 6, 7))
        for n in range(FC):
            last = n >= FC - 4
            slot = 2 * (n % 4)
            up = ("bank", n % 2, u[n % 2] + n // 2 + 1) if n < 4 or last else None
            down = ("down", self.downs + n + 1) if n < FC - 1 else (stage + "y", 3)
            self.load((stage, "up", n), up, slot)
            self.load((stage, "down", n), down, slot + 1)
        self.downs += FC - 1

    def moe(self):
        u = self.bank_fills[0:4]
        self.fills["moe", "first"] = (tuple(u), self.downs)
        for b in range(4):
            self.bank_fills[b] += NE // 2
        self.fill_each("moey", 4, (4, 5, 6, 7))
        for n in range(2):
            self.load(("moe", "gate", n), None, 3 * n)
            self.load(("moe", "up", n), None, 3 * n + 1)
            self.load(("moe", "down", n), None, 3 * n + 2)


def plan():
    c = Counts()
    c.fill(0, "cols", 0)
    c.fill_each("xT", 4, (1, 2, 3, 4))
    c.fill(0, "norm", 0)
    for j in range(12):
        c.load(("qkv", j), ("qk", j) if j < 8 else ("v1", j - 8))
    for j in range(8):
        c.fill(j % 2, "qk", j)
        c.fill(2 + j % 2, "rope1", j)
    c.fill_each("v1", 4, (0, 1))
    c.attention(0, H1, 1)
    for j in range(4):
        c.load(("wo1", j), ("wo1", j))
    c.fill_each("wo1", 4, (6, 7))
    c.mlp(0)
    c.fill(0, "norm", 2)
    c.load(("pool", 0), ("pooly", 3), 7)
    c.fill_each("poolz", 4, (0, 1))
    c.fill_each("pooly", 4, (2, 3))
    c.mlp(1)
    c.fill(0, "norm", 4)
    c.fill(0, "norm", 5)
    c.fill_each("small", 4, (0, 1))
    c.fill(4, "ropek", 0)
    c.fill_each("xbc", 12, (2, 3))
    c.fill(0, "norm", 6)
    c.fill(1, "norm", 7)
    c.fill(0, "dtT", 0)
    c.fill_each("z", 8, (4, 5))
    c.fill_each("gates", 8, (6, 7))
    for j in range(32):
        c.load(("win", j), ("small", j) if j < 4 else ("xbc", j - 4) if j < 16 else ("z", j - 16) if j < 24
               else ("gates", j - 24))
    for g in range(NG):
        c.fill(0, "cb", g)
        c.fill(1, "bn", g)
        c.fill(2, "xsn", g, 0)
        c.fill(3, "xsn", g, 1)
        for q in range(4):
            c.fill(4 + q, "acum", g, q)
        c.fill(1, "state", g)
        c.fill(2, "y", g, 0)
        c.fill(3, "y", g, 1)
        c.fill(0, "norm", 10 + g)
    for j in range(8):
        c.load(("sout", j), ("down", c.downs + j + 1) if j < 7 else ("souty", 3))
    c.fills["sout", "first"] = (None, c.downs)
    c.downs += 7
    c.fill_each("souty", 4, (4, 5, 6, 7))
    for j in range(4):
        c.load(("qb", j), ("qh", 2 * j + 1))
    for j in range(8):
        c.fill(j % 2, "qh", j)
        c.fill(2 + j % 2, "rope2", j)
    for j in range(2):
        c.load(("kvb", j), ("vh", 2 * j + 1))
    c.fill_each("kh", 8, (0, 1))
    c.fill_each("vh", 4, (2, 3))
    c.attention(H1, MH, 2)
    for stage, n, banks in (("mout", 4, (6, 7)), ("wo2", 4, (4, 5))):
        for j in range(n):
            c.load((stage, j), (stage, j))
        c.fill_each(stage, n, banks)
    c.fill_each("memT", 4, (0, 1, 2, 3))
    c.fill(0, "norm", 8)
    c.fill(0, "norm", 14)
    for j in range(8):
        c.load(("xkv", j), ("xk", j) if j < 4 else ("xv", j - 4))
    for j in range(4):
        c.load(("xq", j), ("xq", j))
    c.fill_each("xq", 4, (1, 2))
    c.fill_each("xk", 4, (3, 4))
    c.fill_each("xv", 4, (5, 6))
    c.attention(H1 + MH, XH, 1)
    for j in range(4):
        c.load(("xo", j), ("xo", j))
    c.fill_each("xo", 4, (6, 7))
    c.fill(0, "norm", 15)
    c.fill(1, "logits", 0)
    c.fill(1, "combT", 0)
    c.moe()
    c.fill(0, "norm", 16)
    c.fill_each("outT", 4, (1, 2, 3, 0))
    return c


def build_two_blocks(nc, a, out):
    c = plan()
    W, FILL = c.loads, c.fills

    with ExitStack() as ctx:
        def sb(name, shape, dt=F32):
            return ctx.enter_context(nc.sbuf_tensor(name, shape, dt))

        def sem(name):
            return ctx.enter_context(nc.semaphore(name))

        ring = sb("ring", [P, SLOTS, SLOT])
        consts = sb("consts_sb", [P, C_N])
        rows = sb("rows", [P, 2, P])
        cols = sb("cols", [P, 2 * P])
        dskip = sb("dskip", [P, ZT])
        dskip_all = sb("dskip_all", [P, SH])
        ssd_par = sb("ssd_par", [SH, 4])
        pos_i = sb("pos_i", [P, TOK], I32)
        sin_t = sb("sin_t", [P, TOK])
        cos_t = sb("cos_t", [P, TOK])
        x = sb("xres", [P, KT, TOK])
        xn = sb("xnorm", [P, KT, TOK])
        sq = sb("squares", [P, KT, TOK])
        std = sb("std", [P, 2, TOK])
        smax = sb("smax", [P, 3, 2])
        ssum = sb("ssum", [P, 3, 2])
        srec = sb("srec", [P, 3, 2])
        rope_a = sb("rope_a", [P, 2, TOK])
        rope_b = sb("rope_b", [P, 2, TOK])
        kpe = sb("kpe", [P, TOK])
        dts = sb("dts", [SH, 6, TOK])
        dtn = sb("dtn", [P, 5, SH])
        router_w = sb("router_w", [P, KT, EG + NE])
        router_b = sb("router_b", [P, EG + NE])
        zeros = sb("zeros", [P, 512], BF16)
        eps_col = sb("eps_col", [P, 1])
        arena = sb("arena", [P, ARENA])
        psum = ctx.enter_context(nc.psum_tensor("psum", [P, 8, 512], F32))
        comb_dram = nc.dram_tensor("comb_scratch", (NE, TOK), F32, kind="Internal").ap()

        ident, ones = consts[:, C_ID:C_ID + P], consts[:, C_ONE:C_ONE + P]
        mask3 = consts[:, C_MASK:C_MASK + 3 * P]
        cap = consts[:, C_CAP:C_CAP + P]

        def at(off, *shape):
            n = int(np.prod(shape))
            v = arena[:, off:off + n]
            if len(shape) == 2:
                return v.rearrange("p (a b) -> p a b", a=shape[0])
            if len(shape) == 3:
                return v.rearrange("p (a b c) -> p a b c", a=shape[0], b=shape[1])
            return v

        prob = at(A_P, 3, 512)
        probT = at(A_PT, 4, 512)
        mem = at(A_MEM, KT, TOK)
        qk = at(A_QK, 2 * H1, TOK)
        v1 = at(A_V1, TB, D)
        o1 = at(A_O1, KT, TOK)
        band = at(A_BAND, TB, 4, TOK)
        poolz = at(A_POOLZ, 4, TB, TOK)
        zs = at(A_ZS, ZT, TOK)
        xbc = at(A_XS, ZT + 2 * NG, TOK)
        xs_nat = at(A_XN, TB, DIN)
        gates = at(A_GATE, 2 * KT, TOK)
        qa = at(A_QA, 3, TOK)
        ckv = at(A_KV, 2, TOK)
        convb = at(A_CONV, 4, TOK)
        dec = at(A_E, HPG, TOK)
        eac = at(A_EA, HPG, P)
        xw = at(A_XW, 512)
        st0 = at(A_ST, 512)
        bn_nat = at(A_BN, P)
        qh = at(A_QH, MH, TOK)
        kh = at(A_KH, MH, TOK)
        vh = at(A_VH, TB, D)
        om = at(A_OM, KT, TOK)
        xq, xk, xv, xo = at(A_XQ, KT, TOK), at(A_XK, KT, TOK), at(A_XV, TB, D), at(A_XO, KT, TOK)
        comb_b = at(A_COMB, NE, TOK)
        hid = at(A_HID, 2, 512)
        sgate = at(A_SG, 2, 512)
        xin = at(A_OUT, TB, D)
        mem_in = at(A_OUT + 2048, TB, D)
        yout = at(A_OUT, TB, D)

        full = [sem(f"full{b}") for b in range(8)]
        made = [sem(f"made{b}") for b in range(8)]
        w_in = [sem(f"w_in{s}") for s in range(SLOTS)]
        s = {n: sem(n) for n in (
            "const_in", "rows_in", "x_in", "mem_in", "band_in", "pos_in", "par_in", "router_in", "zeros_set",
            "x_ready", "sq_ready", "xn_ready", "tables_ready", "dve_step", "act_step", "pool_step",
            "mem_ready", "att_max", "exp_done", "p_ready", "rope_done", "hid_ready", "gate_silu", "down_done",
            "dt_ready", "conv_ready", "conv_done", "xw_ready", "cs_ready", "ea_ready", "seg_ready", "dec_ready",
            "m_ready", "y_ready", "kpe_copied", "exp_g", "comb_t", "comb_out", "comb_in", "hid2",
            "out_ready", "out_stored", "rt_sub", "rt_exp", "rt_sub2", "rt_exp2", "dt_u", "dt_e", "angle", "sines",
            "y_sq")}

        def bank(b):
            return psum[:, b, :]

        def bank2(b):
            return psum[:, b, :].rearrange("p (m t) -> p m t", m=2)

        def col(name, i=0):
            j = COL[name] + i
            return cols[:, j:j + 1]

        NORM = {
            0: (x, KT, "norm_mix", 0, xn, "xT"),
            8: (mem, KT, "norm_mem_2", 0, mem, "memT"),
            1: (x, KT, "norm_mlp", 0, xn, "wo1"),
            2: (x, KT, "norm_mix", 8, xn, "mlp0y"),
            3: (x, KT, "norm_mlp", 8, xn, "pooly"),
            4: (x, KT, "norm_final", 0, x, "mlp1y"),
            5: (x, KT, "norm_mix_2", 0, xn, None),
            6: (qa, 3, "q_a_norm_2", 0, qa, None),
            7: (ckv, 2, "kv_a_norm_2", 0, ckv, None),
            14: (x, KT, "norm_xattn_2", 0, xn, "wo2"),
            15: (x, KT, "norm_moe_2", 0, xn, "xo"),
            16: (x, KT, "norm_final_2", 0, xn, "moey"),
        }
        for g in range(NG):
            NORM[10 + g] = (zs[:, 4 * g:4 * g + 4, :], 4, "ssd_norm_2", 4 * g, zs[:, 4 * g:4 * g + 4, :], None)
        NORM_ORDER = [0, 1, 2, 3, 4, 5, 6, 7, 10, 11, 12, 13, 8, 14, 15, 16]
        SQ_NO = {n: i + 1 for i, n in enumerate(NORM_ORDER)}
        XN_NO, total = {}, 0
        for n in NORM_ORDER:
            XN_NO[n] = total
            total += NORM[n][1]

        RT, off = {}, 0
        for name, n in (("logits", EG + NE), ("gmax", 1), ("gs", EG), ("geq", EG), ("gcand", EG), ("gm", 1),
                        ("goh", EG), ("pick", NE), ("ein", EPG), ("v1", 1), ("eq1", EPG), ("cand", EPG), ("m", 1),
                        ("oh1", EPG), ("rest", EPG), ("v2", 1), ("ds", 1), ("eq2", EPG), ("oh2", EPG), ("ge", EG),
                        ("de", 1), ("gsum", 1), ("gw", 1), ("dsum", 1), ("w1", 1), ("w2", 1), ("comb", NE)):
            RT[name] = at(A_RT + off, TB, n)
            off += TB * n
        combT = arena[0:NE, A_RT + off:A_RT + off + TOK]

        def rt(name):
            return RT[name]

        block = ctx.enter_context(nc.Block())

        @block.sync
        def _(sp):
            def rows_of(w, n):
                return w.rearrange("(k p) n -> p k n", p=P)[:, :, n]

            def wait_free(freed):
                if freed is None:
                    return
                if freed[0] == "down":
                    sp.wait_ge(s["down_done"], freed[1])
                elif freed[0] == "bank":
                    sp.wait_ge(full[freed[1]], freed[2])
                else:
                    b, n = FILL[freed]
                    sp.wait_ge(full[b], n)

            def load(stage, j, src, cols_n):
                slot, n, freed = W[stage, j]
                wait_free(freed)
                k = src.shape[1]
                dst = ring[:, slot, 0:k * cols_n].rearrange("p (k n) -> p k n", k=k)
                sp.dma_start(dst, src).then_inc(w_in[slot], 16)

            sp.dma_start(consts[:], a["consts"]).then_inc(s["const_in"], 16)
            x_rows = a["x"].rearrange("a (b p) d -> p (a b) d", p=P)
            sp.dma_start(xin, x_rows).then_inc(s["x_in"], 16)
            for tile, table in ((0, ROWS_A), (1, ROWS_B)):
                r = 0
                for name, n in table:
                    v = a[name]
                    flat = {1: "a -> a", 2: "a b -> (a b)", 3: "a b c -> (a b c)"}[len(v.shape)]
                    v = v if len(v.shape) == 1 else v.rearrange(flat)
                    sp.dma_start(rows[r:r + n, tile, :], v.rearrange("(r c) -> r c", c=P)).then_inc(s["rows_in"], 16)
                    r += n
            sp.dma_start(pos_i[0:64, :], a["positions"].to_broadcast([64, TOK])).then_inc(s["pos_in"], 16)
            sp.dma_start(pos_i[64:P, :], a["positions_2"].to_broadcast([64, TOK])).then_inc(s["pos_in"], 16)

            wq = a["attn_w_qkv"][0]
            for j in range(12):
                load("qkv", j, rows_of(wq, slice(j * TOK, (j + 1) * TOK)), TOK)
            sp.dma_start(band, a["band"].rearrange("(b p) g t -> p b g t", p=P)).then_inc(s["band_in"], 16)
            sp.dma_start(dskip_all[:], a["d_skip_2"].to_broadcast([P, SH])).then_inc(s["par_in"], 16)
            sp.dma_start(ssd_par[:, 0:1], a["dt_bias_2"].rearrange("a h -> h a")).then_inc(s["par_in"], 16)
            sp.dma_start(ssd_par[:, 1:2], a["a_log_2"].rearrange("a h -> h a")).then_inc(s["par_in"], 16)
            sp.dma_start(router_w[:, :, 0:EG], rows_of(a["w_router_group_2"][0], slice(0, EG))).then_inc(s["router_in"], 16)
            sp.dma_start(router_w[:, :, EG:], rows_of(a["w_router_expert_2"][0], slice(0, NE))).then_inc(s["router_in"], 16)
            sp.dma_start(router_b[:, 0:EG], a["b_router_group_2"].to_broadcast([P, EG])).then_inc(s["router_in"], 16)
            sp.dma_start(router_b[:, EG:], a["b_router_expert_2"].to_broadcast([P, NE])).then_inc(s["router_in"], 16)
            for j in range(4):
                load("wo1", j, rows_of(a["attn_w_o"][0], slice(j * TOK, (j + 1) * TOK)), TOK)

            def mlp_loads(i):
                up = a["mlp_w_up"][i].rearrange("(k p) (c n) -> c p k n", p=P, n=TOK)
                down = a["mlp_w_down"][i].rearrange("(c k p) n -> c p k n", p=P, k=2)
                u, downs = FILL[f"mlp{i}", "first"]

                for j in range(4):
                    for part, src, half in (("up", up, 0), ("down", down, 1)):
                        slot, _, freed = W[f"mlp{i}", part, j]
                        wait_free(freed)
                        dst = ring[:, slot, :].rearrange("p (k n) -> p k n", k=(KT, 2)[half])
                        sp.dma_start(dst, src[j]).then_inc(w_in[slot], 16)
                with sp.Fori(1, FC // 4) as it:
                    for j in range(4):
                        for part, src, half in (("up", up, 0), ("down", down, 1)):
                            slot = W[f"mlp{i}", part, j][0]
                            if half == 0:
                                sp.wait_ge(full[j % 2], it * 2 + (u[j % 2] + j // 2 - 1))
                            else:
                                sp.wait_ge(s["down_done"], it * 4 + (downs + j - 3))
                            dst = ring[:, slot, :].rearrange("p (k n) -> p k n", k=(KT, 2)[half])
                            sp.dma_start(dst, src[it * 4 + j]).then_inc(w_in[slot], 16)

            mlp_loads(0)
            pw = a["pool_w"][0].rearrange("g (k p) n -> p (g k) n", p=P)
            load("pool", 0, pw, TOK)
            mlp_loads(1)

            wi = a["w_in_2"][0]
            for j, (c0, n) in enumerate(((O_DT, SH + P), (O_QA + P, 2 * P), (O_KV, KLR), (O_KR, ROT))):
                load("win", j, rows_of(wi, slice(c0, c0 + n)), n)
            for j in range(12):
                load("win", 4 + j, rows_of(wi, slice(O_XBC + j * TOK, O_XBC + (j + 1) * TOK)), TOK)
            for j in range(8):
                load("win", 16 + j, rows_of(wi, slice(O_Z + j * TOK, O_Z + (j + 1) * TOK)), TOK)
            for j in range(8):
                load("win", 24 + j, rows_of(wi, slice(O_GS + j * TOK, O_GS + (j + 1) * TOK)), TOK)
            so = a["w_ssd_out_2"][0].rearrange("(c k p) n -> c p k n", p=P, k=2)
            for j in range(8):
                load("sout", j, so[j], D)
            for j in range(4):
                load("qb", j, rows_of(a["w_q_b_2"][0], slice(j * 4 * QK, (j + 1) * 4 * QK)), 4 * QK)
            for j in range(2):
                load("kvb", j, rows_of(a["w_kv_b_2"][0], slice(j * D, (j + 1) * D)), D)
            for stage, w, n in (("mout", "w_mla_out_2", 4), ("wo2", "w_o_2", 4), ("xkv", "w_xkv_2", 8),
                                ("xq", "w_xq_2", 4), ("xo", "w_xo_2", 4)):
                if stage == "xkv":
                    b, n_mout = FILL["mout", 3]
                    sp.wait_ge(made[b], n_mout)
                    sp.dma_start(mem_in, a["mem_2"].rearrange("a (b p) d -> p (a b) d", p=P)).then_inc(s["mem_in"], 16)
                for j in range(n):
                    load(stage, j, rows_of(a[w][0], slice(j * TOK, (j + 1) * TOK)), TOK)
            wg = a["w_exp_gate_2"][0].rearrange("e (k p) n -> e p k n", p=P)
            wu = a["w_exp_up_2"][0].rearrange("e (k p) n -> e p k n", p=P)
            wd = a["w_exp_down_2"][0].rearrange("e (k p) n -> e p k n", p=P)
            u, downs = FILL["moe", "first"]
            for n in range(2):
                for part, src in (("gate", wg), ("up", wu), ("down", wd)):
                    slot, _, freed = W["moe", part, n]
                    wait_free(freed)
                    dst = ring[:, slot, :].rearrange("p (k n) -> p k n", k=src.shape[2])
                    sp.dma_start(dst, src[n]).then_inc(w_in[slot], 16)
            with sp.Fori(1, NE // 2) as it:
                for n in range(2):
                    for part, src in (("gate", wg), ("up", wu), ("down", wd)):
                        slot = W["moe", part, n][0]
                        if part == "gate":
                            sp.wait_ge(full[n], it + u[n])
                        elif part == "up":
                            sp.wait_ge(full[2 + n], it + u[2 + n])
                        else:
                            sp.wait_ge(s["down_done"], it * 2 + (downs + n - 1))
                        dst = ring[:, slot, :].rearrange("p (k n) -> p k n", k=src.shape[2])
                        sp.dma_start(dst, src[it * 2 + n]).then_inc(w_in[slot], 16)
            o = out.rearrange("a (b p) d -> p (a b) d", p=P)
            for b in range(TB):
                for half in range(2):
                    bk, n = FILL["outT", 2 * b + half]
                    sp.wait_ge(made[bk], n)
                sp.dma_start(o[:, b, :], yout[:, b, :]).then_inc(s["out_stored"], 16)
            sp.wait_ge(s["out_stored"], 16 * TB)

        @block.tensor
        def _(pe):
            def open_bank(*key):
                b, n = FILL[key]
                if n > 1:
                    pe.wait_ge(made[b], n - 1)
                return b

            def wait_made(*key):
                b, n = FILL[key]
                pe.wait_ge(made[b], n)

            def weights(stage, j, k, n):
                slot, no, _ = W[stage, j]
                pe.wait_ge(w_in[slot], 16 * no)
                return ring[:, slot, 0:k * n].rearrange("p (k n) -> p k n", k=k)

            def norm_sum(n):
                tiles = NORM[n][1]
                b = open_bank("norm", n)
                pe.wait_ge(s["sq_ready"], SQ_NO[n])
                for k in range(tiles):
                    mm = pe.matmul(bank(b)[:, 0:TOK], ones, sq[:, k, :], start=(k == 0), stop=(k == tiles - 1))
                mm.then_inc(full[b], 1)

            def product(b, w, src, kt, parts, xn_from=None):
                for m, (p0, c0, width) in enumerate(parts):
                    for k in range(kt):
                        if xn_from is not None and m == 0:
                            pe.wait_ge(s["xn_ready"], xn_from + k + 1)
                        mm = pe.matmul(bank2(b)[p0:p0 + width, m, :], w[:, k, c0:c0 + width], src[:, k, :],
                                       start=(k == 0), stop=(k == kt - 1))
                return mm

            BOTH = ((0, 0, P), (0, P, P))

            def project(stage, j, key, src, xn_from=None, parts=BOTH, n=TOK):
                b = open_bank(*key)
                w = weights(stage, j, KT, n)
                product(b, w, src, KT, parts, xn_from).then_inc(full[b], 1)

            def project_natural(stage, j, key, src):
                b = open_bank(*key)
                w = weights(stage, j, KT, TOK)
                for tb in range(TB):
                    for k in range(KT):
                        mm = pe.matmul(bank2(b)[:, tb, :], src[:, k, tb * P:(tb + 1) * P], w[:, k, :],
                                       start=(k == 0), stop=(k == KT - 1))
                mm.then_inc(full[b], 1)

            def rotate(key, src, heads=2):
                b = open_bank(*key)
                p0 = src[1]
                pe.matmul(bank(b)[p0:p0 + ROT, 0:heads * TOK], consts[p0:p0 + ROT, C_ROT:C_ROT + ROT], src[0],
                          start=True, stop=True).then_inc(full[b], 1)

            def attention(first, heads, pair, scores, values, key_blocks):
                for i in range(heads + 3):
                    if i < heads:
                        b = open_bank("S", first + i)
                        scores(i, b).then_inc(full[b], 1)
                    n = i - 2
                    if 0 <= n < heads:
                        b = open_bank("T", first + n)
                        pe.wait_ge(s["p_ready"], 2 * (first + n + 1))
                        for t, (src, dst) in enumerate(key_blocks):
                            mm = pe.transpose(bank(b)[:, dst:dst + P], prob[:, (first + n) % 3, src:src + P], ident)
                        mm.then_inc(full[b], 1)
                    n = i - 3
                    if n >= 0:
                        lead = first + n - n % pair
                        b = open_bank("O", lead) if n % pair == 0 else FILL["O", lead][0]
                        wait_made("T", first + n)
                        mm = values(n, b, probT[:, (first + n) % 4, :])
                        if n % pair == pair - 1:
                            mm.then_inc(full[b], 1)

            CAUSAL = ((0, 0), (P, P), (2 * P, 2 * P))
            CROSS = ((0, 0), (P, 2 * P), (2 * P, P), (3 * P, 3 * P))

            def mlp(i):
                stage = f"mlp{i}"
                u, _ = FILL[stage, "first"]
                for b in range(4):
                    open_bank(stage + "y", b)

                def up(it, j):
                    slot, no, _ = W[stage, "up", j]
                    b = j % 2
                    pe.wait_ge(made[b], it * 2 + (u[b] + j // 2))
                    pe.wait_ge(w_in[slot], it * 16 + 16 * no)
                    w = ring[:, slot, :].rearrange("p (k n) -> p k n", k=KT)
                    product(b, w, xn, KT, BOTH).then_inc(full[b], 1)

                def down(it, j, last=False):
                    slot, no, _ = W[stage, "down", j]
                    pe.wait_ge(made[j % 2], it * 2 + (u[j % 2] + j // 2 + 1))
                    pe.wait_ge(w_in[slot], it * 16 + 16 * no)
                    w = ring[:, slot, :].rearrange("p (k n) -> p k n", k=2)
                    add_down(w, hid[:, j % 2, :].rearrange("p (k t) -> p k t", k=2), last)

                clear_sums()
                pe.wait_ge(s["xn_ready"], XN_NO[2 * i + 1] + KT)
                up(0, 0)
                with pe.Fori(0, FC // 4 - 1) as it:
                    for j in range(4):
                        up(it + (j + 1) // 4, (j + 1) % 4)
                        down(it, j)
                for j in range(4):
                    if j < 3:
                        up(FC // 4 - 1, j + 1)
                    down(FC // 4 - 1, j, last=(j == 3))

            def clear_sums():
                pe.wait_ge(s["zeros_set"], 1)
                for b in range(4, 8):
                    pe.matmul(bank(b), zeros[:, 0:P], zeros[:, :], start=True, stop=False, skip_group_check=True)

            def add_down(w, src, last, first=False):
                for m in range(KT):
                    for k in range(2):
                        mm = pe.matmul(bank2(4 + m // 2)[:, m % 2, :], w[:, k, m * P:(m + 1) * P], src[:, k, :],
                                       start=(first and k == 0 and m % 2 == 0), stop=(last and k == 1),
                                       skip_group_check=True)
                        if last and m % 2 == 1 and k == 1:
                            mm.then_inc(full[4 + m // 2], 1)
                if not last:
                    mm.then_inc(s["down_done"], 1)

            pe.wait_ge(s["const_in"], 16)
            pe.wait_ge(s["x_in"], 16)
            for j in range(4):
                b = open_bank("xT", j)
                for m in range(2):
                    for tb in range(TB):
                        mm = pe.transpose(bank2(b)[:, m, tb * P:(tb + 1) * P],
                                          xin[:, tb, (2 * j + m) * P:(2 * j + m + 1) * P], ident)
                mm.then_inc(full[b], 1)
            pe.wait_ge(s["rows_in"], 16 * (len(ROWS_A) + len(ROWS_B)))
            b = open_bank("cols", 0)
            pe.transpose(bank(b)[:, 0:N_A], rows[0:N_A, 0, :], consts[0:N_A, C_ID:C_ID + N_A])
            pe.transpose(bank(b)[:, P:P + N_B], rows[0:N_B, 1, :], consts[0:N_B, C_ID:C_ID + N_B]).then_inc(full[b], 1)
            norm_sum(0)

            def rope1(j):
                wait_made("qk", j)
                rotate(("rope1", j), (qk[0:ROT, 2 * j:2 * j + 2, :], 0))

            for j in range(8):
                project("qkv", j, ("qk", j), xn, XN_NO[0] if j == 0 else None)
                if j:
                    rope1(j - 1)
            project_natural("qkv", 8, ("v1", 0), xn)
            rope1(7)
            for j in range(1, 4):
                project_natural("qkv", 8 + j, ("v1", j), xn)

            def scores1(h, b):
                pe.matmul(bank(b)[:, 0:P], qk[:, h, 0:P], qk[:, H1 + h, 0:P], start=True, stop=True)
                return pe.matmul(bank(b)[:, P:3 * P], qk[:, h, P:TOK], qk[:, H1 + h, :], start=True, stop=True)

            def values1(h, b, pt):
                pe.matmul(bank(b)[:, 0:TOK], v1[:, 0, h * P:(h + 1) * P], pt[:, 0:TOK], start=True, stop=False)
                return pe.matmul(bank(b)[:, P:TOK], v1[:, 1, h * P:(h + 1) * P], pt[:, TOK:TOK + P],
                                 start=False, stop=True)

            pe.wait_ge(s["rope_done"], 8)
            for j in range(2, 4):
                wait_made("v1", j)
            attention(0, H1, 1, scores1, values1, CAUSAL)
            for h in range(H1 - 2, H1):
                wait_made("O", h)
            for j in range(4):
                project("wo1", j, ("wo1", j), o1)
            norm_sum(1)
            mlp(0)

            norm_sum(2)
            slot, no, _ = W["pool", 0]
            pe.wait_ge(w_in[slot], 16 * no)
            pe.wait_ge(s["band_in"], 16)
            wp = ring[:, slot, :].rearrange("p (k n) -> p k n", k=KT)
            for g in range(4):
                b = open_bank("poolz", g)
                pe.wait_ge(s["xn_ready"], XN_NO[2] + 2 * g + 2)
                for tb in range(TB):
                    for k in range(2):
                        mm = pe.matmul(bank2(b)[:, tb, :], xn[:, 2 * g + k, tb * P:(tb + 1) * P], wp[:, 2 * g + k, :],
                                       start=(k == 0), stop=(k == 1))
                mm.then_inc(full[b], 1)
            for g in range(4):
                wait_made("poolz", g)
                b = open_bank("pooly", g)
                for m in range(2):
                    pe.matmul(bank2(b)[:, m, :], poolz[:, g, 0, m * P:(m + 1) * P], band[:, 0, g, :],
                              start=True, stop=False)
                    mm = pe.matmul(bank2(b)[:, m, P:TOK], poolz[:, g, 1, m * P:(m + 1) * P], band[:, 1, g, P:TOK],
                                   start=False, stop=True)
                mm.then_inc(full[b], 1)
            norm_sum(3)
            mlp(1)
            norm_sum(4)
            norm_sum(5)

            SMALL = (((0, 0, SH), (0, SH, P)), BOTH, BOTH, ((64, 0, ROT),))
            for j, n in enumerate((SH + P, TOK, TOK, ROT)):
                project("win", j, ("small", j), xn, XN_NO[5] if j == 0 else None, SMALL[j], n)
            for j in range(12):
                project("win", 4 + j, ("xbc", j), xn)
                if j == 0:
                    wait_made("small", 3)
                    rotate(("ropek", 0), (kpe[64:64 + ROT, :], 64), 1)
                if j == 1:
                    norm_sum(6)
                    norm_sum(7)
            b = open_bank("dtT", 0)
            pe.wait_ge(s["dt_ready"], 1)
            for i, (row, t0) in enumerate(((1, 0), (1, P), (0, 0), (0, P), (5, 0))):
                mm = pe.transpose(bank(b)[:, SH * i:SH * (i + 1)], dts[:, row, t0:t0 + P], consts[0:SH, C_ID:C_ID + SH])
            mm.then_inc(full[b], 1)
            for j in range(8):
                project("win", 16 + j, ("z", j), xn)
            for j in range(8):
                project("win", 24 + j, ("gates", j), xn)

            pe.wait_ge(s["conv_done"], 12)
            for g in range(NG):
                b = open_bank("cb", g)
                for ch in range(TB):
                    mm = pe.matmul(bank(b)[:, ch * P:(ch + 1) * P], xbc[:, ZT + g, ch * P:(ch + 1) * P],
                                   xbc[:, ZT + NG + g, ch * P:(ch + 1) * P], start=True, stop=True)
                mm.then_inc(full[b], 1)
                b = open_bank("bn", g)
                pe.transpose(bank(b)[:, 0:P], xbc[:, ZT + g, 0:P], ident).then_inc(full[b], 1)
                for ch in range(TB):
                    b = open_bank("xsn", g, ch)
                    for i in range(4):
                        mm = pe.transpose(bank(b)[:, i * P:(i + 1) * P], xbc[:, 4 * g + i, ch * P:(ch + 1) * P], ident)
                    mm.then_inc(full[b], 1)
                for q in range(4):
                    b = open_bank("acum", g, q)
                    for hh in range(2):
                        h = HPG * g + 2 * q + hh
                        mm = pe.matmul(bank2(b)[:, hh, :], consts[0:SH, C_ID + h:C_ID + h + 1].to_broadcast([SH, P]),
                                       dts[:, 1, :], start=True, stop=True)
                    mm.then_inc(full[b], 1)
                wait_made("bn", g)
                pe.wait_ge(s["xw_ready"], g + 1)
                b = open_bank("state", g)
                pe.matmul(bank(b), bn_nat, xw, start=True, stop=True).then_inc(full[b], 1)
                wait_made("state", g)
                pe.wait_ge(s["cs_ready"], g + 1)
                wait_made("xsn", g, 0)
                wait_made("xsn", g, 1)
                for half in range(2):
                    b = open_bank("y", g, half)
                    for hp in range(4):
                        h = 4 * half + hp
                        if h < HPG - 1:
                            pe.wait_ge(s["m_ready"], (HPG - 1) * g + h + 1)
                        else:
                            wait_made("cb", g)
                        o = bank2(b)[64 * (h % 2):64 * (h % 2) + 64, (h // 2) % 2, :]
                        hc = slice((HPG * g + h) * 64, (HPG * g + h + 1) * 64)
                        pe.matmul(o[:, 0:P], xs_nat[:, 0, hc], dec[:, h, 0:P], start=True, stop=True)
                        pe.matmul(o[:, P:TOK], xs_nat[:, 1, hc], dec[:, h, P:TOK], start=True, stop=False)
                        mm = pe.matmul(o[:, P:TOK], st0[:, h * 64:(h + 1) * 64], eac[:, h, :], start=False, stop=True)
                    mm.then_inc(full[b], 1)
                norm_sum(10 + g)
            for b in range(4):
                open_bank("souty", b)
            for j in range(8):
                pe.wait_ge(s["xn_ready"], XN_NO[10 + j // 2] + 4)
                w = weights("sout", j, 2, D)
                add_down(w, zs[:, 2 * j:2 * j + 2, :], last=(j == 7), first=(j == 0))

            def rope2(j):
                wait_made("qh", j)
                rotate(("rope2", j), (qh[64:64 + ROT, 2 * j:2 * j + 2, :], 64))

            pe.wait_ge(s["xn_ready"], XN_NO[7] + 2)
            for j in range(8):
                b = open_bank("qh", j)
                w = weights("qb", j // 2, 3, 4 * QK)
                c0 = j % 2 * 2 * QK
                product(b, w, qa, 3, ((0, c0, QK), (0, c0 + QK, QK))).then_inc(full[b], 1)
                if j:
                    rope2(j - 1)
            for j in range(8):
                b = open_bank("kh", j)
                w = weights("kvb", j // 4, 2, D)
                c0 = j % 4 * 2 * P
                product(b, w, ckv, 2, ((0, c0, NOPE), (0, c0 + P, NOPE))).then_inc(full[b], 1)
                if j == 0:
                    rope2(7)
                if j % 4 == 3:
                    wv = w.rearrange("p k (h c) -> p k h c", c=P)[:, :, :, NOPE:]
                    for tb in range(TB):
                        b = open_bank("vh", j // 4 * 2 + tb)
                        for k in range(2):
                            mm = pe.matmul(bank(b), ckv[:, k, tb * P:(tb + 1) * P], wv[:, k, :, :],
                                           start=(k == 0), stop=(k == 1))
                        mm.then_inc(full[b], 1)

            def scores2(h, b):
                pe.matmul(bank(b)[:, 0:P], qh[0:QK, h, 0:P], kh[0:QK, h, 0:P], start=True, stop=True)
                return pe.matmul(bank(b)[:, P:3 * P], qh[0:QK, h, P:TOK], kh[0:QK, h, :], start=True, stop=True)

            def values2(h, b, pt):
                o = bank(b)[64 * (h % 2):64 * (h % 2) + 64, :]
                pe.matmul(o[:, 0:TOK], vh[:, 0, h * VH:(h + 1) * VH], pt[:, 0:TOK], start=True, stop=False,
                          skip_group_check=True)
                return pe.matmul(o[:, P:TOK], vh[:, 1, h * VH:(h + 1) * VH], pt[:, TOK:TOK + P],
                                 start=False, stop=True, skip_group_check=True)

            pe.wait_ge(s["rope_done"], 17)
            pe.wait_ge(s["kpe_copied"], 1)
            for key in (("kh", 6), ("kh", 7), ("vh", 2), ("vh", 3)):
                wait_made(*key)
            attention(H1, MH, 2, scores2, values2, CAUSAL)
            for h in (MH - 4, MH - 2):
                wait_made("O", H1 + h)
            for j in range(4):
                project("mout", j, ("mout", j), om)
            pe.wait_ge(s["y_ready"], 2 * NG + 4)
            pe.wait_ge(s["mem_in"], 16)
            for j in range(4):
                b = open_bank("memT", j)
                for m in range(2):
                    for tb in range(TB):
                        mm = pe.transpose(bank2(b)[:, m, tb * P:(tb + 1) * P],
                                          mem_in[:, tb, (2 * j + m) * P:(2 * j + m + 1) * P], ident)
                mm.then_inc(full[b], 1)
            norm_sum(8)
            for j in range(4):
                project("wo2", j, ("wo2", j), xn)
            norm_sum(14)

            pe.wait_ge(s["xn_ready"], XN_NO[8] + KT)
            for j in range(4):
                project("xkv", j, ("xk", j), mem)
            for j in range(4):
                project_natural("xkv", 4 + j, ("xv", j), mem)
            for j in range(4):
                project("xq", j, ("xq", j), xn, XN_NO[14] if j == 0 else None)

            def scores3(h, b):
                for qb in range(2):
                    for kk in range(2):
                        mm = pe.matmul(bank2(b)[:, qb, :], xq[:, 2 * h + kk, qb * P:(qb + 1) * P],
                                       xk[:, 2 * h + kk, :], start=(kk == 0), stop=(kk == 1))
                return mm

            def values3(h, b, pt):
                for m in range(2):
                    for kb in range(2):
                        mm = pe.matmul(bank2(b)[:, m, :], xv[:, kb, (2 * h + m) * P:(2 * h + m + 1) * P],
                                       pt[:, kb * TOK:(kb + 1) * TOK], start=(kb == 0), stop=(kb == 1))
                return mm

            for stage in ("xk", "xv", "xq"):
                for j in (2, 3):
                    wait_made(stage, j)
            attention(H1 + MH, XH, 1, scores3, values3, CROSS)
            for h in (XH - 2, XH - 1):
                wait_made("O", H1 + MH + h)
            for j in range(4):
                project("xo", j, ("xo", j), xo)
            norm_sum(15)

            pe.wait_ge(s["router_in"], 64)
            pe.wait_ge(s["xn_ready"], XN_NO[15] + KT)
            b = open_bank("logits", 0)
            for tb in range(TB):
                for k in range(KT):
                    mm = pe.matmul(bank(b)[:, tb * (EG + NE):(tb + 1) * (EG + NE)], xn[:, k, tb * P:(tb + 1) * P],
                                   router_w[:, k, :], start=(k == 0), stop=(k == KT - 1))
            mm.then_inc(full[b], 1)

            for b in range(4):
                open_bank("moey", b)
            clear_sums()
            u, _ = FILL["moe", "first"]

            def gate_up(it, n):
                for part, b in (("gate", n), ("up", 2 + n)):
                    slot, no, _ = W["moe", part, n]
                    pe.wait_ge(made[b], it + u[b])
                    pe.wait_ge(w_in[slot], it * 16 + 16 * no)
                    w = ring[:, slot, :].rearrange("p (k n) -> p k n", k=KT)
                    product(b, w, xn, KT, BOTH).then_inc(full[b], 1)

            def expert_down(it, n, last=False):
                slot, no, _ = W["moe", "down", n]
                pe.wait_ge(s["hid2"], it * 2 + (n + 1))
                pe.wait_ge(w_in[slot], it * 16 + 16 * no)
                w = ring[:, slot, :].rearrange("p (k n) -> p k n", k=2)
                add_down(w, hid[:, n, :].rearrange("p (k t) -> p k t", k=2), last)

            b = open_bank("combT", 0)
            gate_up(0, 0)
            pe.wait_ge(s["comb_t"], 1)
            for tb in range(TB):
                mm = pe.transpose(bank(b)[0:NE, tb * P:(tb + 1) * P], rt("comb")[:, tb, :], ident)
            mm.then_inc(full[b], 1)
            with pe.Fori(0, NE // 2 - 1) as it:
                gate_up(it, 1)
                expert_down(it, 0)
                gate_up(it + 1, 0)
                expert_down(it, 1)
            gate_up(NE // 2 - 1, 1)
            expert_down(NE // 2 - 1, 0)
            expert_down(NE // 2 - 1, 1, last=True)

            norm_sum(16)
            for j in range(4):
                b = open_bank("outT", j)
                for i in range(4):
                    k = 4 * (j % 2) + i
                    pe.wait_ge(s["xn_ready"], XN_NO[16] + k + 1)
                    mm = pe.transpose(bank(b)[:, i * P:(i + 1) * P], xn[:, k, (j // 2) * P:(j // 2 + 1) * P], ident)
                mm.then_inc(full[b], 1)

        @block.scalar
        def _(act):
            def wait_full(*key):
                b, n = FILL[key]
                act.wait_ge(full[b], n)
                return b

            def wait_made(*key):
                b, n = FILL[key]
                act.wait_ge(made[b], n)

            def copy_out(dst, *key, view=None):
                b = wait_full(*key)
                act.activation(dst, view(b) if view else bank2(b), ACT.Copy).then_inc(made[b], 1)

            def norm(n):
                src, tiles, _, _, _, after = NORM[n]
                if after is not None:
                    for j in range(4):
                        wait_made(after, j)
                elif n == 5:
                    act.wait_ge(s["xn_ready"], XN_NO[4] + KT)
                elif n == 6:
                    wait_made("small", 0)
                    wait_made("small", 1)
                elif n == 7:
                    wait_made("small", 2)
                else:
                    act.wait_ge(s["y_ready"], 2 * (n - 9))
                act.activation(sq[:, 0:tiles, :], src[:, 0:tiles, :], ACT.Square).then_inc(s["sq_ready"], 1)
                b = wait_full("norm", n)
                if XN_NO[n]:
                    act.wait_ge(s["xn_ready"], XN_NO[n])
                act.activation(std[:, 0, :], bank(b)[:, 0:TOK], ACT.Sqrt, bias=eps_col[:, 0:1],
                               scale=1.0 / (tiles * P)).then_inc(made[b], 1)

            def attention(first, heads, segments):
                for i in range(heads + 2):
                    if i < heads:
                        n = first + i
                        act.wait_ge(s["att_max"], 2 * (n + 1))
                        for e, (c0, c1) in enumerate(segments):
                            act.activation(prob[:, n % 3, c0:c1], prob[:, n % 3, c0:c1], ACT.Exp,
                                           bias=smax[:, n % 3, e:e + 1],
                                           accum_out=ssum[:, n % 3, e:e + 1]).then_inc(s["exp_done"], 1)
                    n = first + i - 2
                    if i >= 2:
                        if n - 4 >= first:
                            lead = [k for k in FILL if k[0] == "O" and first <= k[1] <= n - 4]
                            wait_full("O", max(k[1] for k in lead))
                        w = segments[-1][1]
                        copy_out(probT[:, n % 4, 0:w], "T", n, view=lambda b: bank(b)[:, 0:w])

            CAUSAL = ((0, P), (P, 3 * P))
            CROSS = ((0, TOK), (TOK, 2 * TOK))

            act.wait_ge(s["zeros_set"], 1)
            norm(0)
            act.wait_ge(s["angle"], 1)
            act.activation(sin_t[:], rope_b[:, 0, :], ACT.Sin).then_inc(s["sines"], 1)
            act.activation(cos_t[:], rope_b[:, 1, :], ACT.Sin).then_inc(s["sines"], 1)
            for j in range(8):
                copy_out(qk[:, 2 * j:2 * j + 2, :], "qk", j)
            for j in range(4):
                copy_out(v1[:, :, j * TOK:(j + 1) * TOK], "v1", j)
            attention(0, H1, CAUSAL)
            norm(1)

            def mlp_relu(i):
                u, _ = FILL[f"mlp{i}", "first"]
                with act.Fori(0, FC // 4) as it:
                    for j in range(4):
                        b = j % 2
                        act.wait_ge(full[b], it * 2 + (u[b] + j // 2 + 1))
                        act.activation(sgate[:, b, :], bank(b), ACT.Relu).then_inc(s["gate_silu"], 1)

            mlp_relu(0)
            norm(2)
            for g in range(4):
                copy_out(poolz[:, g, :, :], "poolz", g)
            norm(3)
            mlp_relu(1)
            norm(4)
            norm(5)

            act.wait_ge(s["dt_u"], 1)
            copy_out(qa[:, 0, :], "small", 0, view=lambda b: bank2(b)[:, 1, :])
            copy_out(qa[:, 1:3, :], "small", 1)
            copy_out(ckv, "small", 2)
            copy_out(kpe[64:64 + ROT, :], "small", 3, view=lambda b: bank(b)[64:64 + ROT, 0:TOK])
            act.activation(ssd_par[:, 2:3], ssd_par[:, 1:2], ACT.Exp).then_inc(s["dt_e"], 1)
            act.wait_ge(s["dt_u"], 2)
            act.activation(dts[:, 2, :], dts[:, 1, :], ACT.Exp, scale=-1.0).then_inc(s["dt_e"], 1)
            for j in range(12):
                wait_made("xbc", j)
                act.activation(xbc[:, 2 * j:2 * j + 2, :], convb[:, 2 * (j % 2):2 * (j % 2) + 2, :],
                               ACT.Silu).then_inc(s["conv_done"], 1)
                if j == 1:
                    norm(6)
                    norm(7)
                if j == 3:
                    act.wait_ge(s["dt_u"], 3)
                    act.activation(dts[:, 4, 0:P], dts[:, 1, 0:P], ACT.Exp, bias=dts[:, 1, P - 1:P],
                                   scale=-1.0).then_inc(s["dt_e"], 1)
            copy_out(dtn[:], "dtT", 0, view=lambda b: bank(b)[:, 0:5 * SH].rearrange("p (a h) -> p a h", a=5))
            for j in range(8):
                b = wait_full("z", j)
                act.activation(zs[:, 2 * j:2 * j + 2, :], bank2(b), ACT.Silu).then_inc(made[b], 1)
            for j in range(8):
                b = wait_full("gates", j)
                act.activation(gates[:, 2 * j:2 * j + 2, :], bank2(b), ACT.Sigmoid).then_inc(made[b], 1)
            for g in range(NG):
                copy_out(bn_nat, "bn", g, view=lambda b: bank(b)[:, 0:P])
                for ch in range(TB):
                    copy_out(xs_nat[:, ch, g * 512:(g + 1) * 512], "xsn", g, ch, view=bank)
                if g:
                    wait_full("y", g - 1, 0)
                    wait_full("y", g - 1, 1)
                for q in range(4):
                    b = wait_full("acum", g, q)
                    act.activation(eac[:, 2 * q:2 * q + 2, :], bank2(b)[:, :, P:TOK], ACT.Exp).then_inc(s["ea_ready"], 1)
                for q in range(4):
                    wait_made("acum", g, q)
                    act.activation(dec[:, 2 * q:2 * q + 2, :], dec[:, 2 * q:2 * q + 2, :],
                                   ACT.Exp).then_inc(s["dec_ready"], 1)
                copy_out(st0, "state", g, view=bank)
                norm(10 + g)
            for j in range(8):
                if j == 0:
                    for b4 in range(4):
                        wait_full("souty", b4)
                copy_out(qh[0:QK, 2 * j:2 * j + 2, :], "qh", j, view=lambda b: bank2(b)[0:QK])
            for j in range(8):
                copy_out(kh[0:NOPE, 2 * j:2 * j + 2, :], "kh", j, view=lambda b: bank2(b)[0:NOPE])
                if j % 4 == 3:
                    for tb in range(TB):
                        copy_out(vh[:, tb, j // 4 * 512:(j // 4 + 1) * 512], "vh", j // 4 * 2 + tb, view=bank)
            attention(H1, MH, CAUSAL)
            for j in range(4):
                copy_out(mem[:, 2 * j:2 * j + 2, :], "memT", j)
            norm(8)
            norm(14)
            for j in range(4):
                copy_out(xk[:, 2 * j:2 * j + 2, :], "xk", j)
            for j in range(4):
                copy_out(xv[:, :, j * TOK:(j + 1) * TOK], "xv", j)
            for j in range(4):
                copy_out(xq[:, 2 * j:2 * j + 2, :], "xq", j)
            attention(H1 + MH, XH, CROSS)
            norm(15)
            act.wait_ge(s["rt_sub"], 1)
            act.activation(rt("ge"), rt("gs"), ACT.Exp).then_inc(s["rt_exp"], 1)
            act.wait_ge(s["rt_sub"], 2)
            act.activation(rt("de"), rt("ds"), ACT.Exp).then_inc(s["rt_exp"], 1)
            u, _ = FILL["moe", "first"]

            def silu_gate(it, n):
                act.wait_ge(full[n], it + (u[n] + 1))
                act.activation(sgate[:, n, :], bank(n), ACT.Silu).then_inc(made[n], 1)

            silu_gate(0, 0)
            copy_out(combT, "combT", 0, view=lambda b: bank(b)[0:NE, 0:TOK])
            wait_made("combT", 0)
            act.dma_start(comb_dram, combT).then_inc(s["comb_out"], 16)
            act.wait_ge(s["comb_out"], 16)
            for q in range(4):
                e0 = q * NE // 4
                src = comb_dram[e0:e0 + NE // 4, :].rearrange("(o e) t -> o e t", o=1)
                act.dma_start(comb_b[:, e0:e0 + NE // 4, :], src.to_broadcast([P, NE // 4, TOK])).then_inc(s["comb_in"], 16)
            silu_gate(0, 1)
            with act.Fori(1, NE // 2) as it:
                for n in range(2):
                    act.wait_ge(s["hid2"], it * 2 + (n - 1))
                    silu_gate(it, n)
            norm(16)

        @block.vector
        def _(dve):
            steps, ropes = [0], [0]

            def link(ins):
                steps[0] += 1
                ins.then_inc(s["dve_step"], 1)
                dve.wait_ge(s["dve_step"], steps[0])

            def wait_full(*key):
                b, n = FILL[key]
                dve.wait_ge(full[b], n)
                return b

            def wait_made(*key):
                b, n = FILL[key]
                dve.wait_ge(made[b], n)

            def norm(n):
                src, tiles, gain, first, dst, _ = NORM[n]
                wait_made("norm", n)
                link(dve.reciprocal(std[:, 1, :], std[:, 0, :]))
                for k in range(tiles):
                    dve.scalar_tensor_tensor(dst[:, k, :], src[:, k, :], col(gain, first + k), std[:, 1, :],
                                             ALU.mult, ALU.mult).then_inc(s["xn_ready"], 1)

            def add_to_x(stage, j, scale=None):
                b = wait_full(stage, j)
                dve.tensor_tensor(x[:, 2 * j:2 * j + 2, :], bank2(b), x[:, 2 * j:2 * j + 2, :],
                                  ALU.add).then_inc(made[b], 1)

            def pair_bcast(t):
                return t.rearrange("p (o t) -> p o t", o=1).to_broadcast([t.shape[0], 2, TOK])

            def rope(key, t, p0, heads=2):
                r = slice(p0, p0 + ROT)
                b = wait_full(*key)
                if heads == 2:
                    swapped, sin_b, cos_b = bank2(b)[r], pair_bcast(sin_t[r, :]), pair_bcast(cos_t[r, :])
                    ta, tb_ = rope_a[r, :, :], rope_b[r, :, :]
                else:
                    swapped, sin_b, cos_b = bank(b)[r, 0:TOK], sin_t[r, :], cos_t[r, :]
                    ta, tb_ = rope_a[r, 0, :], rope_b[r, 0, :]
                if ropes[0]:
                    dve.wait_ge(s["rope_done"], ropes[0])
                ropes[0] += 1
                dve.tensor_tensor(ta, swapped, sin_b, ALU.mult).then_inc(made[b], 1)
                wait_made(*key)
                link(dve.tensor_tensor(tb_, t, cos_b, ALU.mult))
                dve.tensor_tensor(t, ta, tb_, ALU.add).then_inc(s["rope_done"], 1)

            def attention(first, heads, pair, segments, scale, masked, outs):
                w = segments[-1][1]
                for i in range(heads + 3):
                    if i < heads:
                        n = first + i
                        b = wait_full("S", n)
                        if i >= 3:
                            wait_full("T", n - 3)
                        if masked:
                            ins = dve.scalar_tensor_tensor(prob[:, n % 3, 0:w], bank(b)[:, 0:w], scale, mask3,
                                                           ALU.mult, ALU.add)
                        else:
                            ins = dve.tensor_scalar(prob[:, n % 3, 0:w], bank(b)[:, 0:w], scale, None, ALU.mult)
                        ins.then_inc(made[b], 1)
                        wait_made("S", n)
                        for e, (c0, c1) in enumerate(segments):
                            dve.tensor_reduce(smax[:, n % 3, e:e + 1], prob[:, n % 3, c0:c1], AX_X, ALU.max,
                                              negate=True).then_inc(s["att_max"], 1)
                    if 1 <= i <= heads:
                        n = first + i - 1
                        dve.wait_ge(s["exp_done"], 2 * (n + 1))
                        link(dve.reciprocal(srec[:, n % 3, :], ssum[:, n % 3, :]))
                        for e, (c0, c1) in enumerate(segments):
                            dve.tensor_scalar(prob[:, n % 3, c0:c1], prob[:, n % 3, c0:c1], srec[:, n % 3, e:e + 1],
                                              None, ALU.mult).then_inc(s["p_ready"], 1)
                    n = i - 3
                    if n >= 0 and n % pair == pair - 1:
                        b = wait_full("O", first + n - pair + 1)
                        dst, src = outs(n // pair, b)
                        dve.tensor_copy(dst, src).then_inc(made[b], 1)

            CAUSAL = ((0, P), (P, 3 * P))
            CROSS = ((0, TOK), (TOK, 2 * TOK))

            link(dve.memset(eps_col[:], EPS))
            dve.memset(zeros[:], 0.0).then_inc(s["zeros_set"], 1)
            for j in range(4):
                b = wait_full("xT", j)
                dve.tensor_copy(x[:, 2 * j:2 * j + 2, :], bank2(b)).then_inc(made[b], 1)
            b = wait_full("cols", 0)
            link(dve.tensor_copy(cols[:, 0:N_A], bank(b)[:, 0:N_A]))
            dve.tensor_copy(cols[:, P:P + N_B], bank(b)[:, P:P + N_B]).then_inc(made[b], 1)
            wait_made("cols", 0)
            norm(0)

            dve.wait_ge(s["pos_in"], 32)
            dve.wait_ge(s["const_in"], 16)
            ang, turns, red, comp = rope_a[:, 0, :], rope_a[:, 1, :], rope_b[:, 0, :], rope_b[:, 1, :]
            magic = 1.5 * 2.0 ** 23
            c1 = 6.28125
            c2 = float(np.float32(round((2 * math.pi - c1) * 2 ** 20) / 2 ** 20))
            c3 = 2 * math.pi - c1 - c2
            link(dve.tensor_copy(ang, pos_i[:]))
            link(dve.tensor_scalar(ang, ang, consts[:, C_INVF:C_INVF + 1], None, ALU.mult))
            link(dve.tensor_scalar(turns, ang, 1 / (2 * math.pi), magic, ALU.mult, ALU.add))
            link(dve.tensor_scalar(turns, turns, magic, None, ALU.subtract))
            link(dve.scalar_tensor_tensor(red, turns, -c1, ang, ALU.mult, ALU.add))
            link(dve.scalar_tensor_tensor(red, turns, -c2, red, ALU.mult, ALU.add))
            link(dve.scalar_tensor_tensor(red, turns, -c3, red, ALU.mult, ALU.add))
            link(dve.tensor_scalar(red, red, 3.1415925, -3.1415925, ALU.min, ALU.max))
            link(dve.scalar_tensor_tensor(comp, red, -1.0, red, ALU.mult, ALU.max))
            dve.tensor_scalar(comp, comp, -1.0, math.pi / 2, ALU.mult, ALU.add).then_inc(s["angle"], 1)
            dve.wait_ge(s["sines"], 2)

            for j in range(8):
                rope(("rope1", j), qk[0:ROT, 2 * j:2 * j + 2, :], 0)
            attention(0, H1, 1, CAUSAL, float(P) ** -0.5, True, lambda h, b: (o1[:, h, :], bank(b)[:, 0:TOK]))
            for j in range(4):
                add_to_x("wo1", j)
            norm(1)

            def mlp_square(i):
                u, downs = FILL[f"mlp{i}", "first"]
                silus = i * FC

                def chunk(it, j, first):
                    b = j % 2
                    dve.wait_ge(s["gate_silu"], it * 4 + (silus + j + 1))
                    if not first:
                        dve.wait_ge(s["down_done"], it * 4 + (downs + j - 1))
                    dve.scalar_tensor_tensor(hid[:, b, :], bank(b), 0.0, sgate[:, b, :], ALU.max,
                                             ALU.mult).then_inc(made[b], 1)

                for j in range(4):
                    chunk(0, j, j < 2)
                with dve.Fori(1, FC // 4) as it:
                    for j in range(4):
                        chunk(it, j, False)
                for j in range(4):
                    add_to_x(f"mlp{i}y", j)

            mlp_square(0)
            norm(2)
            for g in range(4):
                b = wait_full("pooly", g)
                for m in range(2):
                    ins = dve.scalar_tensor_tensor(x[:, 2 * g + m, :], bank2(b)[:, m, :], col("pool_scale", 2 * g + m),
                                                   x[:, 2 * g + m, :], ALU.mult, ALU.add)
                ins.then_inc(made[b], 1)
            norm(3)
            mlp_square(1)
            norm(4)
            norm(5)

            dve.wait_ge(s["par_in"], 48)
            for half in range(2):
                r = slice(64 * half, 64 * half + 64)
                link(dve.tensor_copy(dskip[r, :], dskip_all[r, :].rearrange("p (t h) -> p t h", h=2)[:, :, half]))
            b = wait_full("small", 0)
            dve.tensor_scalar(dts[:, 0, :], bank(b)[0:SH, 0:TOK], ssd_par[:, 0:1], None, ALU.add).then_inc(s["dt_u"], 1)
            dve.wait_ge(s["dt_u"], 1)
            dve.scalar_tensor_tensor(dts[:, 1, :], dts[:, 0, :], -1.0, dts[:, 0, :], ALU.mult,
                                     ALU.max).then_inc(s["dt_u"], 1)
            dve.wait_ge(s["dt_e"], 2)
            e, den, z, z2 = dts[:, 2, :], dts[:, 3, :], dts[:, 4, :], dts[:, 5, :]
            link(dve.tensor_scalar(den, e, 2.0, None, ALU.add))
            link(dve.reciprocal(den, den))
            link(dve.tensor_tensor(z, e, den, ALU.mult))
            link(dve.tensor_tensor(z2, z, z, ALU.mult))
            poly = den
            link(dve.tensor_scalar(poly, z2, 1 / 15, None, ALU.mult))
            for k in (13, 11, 9, 7, 5, 3):
                link(dve.scalar_tensor_tensor(poly, poly, 1 / k, z2, ALU.add, ALU.mult))
            link(dve.scalar_tensor_tensor(poly, poly, 1.0, z, ALU.add, ALU.mult))
            link(dve.tensor_scalar(z, dts[:, 0, :], 0.0, None, ALU.max))
            link(dve.scalar_tensor_tensor(dts[:, 0, :], poly, 2.0, z, ALU.mult, ALU.add))
            link(dve.tensor_scalar(dts[:, 3, :], dts[:, 0, :], ssd_par[:, 2:3], -1.0, ALU.mult, ALU.mult))
            for ch in range(TB):
                t = slice(ch * P, (ch + 1) * P)
                ins = dve.tensor_tensor_scan(dts[:, 1, t], consts[0:SH, C_ONE:C_ONE + P], dts[:, 3, t], 0.0,
                                             ALU.mult, ALU.add)
            ins.then_inc(s["dt_u"], 1)

            def conv(j):
                b = wait_full("xbc", j)
                if j >= 2:
                    dve.wait_ge(s["conv_done"], j - 1)
                for m in range(2):
                    t = 2 * j + m
                    acc, u = convb[:, t % 4, :], bank2(b)[:, m, :]
                    link(dve.tensor_scalar(acc, u, col("conv_w_2", 3 * (XBC // P) + t), col("conv_b_2", t),
                                           ALU.mult, ALU.add))
                    for tap in (2, 1, 0):
                        sh = CONV - 1 - tap
                        ins = dve.scalar_tensor_tensor(acc[:, sh:], u[:, 0:TOK - sh], col("conv_w_2", tap * (XBC // P) + t),
                                                       acc[:, sh:], ALU.mult, ALU.add)
                        if tap:
                            link(ins)
                    if m == 0:
                        link(ins)
                ins.then_inc(made[b], 1)

            for j in range(12):
                conv(j)
                if j == 0:
                    rope(("ropek", 0), kpe[64:64 + ROT, :], 64, 1)
                if j == 2:
                    norm(6)
                    norm(7)
                if j == 4:
                    dve.wait_ge(s["dt_e"], 3)
                    dve.tensor_tensor(dts[:, 5, 0:P], dts[:, 4, 0:P], dts[:, 0, 0:P], ALU.mult).then_inc(s["dt_ready"], 1)

            wait_made("dtT", 0)
            for g in range(NG):
                if g:
                    wait_full("y", g - 1, 0)
                    wait_full("y", g - 1, 1)
                for q in range(4):
                    dve.wait_ge(s["ea_ready"], 4 * g + q + 1)
                    b = wait_full("acum", g, q)
                    for hh in range(2):
                        for ch in range(TB):
                            h = HPG * g + 2 * q + hh
                            ins = dve.scalar_tensor_tensor(dec[:, 2 * q + hh, ch * P:(ch + 1) * P],
                                                           bank2(b)[:, hh, ch * P:(ch + 1) * P], dtn[:, ch, h:h + 1],
                                                           cap, ALU.subtract, ALU.min)
                    ins.then_inc(made[b], 1)
                b = wait_full("cb", g)
                for h in range(HPG):
                    dve.wait_ge(s["dec_ready"], 4 * g + h // 2 + 1)
                    for ch in range(TB):
                        d = dec[:, h, ch * P:(ch + 1) * P]
                        ins = dve.scalar_tensor_tensor(d, d, dtn[:, 2 + ch, HPG * g + h:HPG * g + h + 1],
                                                       bank(b)[:, ch * P:(ch + 1) * P], ALU.mult, ALU.mult)
                    ins.then_inc(s["m_ready"] if h < HPG - 1 else made[b], 1)
                for half in range(2):
                    b = wait_full("y", g, half)
                    for m in range(2):
                        t = 4 * g + 2 * half + m
                        ins = dve.scalar_tensor_tensor(rope_a[:, m, :], xbc[:, t, :], dskip[:, t:t + 1],
                                                       bank2(b)[:, m, :], ALU.mult, ALU.add)
                    ins.then_inc(made[b], 1)
                    wait_made("y", g, half)
                    zt = zs[:, 4 * g + 2 * half:4 * g + 2 * half + 2, :]
                    dve.tensor_tensor(zt, rope_a[:], zt, ALU.mult).then_inc(s["y_ready"], 1)
                    if half == 0:
                        dve.wait_ge(s["y_ready"], 2 * g + 1)
                norm(10 + g)
            for j in range(4):
                b = wait_full("souty", j)
                dve.tensor_tensor(xn[:, 2 * j:2 * j + 2, :], bank2(b), gates[:, 2 * j:2 * j + 2, :],
                                  ALU.mult).then_inc(made[b], 1)
            for j in range(8):
                rope(("rope2", j), qh[64:64 + ROT, 2 * j:2 * j + 2, :], 64)
            attention(H1, MH, 2, CAUSAL, float(QK) ** -0.5, True, lambda p, b: (om[:, p, :], bank(b)[:, 0:TOK]))
            for j in range(4):
                b = wait_full("mout", j)
                if j:
                    dve.wait_ge(s["y_ready"], 2 * NG + j)
                dve.tensor_tensor(rope_a[:], bank2(b), gates[:, KT + 2 * j:KT + 2 * j + 2, :],
                                  ALU.mult).then_inc(made[b], 1)
                wait_made("mout", j)
                dve.tensor_tensor(xn[:, 2 * j:2 * j + 2, :], xn[:, 2 * j:2 * j + 2, :], rope_a[:],
                                  ALU.add).then_inc(s["y_ready"], 1)
            norm(8)
            for j in range(4):
                add_to_x("wo2", j)
            norm(14)
            attention(H1 + MH, XH, 1, CROSS, float(TOK) ** -0.5, False,
                      lambda h, b: (xo[:, 2 * h:2 * h + 2, :], bank2(b)))
            for j in range(4):
                add_to_x("xo", j)
            norm(15)

            def first_of(eq, n, iota, cand, m, onehot):
                link(dve.scalar_tensor_tensor(cand, eq, -float(n), iota, ALU.mult, ALU.add))
                link(dve.tensor_reduce(m, cand, AX_X, ALU.min))
                link(dve.tensor_tensor(onehot, cand, m.to_broadcast([P, TB, n]), ALU.is_equal))

            def spread(t, n):
                return t.to_broadcast([P, TB, n])

            b = wait_full("logits", 0)
            lg = rt("logits")
            bias = router_b[:].rearrange("p (o e) -> p o e", o=1).to_broadcast([P, TB, EG + NE])
            dve.tensor_tensor(lg, bank(b)[:, 0:TB * (EG + NE)].rearrange("p (b e) -> p b e", b=TB), bias,
                              ALU.add).then_inc(made[b], 1)
            wait_made("logits", 0)
            iota = consts[:, C_IOTA:C_IOTA + EPG].rearrange("p (o e) -> p o e", o=1).to_broadcast([P, TB, EPG])
            glog = lg[:, :, 0:EG]
            link(dve.tensor_reduce(rt("gmax"), glog, AX_X, ALU.max))
            dve.tensor_tensor(rt("gs"), glog, spread(rt("gmax"), EG), ALU.subtract).then_inc(s["rt_sub"], 1)
            link(dve.tensor_tensor(rt("geq"), glog, spread(rt("gmax"), EG), ALU.is_equal))
            first_of(rt("geq"), EG, iota[:, :, 0:EG], rt("gcand"), rt("gm"), rt("goh"))
            pick = rt("pick").rearrange("p b (g e) -> p b g e", g=EG)
            goh4 = rt("goh").rearrange("p b (g o) -> p b g o", o=1).to_broadcast([P, TB, EG, EPG])
            link(dve.tensor_tensor(pick, lg[:, :, EG:].rearrange("p b (g e) -> p b g e", g=EG), goh4, ALU.mult))
            link(dve.tensor_reduce(rt("ein"), pick.rearrange("p b g e -> p b e g"), AX_X, ALU.add))
            link(dve.tensor_reduce(rt("v1"), rt("ein"), AX_X, ALU.max))
            link(dve.tensor_tensor(rt("eq1"), rt("ein"), spread(rt("v1"), EPG), ALU.is_equal))
            first_of(rt("eq1"), EPG, iota, rt("cand"), rt("m"), rt("oh1"))
            link(dve.scalar_tensor_tensor(rt("rest"), rt("oh1"), NEG, rt("ein"), ALU.mult, ALU.add))
            link(dve.tensor_reduce(rt("v2"), rt("rest"), AX_X, ALU.max))
            dve.tensor_tensor(rt("ds"), rt("v2"), rt("v1"), ALU.subtract).then_inc(s["rt_sub"], 1)
            link(dve.tensor_tensor(rt("eq2"), rt("rest"), spread(rt("v2"), EPG), ALU.is_equal))
            first_of(rt("eq2"), EPG, iota, rt("cand"), rt("m"), rt("oh2"))
            dve.wait_ge(s["rt_exp"], 2)
            link(dve.tensor_reduce(rt("gsum"), rt("ge"), AX_X, ALU.add))
            link(dve.reciprocal(rt("gw"), rt("gsum")))
            link(dve.tensor_scalar(rt("dsum"), rt("de"), 1.0, None, ALU.add))
            link(dve.reciprocal(rt("w1"), rt("dsum")))
            link(dve.tensor_tensor(rt("w2"), rt("de"), rt("w1"), ALU.mult))
            link(dve.tensor_tensor(rt("oh1"), rt("oh1"), spread(rt("w1"), EPG), ALU.mult))
            link(dve.tensor_tensor(rt("oh2"), rt("oh2"), spread(rt("w2"), EPG), ALU.mult))
            link(dve.tensor_tensor(rt("oh1"), rt("oh1"), rt("oh2"), ALU.add))
            link(dve.tensor_tensor(rt("oh1"), rt("oh1"), spread(rt("gw"), EPG), ALU.mult))
            w_e = rt("oh1").rearrange("p b (o e) -> p b o e", o=1).to_broadcast([P, TB, EG, EPG])
            dve.tensor_tensor(rt("comb").rearrange("p b (g e) -> p b g e", g=EG), goh4, w_e,
                              ALU.mult).then_inc(s["comb_t"], 1)

            u, downs = FILL["moe", "first"]

            def expert(it, n, first):
                dve.wait_ge(made[n], it + (u[n] + 1))
                dve.wait_ge(full[2 + n], it + (u[2 + n] + 1))
                dve.tensor_tensor(sgate[:, n, :], sgate[:, n, :], bank(2 + n), ALU.mult).then_inc(made[2 + n], 1)
                dve.wait_ge(made[2 + n], it + (u[2 + n] + 1))
                if first:
                    dve.wait_ge(s["comb_in"], 64)
                else:
                    dve.wait_ge(s["down_done"], it * 2 + (downs + n - 1))
                cw = comb_b[:, bass.ds(it * 2 + n, 1), :].to_broadcast([P, 2, TOK])
                dve.tensor_tensor(hid[:, n, :].rearrange("p (k t) -> p k t", k=2),
                                  sgate[:, n, :].rearrange("p (k t) -> p k t", k=2), cw,
                                  ALU.mult).then_inc(s["hid2"], 1)

            for n in range(2):
                expert(0, n, True)
            with dve.Fori(1, NE // 2) as it:
                for n in range(2):
                    expert(it, n, False)
            for j in range(4):
                add_to_x("moey", j)
            norm(16)
            for j in range(4):
                b = wait_full("outT", j)
                dve.tensor_copy(yout[:, j // 2, (j % 2) * 512:(j % 2 + 1) * 512], bank(b)).then_inc(made[b], 1)

        @block.gpsimd
        def _(pool):
            def wait_full(*key):
                b, n = FILL[key]
                pool.wait_ge(full[b], n)

            def wait_made(*key):
                b, n = FILL[key]
                pool.wait_ge(made[b], n)

            wait_made("dtT", 0)
            for g in range(NG):
                wait_made("xsn", g, 0)
                if g:
                    wait_full("state", g - 1)
                xg = xs_nat[:, 0, g * 512:(g + 1) * 512].rearrange("p (h c) -> p h c", c=64)
                wg = dtn[:, 4, HPG * g:HPG * (g + 1)].rearrange("p (h o) -> p h o", o=1).to_broadcast([P, HPG, 64])
                pool.tensor_tensor(xw.rearrange("p (h c) -> p h c", c=64), xg, wg, ALU.mult).then_inc(s["xw_ready"], 1)
                pool.wait_ge(s["ea_ready"], 4 * (g + 1))
                cg = xbc[:, ZT + NG + g, P:TOK].rearrange("p (o t) -> p o t", o=1).to_broadcast([P, HPG, P])
                pool.tensor_tensor(eac, eac, cg, ALU.mult).then_inc(s["cs_ready"], 1)
            wait_full("souty", 3)
            pool.wait_ge(s["rope_done"], 9)
            kb = kpe[64:64 + ROT, :].rearrange("p (o t) -> p o t", o=1).to_broadcast([ROT, MH, TOK])
            pool.tensor_copy(kh[64:64 + ROT, :, :], kb).then_inc(s["kpe_copied"], 1)


_INS = ["x", "positions", "norm_mix", "norm_mlp", "attn_w_qkv", "attn_w_o", "pool_w", "pool_scale",
        "mlp_w_up", "mlp_w_down", "norm_final", "mem_2", "positions_2", "norm_mix_2", "w_in_2", "conv_w_2",
        "conv_b_2", "dt_bias_2", "a_log_2", "d_skip_2", "ssd_norm_2", "w_ssd_out_2", "q_a_norm_2", "w_q_b_2",
        "kv_a_norm_2", "w_kv_b_2", "w_mla_out_2", "w_o_2", "norm_xattn_2", "norm_mem_2", "w_xq_2", "w_xkv_2",
        "w_xo_2", "norm_moe_2", "w_router_group_2", "b_router_group_2", "w_router_expert_2",
        "b_router_expert_2", "w_exp_gate_2", "w_exp_up_2", "w_exp_down_2", "norm_final_2"]


def kernel(**inputs):
    import numpy as _np
    import concourse.bacc as _bacc
    from concourse import mybir as _mybir
    from concourse.bass_utils import run_bass_kernel_spmd as _run

    nc = _bacc.Bacc("TRN2", target_bir_lowering=False, num_devices=1)
    arrays = {f"in_{name}": _np.ascontiguousarray(inputs[name]) for name in _INS}
    arrays["in_consts"] = const_array()
    arrays["in_band"] = band_array()
    args = {name[3:]: nc.dram_tensor(name, v.shape, _mybir.dt.from_np(v.dtype), kind="ExternalInput").ap()
            for name, v in arrays.items()}
    out = nc.dram_tensor("out", (1, TOK, D), _mybir.dt.float32, kind="ExternalOutput").ap()
    build_two_blocks(nc, args, out)
    return _run(nc, [arrays], core_ids=[0]).results[0]["out"]
```

```python
import math
from contextlib import ExitStack

import numpy as np

import concourse.bass as bass
from concourse import mybir

F32 = mybir.dt.float32
F32R = mybir.dt.float32r
BF16 = mybir.dt.bfloat16
I32 = mybir.dt.int32
ALU = mybir.AluOpType
ACT = mybir.ActivationFunctionType
AX_X = mybir.AxisListType.X

P = 128
TOK = 256
TB = TOK // P
D = 1024
KT = D // P
EPS = 1e-6
NEG = -1e30

H1 = 8
ROT = 32
DFF = 4096
FC = DFF // TOK
WINDOWS = (2, 4, 8, 16)

DIN = 2048
ZT = DIN // P
NG, NST = 4, 128
SH = 32
HPG = SH // NG
CONV = 4
XBC = DIN + 2 * NG * NST
MH, QK, NOPE, VH = 16, 96, 64, 64
QLR, KLR = 384, 256
XH = 4
EG, EPG = 4, 8
NE = EG * EPG
DE = 256
O_Z, O_XBC, O_DT = 0, DIN, DIN + XBC
O_QA = O_DT + SH
O_KV = O_QA + QLR
O_KR = O_KV + KLR
O_GS = O_KR + ROT
O_GM = O_GS + D

SLOTS = 4
UNITS = 4
UNIT = 1024
SLOT = 2048

C_ID, C_ONE, C_MASK, C_CAP, C_ROT, C_INVF, C_IOTA, C_N = 0, 128, 256, 640, 768, 800, 801, 812

ROWS_A = [("norm_mix", 16), ("norm_mlp", 16), ("pool_scale", 8), ("norm_final", 8), ("norm_mix_2", 8),
          ("norm_xattn_2", 8), ("norm_mem_2", 8), ("norm_moe_2", 8), ("norm_final_2", 8),
          ("q_a_norm_2", 3), ("kv_a_norm_2", 2), ("ssd_norm_2", 16)]
ROWS_B = [("conv_w_2", CONV * XBC // P), ("conv_b_2", XBC // P)]
COL = {}
for _first, _rows in ((0, ROWS_A), (P, ROWS_B)):
    for _name, _n in _rows:
        COL[_name] = _first
        _first += _n
N_A = sum(n for _, n in ROWS_A)
N_B = sum(n for _, n in ROWS_B)

A_QK, A_V1, A_BAND = 0, 4096, 8192
A_POOLZ = 0
A_ZS, A_XS, A_BC, A_XN, A_GATE = 0, 4096, 8192, 10240, 12288
A_DT = A_GATE + 3072
A_QA, A_KV, A_E, A_XW, A_ST, A_BN = 16384, 17152, 17664, 19712, 20224, 20736
A_CONV = A_E
A_MERGE, A_QH, A_KH, A_VH = 2048, 4096, 8192, 18432
A_XQ, A_XK, A_XV, A_MEM, A_MIN = 0, 2048, 4096, 8192, 10240
A_COMB, A_RT = 0, 8192
A_P = A_QA
A_SG = A_QA
A_LATE = 4096
A_OUT, A_ROWS, A_POS = 12288, 14336, 14592
ARENA = 20864


def const_array():
    c = np.zeros((P, C_N), np.float32)
    c[:, C_ID:C_ID + P] = np.eye(P)
    c[:, C_ONE:C_ONE + P] = 1.0
    i = np.arange(P)
    tri = np.where(i[None, :] <= i[:, None], 0.0, NEG)
    c[:, C_MASK:C_MASK + P] = tri
    c[:, C_MASK + 2 * P:C_MASK + 3 * P] = tri
    c[:, C_CAP:C_CAP + P] = np.where(i[None, :] >= i[:, None], 0.0, NEG)
    h = ROT // 2
    for base in (0, 64):
        for j in range(h):
            c[base + j + h, C_ROT + j] = -1.0
            c[base + j, C_ROT + j + h] = 1.0
    f = np.float32
    f1 = f(500000.0) ** (-np.arange(0, ROT, 2, dtype=f) / f(ROT))
    f2 = f(10000.0) ** (-np.arange(h, dtype=f) / f(h))
    for base, fr in ((0, f1), (64, f2)):
        c[base:base + ROT, C_INVF] = np.tile(fr.astype(f), 2)
    c[:, C_IOTA:C_IOTA + EPG] = np.arange(EPG)
    return c


def band_array():
    b = np.zeros((TOK, len(WINDOWS), TOK), np.float32)
    for g, w in enumerate(WINDOWS):
        for t in range(TOK):
            lo = max(0, t - w + 1)
            b[lo:t + 1, g, t] = np.float32(1.0) / np.float32(t + 1 - lo)
            b[t, g, t] -= np.float32(1.0)
    return b


class Heads:

    def __init__(self, first, heads, pair, s_banks, t_banks, o_banks, t_lag, o_lag, bufs, t_bufs):
        self.first, self.heads, self.pair = first, heads, pair
        self.s_banks, self.t_banks, self.o_banks = s_banks, t_banks, o_banks
        self.t_lag, self.o_lag, self.bufs, self.t_bufs = t_lag, o_lag, bufs, t_bufs

    def lead(self, n):
        return self.first + n - n % self.pair


MOBA = Heads(0, H1, 1, (0, 1), (2, 3), (4, 5), 2, 3, 3, 4)
LATENT = Heads(H1, MH, 2, (0, 1), (2,), (3,), 1, 1, 2, 2)
CROSSED = Heads(H1 + MH, XH, 1, (0, 1), (2, 3), (4, 5), 2, 3, 3, 4)


class Counts:

    def __init__(self):
        self.loads, self.fills, self.split, self.ordinal = {}, {}, [], {}
        self.freed = []
        self.bank_fills = [0] * 8
        self.bank_signals = [0] * 8

    def load(self, key, freed_by=None, kind=None):
        n = len(self.freed)
        self.loads[key] = (n % SLOTS, n // SLOTS + 1, self.freed[n - SLOTS] if n >= SLOTS else None)
        if kind:
            self.ordinal[key] = len(self.split)
            self.split.append((key, kind))
            freed_by = ("lo", 2 * len(self.split))
        self.freed.append(freed_by)

    def fill(self, bank, *key, units=None):
        self.bank_fills[bank] += 1
        if units is None:
            self.bank_signals[bank] += 1
        self.fills[key] = (bank, self.bank_fills[bank], units or self.bank_signals[bank], units is not None)

    def done(self, key, halves=2):
        return 2 * self.ordinal[key] + halves

    def fill_each(self, stage, n, banks, units=None):
        for j in range(n):
            self.fill(banks[j % len(banks)], stage, j, units=units(j) if units else None)

    def attention(self, at):
        for i in range(at.heads + at.o_lag):
            n = i - at.t_lag
            if i < at.heads:
                self.fill(at.s_banks[i % len(at.s_banks)], "S", at.first + i)
            if 0 <= n < at.heads:
                self.fill(at.t_banks[n % len(at.t_banks)], "T", at.first + n)
            n = i - at.o_lag
            if n >= 0 and n % at.pair == 0:
                self.fill(at.o_banks[n // at.pair % len(at.o_banks)], "O", at.first + n)

    def mlp(self, i):
        self.fill(2, "norm", 2 * i + 1)
        stage = f"mlp{i}"
        for n in range(2 * FC):
            self.load((stage, n), kind="cols")
        self.fills[stage, "first"] = (tuple(self.bank_fills[0:2]), self.ordinal[stage, 0])
        for b in range(2):
            self.bank_fills[b] += FC // 2
        last = (stage, 2 * FC - 1)
        self.fill_each(stage + "y", 4, (4, 5, 6, 7), lambda j: self.done(last, 1 + j // 2))

    def moe(self):
        for n in range(3 * NE):
            self.load(("moe", n), kind="cols")
        self.fills["moe", "first"] = (tuple(self.bank_fills[0:4]), self.ordinal["moe", 0])
        for b in range(4):
            self.bank_fills[b] += NE // 2
        self.fill_each("moey", 4, (4, 5, 6, 7), lambda j: self.done(("moe", 3 * NE - 1), 1 + j // 2))


def plan():
    c = Counts()
    c.fill(0, "cols", 0)
    c.fill_each("xT", 4, (1, 2, 3, 4))
    c.fill(0, "norm", 0)
    for j in range(12):
        c.load(("qkv", j), kind="cols" if j < 8 else "k")
    for j in range(8):
        c.fill(j % 2, "qk", j, units=c.done(("qkv", j)))
        c.fill(2 + j % 2, "rope1", j)
    c.fill_each("v1", 4, (0, 1), lambda j: c.done(("qkv", 8 + j)))
    c.attention(MOBA)
    for j in range(4):
        c.load(("wo1", j), kind="cols")
    c.fill_each("wo1", 4, (6, 7), lambda j: c.done(("wo1", j)))
    c.mlp(0)
    c.fill(6, "norm", 2)
    c.load(("pool", 0), kind="k")
    c.fill_each("poolz", 4, (0, 1, 4, 5), lambda g: c.done(("pool", 0), 1 + g // 2))
    c.fill_each("pooly", 4, (2, 3))
    c.mlp(1)
    c.fill(0, "norm", 4)
    c.fill(1, "norm", 5)
    for j in range(32):
        c.load(("win", j), ("small", 3) if j == 3 else None, kind=None if j == 3 else "cols")
    c.fill_each("small", 3, (0, 1), lambda j: c.done(("win", j)))
    c.fill(1, "small", 3)
    c.fill(4, "ropek", 0)
    c.fill_each("xbc", 12, (2, 3), lambda j: c.done(("win", 4 + j)))
    c.fill(0, "norm", 6)
    c.fill(1, "norm", 7)
    c.fill(0, "dtT", 0)
    c.fill_each("z", 8, (4, 5), lambda j: c.done(("win", 16 + j)))
    c.fill_each("gates", 8, (6, 7), lambda j: c.done(("win", 24 + j)))
    for g in range(NG):
        c.fill(0, "cb", g)
        c.fill(1, "bn", g)
        c.fill(2, "xsn", g, 0)
        c.fill(3, "xsn", g, 1)
        for q in range(4):
            c.fill(4 + q % 2, "acum", g, q)
        c.fill(1, "state", g)
        c.fill(2, "y", g, 0)
        c.fill(3, "y", g, 1)
        c.fill(0, "norm", 10 + g)
    for j in range(4):
        c.load(("qb", j), ("qh", 2 * j + 1))
    for j in range(8):
        c.fill(j % 2, "qh", j)
        c.fill(2 + j % 2, "rope2", j)
    for j in range(2):
        c.load(("kvb", j), ("vh", 2 * j + 1))
    c.fill_each("kh", 8, (0, 1))
    c.fill_each("vh", 4, (2, 3))
    for j in range(8):
        c.load(("sout", j), ("down", j + 1) if j < 7 else ("souty", 3))
    c.fill_each("souty", 4, (4, 5, 6, 7))
    c.attention(LATENT)
    for j in range(4):
        c.load(("mout", j), kind="cols")
    c.fill_each("mout", 4, (6, 7), lambda j: c.done(("mout", j)))
    for j in range(4):
        c.load(("wo2", j), ("wo2", j))
    c.fill_each("wo2", 4, (4, 5))
    c.fill_each("memT", 4, (0, 1, 2, 3))
    c.fill(0, "norm", 8)
    c.fill(0, "norm", 14)
    for j in range(8):
        c.load(("xkv", j), ("xk", j) if j < 4 else ("xv", j - 4))
    c.fill_each("xk", 4, (3, 4))
    c.fill_each("xv", 4, (5, 6))
    for j in range(4):
        c.load(("xq", j), kind="cols")
    c.fill_each("xq", 4, (1, 2), lambda j: c.done(("xq", j)))
    c.attention(CROSSED)
    for j in range(4):
        c.load(("xo", j), kind="cols")
    c.fill_each("xo", 4, (6, 7), lambda j: c.done(("xo", j)))
    c.fill(0, "norm", 15)
    c.fill(1, "logits", 0)
    c.fill(1, "combT", 0)
    c.moe()
    c.fill(0, "norm", 16)
    c.fill_each("outT", 4, (1, 2, 3, 0))
    return c


def build_two_blocks(nc, a, out):
    c = plan()
    W, FILL, SPLIT = c.loads, c.fills, c.split

    with ExitStack() as ctx:
        def sb(name, shape, dt=F32):
            return ctx.enter_context(nc.sbuf_tensor(name, shape, dt))

        def sem(name):
            return ctx.enter_context(nc.semaphore(name))

        ring = sb("ring", [P, SLOTS, SLOT])
        consts = sb("consts_sb", [P, C_N])
        wh = sb("weights_high", [P, UNITS, UNIT], F32R)
        wl = sb("weights_low", [P, UNITS, UNIT], F32R)
        cols = sb("cols", [P, 2 * P])
        dskip = sb("dskip", [P, ZT])
        dskip_all = sb("dskip_all", [P, SH])
        ssd_par = sb("ssd_par", [SH, 4])
        sin_t = sb("sin_t", [P, TOK])
        cos_t = sb("cos_t", [P, TOK])
        x = sb("xres", [P, KT, TOK])
        xh = sb("xnorm_high", [P, KT, TOK], F32R)
        xl = sb("xnorm_low", [P, KT, TOK], F32R)
        hid_h = sb("hidden_high", [P, 2, 512], F32R)
        hid_l = sb("hidden_low", [P, 2, 512], F32R)
        sq = sb("squares", [P, KT, TOK])
        cb_sb = sb("cb_sb", [P, TOK])
        std = sb("std", [P, 3, TOK])
        std_col = sb("std_col", [P, 2, TB])
        gain_both = sb("gain_both", [P, KT])
        smax = sb("smax", [P, 3, 2])
        ssum = sb("ssum", [P, 3, 2])
        srec = sb("srec", [P, 3, 2])
        rope_a = sb("rope_a", [P, 2, TOK])
        rope_b = sb("rope_b", [P, 2, TOK])
        kpe = sb("kpe", [P, TOK])
        dta = sb("dta", [SH, 2, TOK])
        dtn = sb("dtn", [P, 5, SH])
        router_w = sb("router_w", [P, KT, EG + NE])
        router_b = sb("router_b", [P, EG + NE])
        zeros = sb("zeros", [P, 512], BF16)
        eps_col = sb("eps_col", [P, 2])
        arena = sb("arena", [P, ARENA])
        psum = ctx.enter_context(nc.psum_tensor("psum", [P, 8, 512], F32))
        comb_dram = nc.dram_tensor("comb_scratch", (NE, TOK), F32, kind="Internal").ap()

        ident, ones = consts[:, C_ID:C_ID + P], consts[:, C_ONE:C_ONE + P]
        mask3 = consts[:, C_MASK:C_MASK + 3 * P]
        cap = consts[:, C_CAP:C_CAP + P]

        def at(off, *shape):
            n = int(np.prod(shape))
            v = arena[:, off:off + n]
            if len(shape) == 2:
                return v.rearrange("p (a b) -> p a b", a=shape[0])
            if len(shape) == 3:
                return v.rearrange("p (a b c) -> p a b c", a=shape[0], b=shape[1])
            return v

        rows = at(A_ROWS, 2, P)
        pos_i = arena[:, A_POS:A_POS + TOK].bitcast(I32)
        dtt = arena[0:SH, A_DT:A_DT + 4 * TOK].rearrange("p (a t) -> p a t", a=4)
        merged = at(A_MERGE, KT, TOK)
        PROB, PROB_T = {}, {}
        for heads in (MOBA, LATENT, CROSSED):
            PROB[heads] = at(A_P, heads.bufs, 512)
            PROB_T[heads] = at(A_P + 512 * heads.bufs, heads.t_bufs, 512)
        mem = at(A_MEM, KT, TOK)
        qk = at(A_QK, 2 * H1, TOK)
        v1 = at(A_V1, TB, D)
        band = at(A_BAND, TB, 4, TOK)
        poolz = at(A_POOLZ, 4, TB, TOK)
        zs = at(A_ZS, ZT, TOK)
        xbc = at(A_XS, ZT + 2 * NG, TOK)
        xs_nat = at(A_XN, 2, TB, 512)
        gates = at(A_GATE, 2 * KT, TOK)
        qa = at(A_QA, 3, TOK)
        ckv = at(A_KV, 2, TOK)
        convb = at(A_CONV, 4, TOK)
        dec = at(A_E, HPG, TOK)
        eac = sq[:, 4:8, :].rearrange("p k t -> p (k t)").rearrange("p (h l) -> p h l", h=HPG)
        xw = at(A_XW, 512)
        st0 = at(A_ST, 512)
        bn_nat = at(A_BN, P)
        qh = at(A_QH, MH, TOK)
        kh = at(A_KH, MH, TOK)
        vh = at(A_VH, TB, D)
        xq, xk, xv = at(A_XQ, KT, TOK), at(A_XK, KT, TOK), at(A_XV, TB, D)
        comb_b = at(A_COMB, NE, TOK)
        sgate = at(A_SG, 2, 512)
        sq_late = at(A_LATE, KT, TOK)
        xin = at(A_OUT, TB, D)
        mem_in = at(A_MIN, TB, D)
        yout = at(A_OUT, TB, D)

        full = [sem(f"full{b}") for b in range(8)]
        made = [sem(f"made{b}") for b in range(8)]
        w_in = [sem(f"w_in{s}") for s in range(SLOTS)]
        s = {n: sem(n) for n in (
            "const_in", "rows_in", "x_in", "mem_in", "band_in", "pos_in", "par_in", "router_in", "zeros_set",
            "x_ready", "sq_ready", "xn_ready", "tables_ready", "dve_step", "act_step", "pool_step",
            "mem_ready", "att_max", "exp_done", "p_ready", "rope_done", "hid_ready", "gate_silu", "down_done",
            "dt_ready", "conv_ready", "conv_done", "xw_ready", "cs_ready", "ea_ready", "seg_ready", "dec_ready",
            "m_ready", "y_ready", "kpe_copied", "exp_g", "comb_t", "comb_out", "comb_in", "hid2",
            "hi_ready", "lo_ready", "units_done", "hid_high", "o_high", "both_ready", "conv_first", "col_ready", "y_scaled", "dve_both", "xt_ready", "xh_ready", "out_stored", "rt_sub", "rt_exp", "rt_sub2", "rt_exp2", "dt_u", "dt_e", "angle", "sines",
            "y_sq")}

        def bank(b):
            return psum[:, b, :]

        def bank2(b):
            return psum[:, b, :].rearrange("p (m t) -> p m t", m=2)

        def col(name, i=0):
            j = COL[name] + i
            return cols[:, j:j + 1]

        NORM = {
            0: (x, KT, "norm_mix", 0, None, "xT"),
            8: (mem, KT, "norm_mem_2", 0, mem, "memT"),
            1: (x, KT, "norm_mlp", 0, None, "wo1"),
            2: (x, KT, "norm_mix", 8, None, "mlp0y"),
            3: (x, KT, "norm_mlp", 8, None, "pooly"),
            4: (x, KT, "norm_final", 0, x, "mlp1y"),
            5: (x, KT, "norm_mix_2", 0, None, None),
            6: (qa, 3, "q_a_norm_2", 0, qa, None),
            7: (ckv, 2, "kv_a_norm_2", 0, ckv, None),
            14: (x, KT, "norm_xattn_2", 0, None, "wo2"),
            15: (x, KT, "norm_moe_2", 0, None, "xo"),
            16: (x, KT, "norm_final_2", 0, x, "moey"),
        }
        SPLIT_NORMS = [n for n in (0, 1, 2, 3, 5, 14, 15)]
        for g in range(NG):
            NORM[10 + g] = (zs[:, 4 * g:4 * g + 4, :], 4, "ssd_norm_2", 4 * g, zs[:, 4 * g:4 * g + 4, :], None)
        NORM_ORDER = [0, 1, 2, 3, 5, 4, 6, 7, 10, 11, 12, 13, 8, 14, 15, 16]
        PIECES = {n: [(0, NORM[n][1])] if n in (6, 7) else [(k, k + 2) for k in range(0, NORM[n][1], 2)]
                  for n in NORM_ORDER}
        SQ_NO, XN_NO, total, pieces = {}, {}, 0, 0
        for n in NORM_ORDER:
            XN_NO[n], SQ_NO[n] = total, pieces
            total += NORM[n][1]
            pieces += len(PIECES[n])

        RT, off = {}, 0
        for name, n in (("logits", EG + NE), ("gmax", 1), ("gs", EG), ("geq", EG), ("gcand", EG), ("gm", 1),
                        ("goh", EG), ("pick", NE), ("ein", EPG), ("v1", 1), ("eq1", EPG), ("cand", EPG), ("m", 1),
                        ("oh1", EPG), ("rest", EPG), ("v2", 1), ("ds", 1), ("eq2", EPG), ("oh2", EPG), ("ge", EG),
                        ("de", 1), ("gsum", 1), ("gw", 1), ("dsum", 1), ("w1", 1), ("w2", 1), ("comb", NE)):
            RT[name] = at(A_RT + off, TB, n)
            off += TB * n
        combT = arena[0:NE, A_RT + off:A_RT + off + TOK]

        def rt(name):
            return RT[name]

        def half_views(n, half):
            key, kind = SPLIT[n]
            slot = W[key][0]
            stage, j = key
            if kind == "k":
                src = ring[:, slot, half * UNIT:(half + 1) * UNIT].rearrange("p (k c) -> p k c", k=4)
            else:
                down = (stage[:3] == "mlp" and (j == 2 * FC - 1 or (j and j % 2 == 0))) or \
                    (stage == "moe" and (j == 3 * NE - 1 or (j > 1 and j % 3 == 1)))
                kt, width = (2, D) if down else (KT, TOK)
                cut = (0, width // 2, width)
                if key == ("win", 0):
                    width, cut = SH + P, (0, SH, SH + P)
                src = ring[:, slot, 0:kt * width].rearrange("p (k c) -> p k c", k=kt)[:, :, cut[half]:cut[half + 1]]
            kt, width = src.shape[1], src.shape[2]
            unit = (2 * n + half) % UNITS
            high, low = (t[:, unit, 0:kt * width].rearrange("p (k c) -> p k c", k=kt) for t in (wh, wl))
            return W[key], src, high, low

        block = ctx.enter_context(nc.Block())

        @block.sync
        def _(sp):
            def rows_of(w, n):
                return w.rearrange("(k p) n -> p k n", p=P)[:, :, n]

            def wait_free(freed):
                if freed is None:
                    return
                if freed[0] == "lo":
                    sp.wait_ge(s["lo_ready"], freed[1])
                elif freed[0] == "down":
                    sp.wait_ge(s["down_done"], freed[1])
                else:
                    b, _, n, _ = FILL[freed]
                    sp.wait_ge(full[b], n)

            def load(stage, j, src, cols_n):
                slot, n, freed = W[stage, j]
                wait_free(freed)
                k = src.shape[1]
                dst = ring[:, slot, 0:k * cols_n].rearrange("p (k n) -> p k n", k=k)
                sp.dma_start(dst, src).then_inc(w_in[slot], 16)

            sp.dma_start(consts[:], a["consts"]).then_inc(s["const_in"], 16)
            x_rows = a["x"].rearrange("a (b p) d -> p (a b) d", p=P)
            sp.dma_start(xin, x_rows).then_inc(s["x_in"], 16)
            for tile, table in ((0, ROWS_A), (1, ROWS_B)):
                r = 0
                for name, n in table:
                    v = a[name]
                    flat = {1: "a -> a", 2: "a b -> (a b)", 3: "a b c -> (a b c)"}[len(v.shape)]
                    v = v if len(v.shape) == 1 else v.rearrange(flat)
                    sp.dma_start(rows[r:r + n, tile, :], v.rearrange("(r c) -> r c", c=P)).then_inc(s["rows_in"], 16)
                    r += n
            sp.dma_start(pos_i[0:64, :], a["positions"].to_broadcast([64, TOK])).then_inc(s["pos_in"], 16)
            sp.dma_start(pos_i[64:P, :], a["positions_2"].to_broadcast([64, TOK])).then_inc(s["pos_in"], 16)

            wq = a["attn_w_qkv"][0]
            for j in range(12):
                load("qkv", j, rows_of(wq, slice(j * TOK, (j + 1) * TOK)), TOK)
            sp.dma_start(band, a["band"].rearrange("(b p) g t -> p b g t", p=P)).then_inc(s["band_in"], 16)
            sp.dma_start(dskip_all[:], a["d_skip_2"].to_broadcast([P, SH])).then_inc(s["par_in"], 16)
            sp.dma_start(ssd_par[:, 0:1], a["dt_bias_2"].rearrange("a h -> h a")).then_inc(s["par_in"], 16)
            sp.dma_start(ssd_par[:, 1:2], a["a_log_2"].rearrange("a h -> h a")).then_inc(s["par_in"], 16)
            sp.dma_start(router_w[:, :, 0:EG], rows_of(a["w_router_group_2"][0], slice(0, EG))).then_inc(s["router_in"], 16)
            sp.dma_start(router_w[:, :, EG:], rows_of(a["w_router_expert_2"][0], slice(0, NE))).then_inc(s["router_in"], 16)
            sp.dma_start(router_b[:, 0:EG], a["b_router_group_2"].to_broadcast([P, EG])).then_inc(s["router_in"], 16)
            sp.dma_start(router_b[:, EG:], a["b_router_expert_2"].to_broadcast([P, NE])).then_inc(s["router_in"], 16)
            for j in range(4):
                load("wo1", j, rows_of(a["attn_w_o"][0], slice(j * TOK, (j + 1) * TOK)), TOK)

            def mlp_loads(i):
                up = a["mlp_w_up"][i].rearrange("(k p) (c n) -> c p k n", p=P, n=TOK)
                down = a["mlp_w_down"][i].rearrange("(c k p) n -> c p k n", p=P, k=2)
                stage = f"mlp{i}"

                def up_down(it, n, parts=(0, 1), first=False):
                    for half in parts:
                        n0 = (2 * n - 1 + half) if n else 0
                        slot, _, freed = W[stage, n0]
                        if first:
                            wait_free(freed)
                        else:
                            sp.wait_ge(s["lo_ready"], it * 16 + 2 * (c.ordinal[stage, n0] - 3))
                        dst = ring[:, slot, :].rearrange("p (k n) -> p k n", k=(KT, 2)[half])
                        sp.dma_start(dst, (up, down)[half][it * 4 + (n - half)]).then_inc(w_in[slot], 16)

                up_down(0, 0, (0,), True)
                for n in range(1, 5):
                    up_down(0, n, first=True)
                with sp.Fori(1, 3) as it:
                    for n in range(1, 5):
                        up_down(it, n)
                for n in range(13, FC):
                    up_down(0, n, first=True)
                slot, _, freed = W[stage, 2 * FC - 1]
                wait_free(freed)
                sp.dma_start(ring[:, slot, :].rearrange("p (k n) -> p k n", k=2), down[FC - 1]).then_inc(w_in[slot], 16)

            mlp_loads(0)
            pw = a["pool_w"][0].rearrange("g (k p) n -> p (g k) n", p=P)
            load("pool", 0, pw, TOK)
            mlp_loads(1)

            wi = a["w_in_2"][0]
            for j, (c0, n) in enumerate(((O_DT, SH + P), (O_QA + P, 2 * P), (O_KV, KLR), (O_KR, ROT))):
                load("win", j, rows_of(wi, slice(c0, c0 + n)), n)
            for j in range(12):
                load("win", 4 + j, rows_of(wi, slice(O_XBC + j * TOK, O_XBC + (j + 1) * TOK)), TOK)
            for j in range(8):
                load("win", 16 + j, rows_of(wi, slice(O_Z + j * TOK, O_Z + (j + 1) * TOK)), TOK)
            for j in range(8):
                load("win", 24 + j, rows_of(wi, slice(O_GS + j * TOK, O_GS + (j + 1) * TOK)), TOK)
            for j in range(4):
                load("qb", j, rows_of(a["w_q_b_2"][0], slice(j * 4 * QK, (j + 1) * 4 * QK)), 4 * QK)
            for j in range(2):
                load("kvb", j, rows_of(a["w_kv_b_2"][0], slice(j * D, (j + 1) * D)), D)
            so = a["w_ssd_out_2"][0].rearrange("(c k p) n -> c p k n", p=P, k=2)
            for j in range(8):
                load("sout", j, so[j], D)
            for stage, w, n in (("mout", "w_mla_out_2", 4), ("wo2", "w_o_2", 4), ("xkv", "w_xkv_2", 8),
                                ("xq", "w_xq_2", 4), ("xo", "w_xo_2", 4)):
                if stage == "xkv":
                    b, _, n_o, _ = FILL["O", H1 + MH - 2]
                    sp.wait_ge(full[b], n_o)
                    sp.dma_start(mem_in, a["mem_2"].rearrange("a (b p) d -> p (a b) d", p=P)).then_inc(s["mem_in"], 16)
                for j in range(n):
                    load(stage, j, rows_of(a[w][0], slice(j * TOK, (j + 1) * TOK)), TOK)
            wg = a["w_exp_gate_2"][0].rearrange("e (k p) n -> e p k n", p=P)
            wu = a["w_exp_up_2"][0].rearrange("e (k p) n -> e p k n", p=P)
            wd = a["w_exp_down_2"][0].rearrange("e (k p) n -> e p k n", p=P)

            def expert_loads(it, n, parts=(0, 1, 2), first=False):
                for part in parts:
                    i = 3 * n - 1 + part if n else part
                    slot, _, freed = W["moe", i]
                    if first:
                        wait_free(freed)
                    else:
                        sp.wait_ge(s["lo_ready"], it * 24 + 2 * (c.ordinal["moe", i] - 3))
                    dst = ring[:, slot, :].rearrange("p (k n) -> p k n", k=(KT, KT, 2)[part])
                    sp.dma_start(dst, (wg, wu, wd)[part][it * 4 + (n - part // 2)]).then_inc(w_in[slot], 16)

            expert_loads(0, 0, (0, 1), True)
            for n in range(1, 5):
                expert_loads(0, n, first=True)
            with sp.Fori(1, 7) as it:
                for n in range(1, 5):
                    expert_loads(it, n)
            for n in range(29, NE):
                expert_loads(0, n, first=True)
            slot, _, freed = W["moe", 3 * NE - 1]
            wait_free(freed)
            sp.dma_start(ring[:, slot, :].rearrange("p (k n) -> p k n", k=2), wd[NE - 1]).then_inc(w_in[slot], 16)
            o = out.rearrange("a (b p) d -> p (a b) d", p=P)
            for b in range(TB):
                for half in range(2):
                    bk, n, _, _ = FILL["outT", 2 * b + half]
                    sp.wait_ge(made[bk], n)
                sp.dma_start(o[:, b, :], yout[:, b, :]).then_inc(s["out_stored"], 16)
            sp.wait_ge(s["out_stored"], 16 * TB)

        @block.tensor
        def _(pe):
            def open_bank(*key):
                b, n, _, _ = FILL[key]
                if n > 1:
                    pe.wait_ge(made[b], n - 1)
                return b

            def wait_made(*key):
                b, n, _, _ = FILL[key]
                pe.wait_ge(made[b], n)

            def weights(stage, j, k, n):
                slot, no, _ = W[stage, j]
                pe.wait_ge(w_in[slot], 16 * no)
                return ring[:, slot, 0:k * n].rearrange("p (k n) -> p k n", k=k)

            def norm_sum(n, squares=sq):
                tiles = NORM[n][1]
                b = open_bank("norm", n)
                for piece, (k0, k1) in enumerate(PIECES[n]):
                    pe.wait_ge(s["sq_ready"], SQ_NO[n] + piece + 1)
                    for k in range(k0, k1):
                        mm = pe.matmul(bank(b)[:, 0:TOK], ones, squares[:, k, :], start=(k == 0), stop=(k == tiles - 1))
                mm.then_inc(full[b], 1)

            def product(b, w, src, kt, parts):
                for m, (p0, c0, width) in enumerate(parts):
                    for k in range(kt):
                        mm = pe.matmul(bank2(b)[p0:p0 + width, m, :], w[:, k, c0:c0 + width], src[:, k, :],
                                       start=(k == 0), stop=(k == kt - 1))
                return mm

            BOTH = ((0, 0, P), (0, P, P))

            def project(stage, j, key, src, parts=BOTH, n=TOK):
                b = open_bank(*key)
                w = weights(stage, j, KT, n)
                product(b, w, src, KT, parts).then_inc(full[b], 1)

            def three(out, lh, ll, rh, rl, start, stop, **more):
                pe.matmul(out, lh, rh, start=start, stop=False, **more)
                pe.matmul(out, lh, rl, start=False, stop=False, **more)
                return pe.matmul(out, ll, rh, start=False, stop=stop, **more)

            def split_half(n, half, shift=0):
                _, _, high, low = half_views(n, half)
                pe.wait_ge(s["lo_ready"], shift + (2 * n + half + 1))
                return high, low

            def project_split(n, b, xn_from=None, shift=0):
                for m in range(2):
                    high, low = split_half(n, m, shift)
                    width = high.shape[2]
                    for k in range(KT):
                        if xn_from is not None and m == 0:
                            pe.wait_ge(s["xn_ready"], xn_from + k + 1)
                        mm = three(bank2(b)[0:width, m, :], high[:, k, :], low[:, k, :], xh[:, k, :], xl[:, k, :],
                                   k == 0, k == KT - 1)
                    mm.then_inc(s["units_done"], 1)

            def project_split_natural(n, b):
                for half in range(2):
                    high, low = split_half(n, half)
                    for tb in range(TB):
                        t = slice(tb * P, (tb + 1) * P)
                        for k in range(4):
                            kk = 4 * half + k
                            mm = three(bank2(b)[:, tb, :], xh[:, kk, t], xl[:, kk, t], high[:, k, :], low[:, k, :],
                                       kk == 0 and tb == 0, kk == KT - 1, skip_group_check=True)
                    mm.then_inc(s["units_done"], 1)

            def project_natural(stage, j, key, src):
                b = open_bank(*key)
                w = weights(stage, j, KT, TOK)
                for tb in range(TB):
                    for k in range(KT):
                        mm = pe.matmul(bank2(b)[:, tb, :], src[:, k, tb * P:(tb + 1) * P], w[:, k, :],
                                       start=(k == 0), stop=(k == KT - 1))
                mm.then_inc(full[b], 1)

            def rotate(key, src, heads=2):
                b = open_bank(*key)
                p0 = src[1]
                pe.matmul(bank(b)[p0:p0 + ROT, 0:heads * TOK], consts[p0:p0 + ROT, C_ROT:C_ROT + ROT], src[0],
                          start=True, stop=True).then_inc(full[b], 1)

            def attention(at, scores, values, key_blocks, meanwhile=None):
                for i in range(at.heads + at.o_lag):
                    if i < at.heads:
                        b = open_bank("S", at.first + i)
                        scores(i, b).then_inc(full[b], 1)
                    n = i - at.t_lag
                    if 0 <= n < at.heads:
                        b = open_bank("T", at.first + n)
                        pe.wait_ge(s["p_ready"], 2 * (at.first + n + 1))
                        for src, dst in key_blocks:
                            mm = pe.transpose(bank(b)[:, dst:dst + P], PROB[at][:, n % at.bufs, src:src + P], ident)
                        mm.then_inc(full[b], 1)
                    if meanwhile is not None:
                        meanwhile(i)
                    n = i - at.o_lag
                    if n >= 0:
                        lead = at.lead(n)
                        b = open_bank("O", lead) if n % at.pair == 0 else FILL["O", lead][0]
                        wait_made("T", at.first + n)
                        mm = values(n, b, PROB_T[at][:, n % at.t_bufs, :])
                        if n % at.pair == at.pair - 1:
                            mm.then_inc(full[b], 1)

            CAUSAL = ((0, 0), (P, P), (2 * P, 2 * P))
            CROSS = ((0, 0), (P, 2 * P), (2 * P, P), (3 * P, 3 * P))

            def mlp(i):
                stage = f"mlp{i}"
                u, first = FILL[stage, "first"]
                for b in range(4):
                    open_bank(stage + "y", b)

                def up(it, n, xn_from=None):
                    b = n % 2
                    pe.wait_ge(made[b], it * 2 + (u[b] + n // 2))
                    project_split(first + (2 * n - 1 if n else 0), b, xn_from, shift=it * 16)

                def down(it, n, last=False):
                    pe.wait_ge(s["hid_ready"], it * 4 + (FC * i + n + 1))
                    add_down(first + (2 * n + 2 if not last else 2 * n + 1), n % 2, it * 16, last)

                clear_sums()
                up(0, 0, XN_NO[2 * i + 1])
                norm_sum(2 * i + 1, sq_late)
                with pe.Fori(0, 3) as it:
                    for n in range(1, 5):
                        up(it, n)
                        down(it, n - 1)
                for n in range(13, FC):
                    up(0, n)
                    down(0, n - 1)
                down(0, FC - 1, last=True)

            def clear_sums():
                pe.wait_ge(s["zeros_set"], 1)
                for b in range(4, 8):
                    pe.matmul(bank(b), zeros[:, 0:P], zeros[:, :], start=True, stop=False, skip_group_check=True)

            def add_down(n, buf, shift, last):
                hh = hid_h[:, buf, :].rearrange("p (k t) -> p k t", k=2)
                hl = hid_l[:, buf, :].rearrange("p (k t) -> p k t", k=2)
                for half in range(2):
                    high, low = split_half(n, half, shift)
                    for mm_ in range(4):
                        m = 4 * half + mm_
                        cc = slice(mm_ * P, (mm_ + 1) * P)
                        for k in range(2):
                            mm = three(bank2(4 + m // 2)[:, m % 2, :], high[:, k, cc], low[:, k, cc], hh[:, k, :],
                                       hl[:, k, :], False, last and k == 1, skip_group_check=True)
                    mm.then_inc(s["units_done"], 1)

            def add_sums(w, src, ms, last, first):
                for m in ms:
                    for k in range(2):
                        mm = pe.matmul(bank2(4 + m // 2)[:, m % 2, :], w[:, k, m * P:(m + 1) * P], src[:, k, :],
                                       start=(first and k == 0 and m % 2 == 0), stop=(last and k == 1),
                                       skip_group_check=True)
                        if last and m % 2 == 1 and k == 1:
                            mm.then_inc(full[4 + m // 2], 1)
                if not last and m == KT - 1:
                    mm.then_inc(s["down_done"], 1)

            pe.wait_ge(s["const_in"], 16)
            pe.wait_ge(s["x_in"], 16)
            for j in range(4):
                b = open_bank("xT", j)
                for m in range(2):
                    for tb in range(TB):
                        mm = pe.transpose(bank2(b)[:, m, tb * P:(tb + 1) * P],
                                          xin[:, tb, (2 * j + m) * P:(2 * j + m + 1) * P], ident)
                mm.then_inc(full[b], 1)
            pe.wait_ge(s["rows_in"], 16 * (len(ROWS_A) + len(ROWS_B)))
            b = open_bank("cols", 0)
            pe.transpose(bank(b)[:, 0:N_A], rows[0:N_A, 0, :], consts[0:N_A, C_ID:C_ID + N_A])
            pe.transpose(bank(b)[:, P:P + N_B], rows[0:N_B, 1, :], consts[0:N_B, C_ID:C_ID + N_B]).then_inc(full[b], 1)
            norm_sum(0)

            def rope1(j):
                wait_made("qk", j)
                rotate(("rope1", j), (qk[0:ROT, 2 * j:2 * j + 2, :], 0))

            for j in range(8):
                project_split(j, open_bank("qk", j), XN_NO[0] if j == 0 else None)
                if j:
                    rope1(j - 1)
            project_split_natural(8, open_bank("v1", 0))
            rope1(7)
            for j in range(1, 4):
                project_split_natural(8 + j, open_bank("v1", j))

            def scores1(h, b):
                pe.matmul(bank(b)[:, 0:P], qk[:, h, 0:P], qk[:, H1 + h, 0:P], start=True, stop=True)
                return pe.matmul(bank(b)[:, P:3 * P], qk[:, h, P:TOK], qk[:, H1 + h, :], start=True, stop=True)

            def values1(h, b, pt):
                pe.matmul(bank(b)[:, 0:TOK], v1[:, 0, h * P:(h + 1) * P], pt[:, 0:TOK], start=True, stop=False)
                return pe.matmul(bank(b)[:, P:TOK], v1[:, 1, h * P:(h + 1) * P], pt[:, TOK:TOK + P],
                                 start=False, stop=True)

            pe.wait_ge(s["rope_done"], 8)
            for j in range(2, 4):
                wait_made("v1", j)
            attention(MOBA, scores1, values1, CAUSAL)
            for h in range(H1 - 2, H1):
                wait_made("O", h)
            for j in range(4):
                project_split(c.ordinal["wo1", j], open_bank("wo1", j))
            mlp(0)

            for half in range(2):
                high, low = split_half(c.ordinal["pool", 0], half)
                for g in (2 * half, 2 * half + 1):
                    b = open_bank("poolz", g)
                    pe.wait_ge(s["xn_ready"], XN_NO[2] + 2 * g + 2)
                    for tb in range(TB):
                        t = slice(tb * P, (tb + 1) * P)
                        for k in range(2):
                            kk = 2 * (g % 2) + k
                            mm = three(bank2(b)[:, tb, :], xh[:, 2 * g + k, t], xl[:, 2 * g + k, t], high[:, kk, :],
                                       low[:, kk, :], k == 0, k == 1)
                mm.then_inc(s["units_done"], 1)
                if half == 0:
                    b = open_bank("norm", 2)
                    pe.wait_ge(s["sq_ready"], SQ_NO[2] + KT // 2)
                    for tb in range(TB):
                        for k in range(KT):
                            mm = pe.matmul(bank(b)[:, tb:tb + 1], sq_late[:, k, tb * P:(tb + 1) * P], ones[:, 0:1],
                                           start=(k == 0), stop=(k == KT - 1))
                    mm.then_inc(full[b], 1)
            pe.wait_ge(s["band_in"], 16)
            for g in range(4):
                wait_made("poolz", g)
                b = open_bank("pooly", g)
                for m in range(2):
                    pe.matmul(bank2(b)[:, m, :], poolz[:, g, 0, m * P:(m + 1) * P], band[:, 0, g, :],
                              start=True, stop=False)
                    mm = pe.matmul(bank2(b)[:, m, P:TOK], poolz[:, g, 1, m * P:(m + 1) * P], band[:, 1, g, P:TOK],
                                   start=False, stop=True)
                mm.then_inc(full[b], 1)
            mlp(1)

            banks = [open_bank("norm", n) for n in (4, 5)]
            for piece in range(KT // 2):
                for i, squares in enumerate((sq, sq_late)):
                    pe.wait_ge(s["sq_ready"], SQ_NO[5] + 2 * piece + i + 1)
                    for k in (2 * piece, 2 * piece + 1):
                        mm = pe.matmul(bank(banks[i])[:, 0:TOK], ones, squares[:, k, :], start=(k == 0), stop=(k == KT - 1))
                    if piece == KT // 2 - 1:
                        mm.then_inc(full[banks[i]], 1)

            for j in range(3):
                project_split(c.ordinal["win", j], open_bank("small", j), XN_NO[5] if j == 0 else None)
            project("win", 3, ("small", 3), sq, ((64, 0, ROT),), ROT)
            for j in range(12):
                project_split(c.ordinal["win", 4 + j], open_bank("xbc", j))
                if j == 0:
                    wait_made("small", 3)
                    rotate(("ropek", 0), (kpe[64:64 + ROT, :], 64), 1)
                if j == 1:
                    norm_sum(6)
                    norm_sum(7)
            b = open_bank("dtT", 0)
            pe.wait_ge(s["dt_ready"], 1)
            for i, src in enumerate((dta[:, 1, 0:P], dta[:, 1, P:TOK], dta[:, 0, 0:P], dta[:, 0, P:TOK], dtt[:, 3, 0:P])):
                mm = pe.transpose(bank(b)[:, SH * i:SH * (i + 1)], src, consts[0:SH, C_ID:C_ID + SH])
            mm.then_inc(full[b], 1)
            for j in range(8):
                project_split(c.ordinal["win", 16 + j], open_bank("z", j))

            def gate_chunk(j):
                project_split(c.ordinal["win", 24 + j], open_bank("gates", j))

            pe.wait_ge(s["conv_done"], 12)
            for g in range(NG):
                b = open_bank("cb", g)
                for ch in range(TB):
                    mm = pe.matmul(bank(b)[:, ch * P:(ch + 1) * P], xbc[:, ZT + g, ch * P:(ch + 1) * P],
                                   xbc[:, ZT + NG + g, ch * P:(ch + 1) * P], start=True, stop=True)
                mm.then_inc(full[b], 1)
                b = open_bank("bn", g)
                pe.transpose(bank(b)[:, 0:P], xbc[:, ZT + g, 0:P], ident).then_inc(full[b], 1)
                for ch in range(TB):
                    b = open_bank("xsn", g, ch)
                    for i in range(4):
                        mm = pe.transpose(bank(b)[:, i * P:(i + 1) * P], xbc[:, 4 * g + i, ch * P:(ch + 1) * P], ident)
                    mm.then_inc(full[b], 1)
                for q in range(4):
                    b = open_bank("acum", g, q)
                    for hh in range(2):
                        h = HPG * g + 2 * q + hh
                        mm = pe.matmul(bank2(b)[:, hh, :], consts[0:SH, C_ID + h:C_ID + h + 1].to_broadcast([SH, P]),
                                       dta[:, 1, :], start=True, stop=True)
                    mm.then_inc(full[b], 1)
                wait_made("bn", g)
                pe.wait_ge(s["xw_ready"], g + 1)
                b = open_bank("state", g)
                pe.matmul(bank(b), bn_nat, xw, start=True, stop=True).then_inc(full[b], 1)
                gate_chunk(2 * g)
                wait_made("state", g)
                pe.wait_ge(s["cs_ready"], g + 1)
                wait_made("xsn", g, 0)
                wait_made("xsn", g, 1)
                for half in range(2):
                    b = open_bank("y", g, half)
                    for hp in range(4):
                        h = 4 * half + hp
                        pe.wait_ge(s["m_ready"], HPG * g + h + 1)
                        o = bank2(b)[64 * (h % 2):64 * (h % 2) + 64, (h // 2) % 2, :]
                        hc = slice(h * 64, (h + 1) * 64)
                        pe.matmul(o[:, 0:P], xs_nat[:, g % 2, 0, hc], dec[:, h, 0:P], start=True, stop=True)
                        pe.matmul(o[:, P:TOK], xs_nat[:, g % 2, 1, hc], dec[:, h, P:TOK], start=True, stop=False)
                        mm = pe.matmul(o[:, P:TOK], st0[:, h * 64:(h + 1) * 64], eac[:, h, :], start=False, stop=True)
                    mm.then_inc(full[b], 1)
                gate_chunk(2 * g + 1)
                norm_sum(10 + g)

            def ssd_out(i):
                if i < 16:
                    if i == 0:
                        for b in range(4):
                            open_bank("souty", b)
                    j = i // 2
                    pe.wait_ge(s["xn_ready"], XN_NO[10 + j // 2] + 4)
                    w = weights("sout", j, 2, D)
                    add_sums(w, zs[:, 2 * j:2 * j + 2, :], range(4 * (i % 2), 4 * (i % 2) + 4), last=(j == 7),
                             first=(j == 0))

            def rope2(j):
                wait_made("qh", j)
                rotate(("rope2", j), (qh[64:64 + ROT, 2 * j:2 * j + 2, :], 64))

            pe.wait_ge(s["xn_ready"], XN_NO[7] + 2)
            for j in range(8):
                b = open_bank("qh", j)
                w = weights("qb", j // 2, 3, 4 * QK)
                c0 = j % 2 * 2 * QK
                product(b, w, qa, 3, ((0, c0, QK), (0, c0 + QK, QK))).then_inc(full[b], 1)
                if j:
                    rope2(j - 1)
            for j in range(8):
                b = open_bank("kh", j)
                w = weights("kvb", j // 4, 2, D)
                c0 = j % 4 * 2 * P
                product(b, w, ckv, 2, ((0, c0, NOPE), (0, c0 + P, NOPE))).then_inc(full[b], 1)
                if j == 0:
                    rope2(7)
                if j % 4 == 3:
                    wv = w.rearrange("p k (h c) -> p k h c", c=P)[:, :, :, NOPE:]
                    for tb in range(TB):
                        b = open_bank("vh", j // 4 * 2 + tb)
                        for k in range(2):
                            mm = pe.matmul(bank(b), ckv[:, k, tb * P:(tb + 1) * P], wv[:, k, :, :],
                                           start=(k == 0), stop=(k == 1))
                        mm.then_inc(full[b], 1)

            def scores2(h, b):
                pe.matmul(bank(b)[:, 0:P], qh[0:QK, h, 0:P], kh[0:QK, h, 0:P], start=True, stop=True)
                return pe.matmul(bank(b)[:, P:3 * P], qh[0:QK, h, P:TOK], kh[0:QK, h, :], start=True, stop=True)

            def values2(h, b, pt):
                o = bank(b)[64 * (h % 2):64 * (h % 2) + 64, :]
                pe.matmul(o[:, 0:TOK], vh[:, 0, h * VH:(h + 1) * VH], pt[:, 0:TOK], start=True, stop=False,
                          skip_group_check=True)
                return pe.matmul(o[:, P:TOK], vh[:, 1, h * VH:(h + 1) * VH], pt[:, TOK:TOK + P],
                                 start=False, stop=True, skip_group_check=True)

            pe.wait_ge(s["rope_done"], 17)
            pe.wait_ge(s["kpe_copied"], 1)
            for key in (("kh", 6), ("kh", 7), ("vh", 2), ("vh", 3)):
                wait_made(*key)
            attention(LATENT, scores2, values2, CAUSAL, ssd_out)
            wait_made("O", H1 + MH - 2)
            for j in range(4):
                project_split(c.ordinal["mout", j], open_bank("mout", j))
            pe.wait_ge(s["y_ready"], 2 * NG + 4)
            pe.wait_ge(s["mem_in"], 16)
            for j in range(4):
                b = open_bank("memT", j)
                for m in range(2):
                    for tb in range(TB):
                        mm = pe.transpose(bank2(b)[:, m, tb * P:(tb + 1) * P],
                                          mem_in[:, tb, (2 * j + m) * P:(2 * j + m + 1) * P], ident)
                mm.then_inc(full[b], 1)
            norm_sum(8)
            for j in range(4):
                project("wo2", j, ("wo2", j), merged)
            norm_sum(14)

            pe.wait_ge(s["xn_ready"], XN_NO[8] + KT)
            for j in range(4):
                project("xkv", j, ("xk", j), mem)
            for j in range(4):
                project_natural("xkv", 4 + j, ("xv", j), mem)
            for j in range(4):
                project_split(c.ordinal["xq", j], open_bank("xq", j), XN_NO[14] if j == 0 else None)

            def scores3(h, b):
                for qb in range(2):
                    for kk in range(2):
                        mm = pe.matmul(bank2(b)[:, qb, :], xq[:, 2 * h + kk, qb * P:(qb + 1) * P],
                                       xk[:, 2 * h + kk, :], start=(kk == 0), stop=(kk == 1))
                return mm

            def values3(h, b, pt):
                for m in range(2):
                    for kb in range(2):
                        mm = pe.matmul(bank2(b)[:, m, :], xv[:, kb, (2 * h + m) * P:(2 * h + m + 1) * P],
                                       pt[:, kb * TOK:(kb + 1) * TOK], start=(kb == 0), stop=(kb == 1))
                return mm

            for stage in ("xk", "xv", "xq"):
                for j in (2, 3):
                    wait_made(stage, j)
            attention(CROSSED, scores3, values3, CROSS)
            for h in (XH - 2, XH - 1):
                wait_made("O", H1 + MH + h)
            for j in range(4):
                project_split(c.ordinal["xo", j], open_bank("xo", j))
            norm_sum(15)

            pe.wait_ge(s["router_in"], 64)
            pe.wait_ge(s["xn_ready"], XN_NO[15] + KT)
            b = open_bank("logits", 0)
            for tb in range(TB):
                for k in range(KT):
                    mm = pe.matmul(bank(b)[:, tb * (EG + NE):(tb + 1) * (EG + NE)], sq[:, k, tb * P:(tb + 1) * P],
                                   router_w[:, k, :], start=(k == 0), stop=(k == KT - 1))
            mm.then_inc(full[b], 1)

            for b in range(4):
                open_bank("moey", b)
            clear_sums()
            u, first = FILL["moe", "first"]

            def gate_up(it, n):
                for part in range(2):
                    b = 2 * part + n % 2
                    pe.wait_ge(made[b], it * 2 + (u[b] + n // 2))
                    project_split(first + (3 * n - 1 + part if n else part), b, shift=it * 24)

            def expert_down(it, n, last=False):
                pe.wait_ge(s["hid_ready"], it * 4 + (2 * FC + n + 1))
                add_down(first + (3 * n + 4 if not last else 3 * n + 2), n % 2, it * 24, last)

            b = open_bank("combT", 0)
            gate_up(0, 0)
            pe.wait_ge(s["comb_t"], 1)
            for tb in range(TB):
                mm = pe.transpose(bank(b)[0:NE, tb * P:(tb + 1) * P], rt("comb")[:, tb, :], ident)
            mm.then_inc(full[b], 1)
            with pe.Fori(0, 7) as it:
                for n in range(1, 5):
                    gate_up(it, n)
                    expert_down(it, n - 1)
            for n in range(29, NE):
                gate_up(0, n)
                expert_down(0, n - 1)
            expert_down(0, NE - 1, last=True)

            norm_sum(16)
            for j in range(4):
                b = open_bank("outT", j)
                for i in range(4):
                    k = 4 * (j % 2) + i
                    pe.wait_ge(s["xn_ready"], XN_NO[16] + k + 1)
                    mm = pe.transpose(bank(b)[:, i * P:(i + 1) * P], x[:, k, (j // 2) * P:(j // 2 + 1) * P], ident)
                mm.then_inc(full[b], 1)

        @block.scalar
        def _(act):
            def wait_full(*key):
                b, _, n, by_units = FILL[key]
                act.wait_ge(s["units_done"] if by_units else full[b], n)
                return b

            def wait_made(*key):
                b, n, _, _ = FILL[key]
                act.wait_ge(made[b], n)

            fed = [0]

            def high_half(n, half, it=0, body=0):
                (slot, no, _), src, high, _ = half_views(n, half)
                if half == 0:
                    act.wait_ge(w_in[slot], it * (16 * body // SLOTS) + 16 * no)
                u = 2 * n + half
                if u >= UNITS:
                    act.wait_ge(s["units_done"], it * (2 * body) + (u - UNITS + 1))
                act.activation(high, src, ACT.Copy).then_inc(s["hi_ready"], 1)

            def feed(halves=1):
                for _ in range(halves):
                    high_half(fed[0] // 2, fed[0] % 2)
                    fed[0] += 1

            def copy_out(dst, *key, view=None):
                b = wait_full(*key)
                act.activation(dst, view(b) if view else bank2(b), ACT.Copy).then_inc(made[b], 1)

            def norm_parts(n):
                for k in range(KT):
                    act.wait_ge(s["xt_ready"], KT * SPLIT_NORMS.index(n) + k + 1)
                    act.activation(xh[:, k, :], sq[:, k, :], ACT.Copy).then_inc(s["xh_ready"], 1)

            def squares_late(n, halves):
                feed(halves)
                norm_parts(n)
                for j in range(KT // 2):
                    act.activation(sq_late[:, 2 * j:2 * j + 2, :], x[:, 2 * j:2 * j + 2, :],
                                   ACT.Square).then_inc(s["sq_ready"], 1)

            def norm(n, halves=0, tail=0, between=None):
                src, tiles, _, _, _, after = NORM[n]
                for j, (k0, k1) in enumerate(PIECES[n]):
                    if after is not None:
                        wait_made(after, j)
                    elif n == 6:
                        wait_made("small", 0)
                        wait_made("small", 1)
                    elif n == 7:
                        wait_made("small", 2)
                    else:
                        act.wait_ge(s["y_ready"], 2 * (n - 10) + j + 1)
                    act.activation(sq[:, k0:k1, :], src[:, k0:k1, :], ACT.Square).then_inc(s["sq_ready"], 1)
                feed(halves)
                if between is not None:
                    between()
                b = wait_full("norm", n)
                if XN_NO[n]:
                    act.wait_ge(s["xn_ready"], XN_NO[n])
                act.activation(std[:, 0, :], bank(b)[:, 0:TOK], ACT.Sqrt, bias=eps_col[:, 0:1],
                               scale=1.0 / (tiles * P)).then_inc(made[b], 1)
                if n in SPLIT_NORMS:
                    norm_parts(n)
                feed(tail)

            def attention(at, segments, high, meanwhile=None):
                prob, probT = PROB[at], PROB_T[at]
                for i in range(at.heads + at.o_lag):
                    if i < at.heads:
                        n = at.first + i
                        act.wait_ge(s["att_max"], 2 * (n + 1))
                        for e, (c0, c1) in enumerate(segments):
                            act.activation(prob[:, i % at.bufs, c0:c1], prob[:, i % at.bufs, c0:c1], ACT.Exp,
                                           bias=smax[:, n % 3, e:e + 1],
                                           accum_out=ssum[:, n % 3, e:e + 1]).then_inc(s["exp_done"], 1)
                    n = i - at.t_lag
                    if 0 <= n < at.heads:
                        if n >= at.t_bufs:
                            wait_full("O", at.lead(n - at.t_bufs))
                        w = segments[-1][1]
                        copy_out(probT[:, n % at.t_bufs, 0:w], "T", at.first + n, view=lambda b: bank(b)[:, 0:w])
                    if meanwhile is not None:
                        meanwhile(i)
                    n = i - at.o_lag
                    if n >= 0 and n % at.pair == at.pair - 1:
                        b = wait_full("O", at.lead(n))
                        dst, src = high(n // at.pair, b)
                        act.activation(dst, src, ACT.Copy).then_inc(s["o_high"], 1)

            CAUSAL = ((0, P), (P, 3 * P))
            CROSS = ((0, TOK), (TOK, 2 * TOK))

            act.wait_ge(s["zeros_set"], 1)
            feed(4)
            norm(0)
            act.wait_ge(s["angle"], 1)
            act.activation(sin_t[:], rope_b[:, 0, :], ACT.Sin).then_inc(s["sines"], 1)
            act.activation(cos_t[:], rope_b[:, 1, :], ACT.Sin).then_inc(s["sines"], 1)
            for j in range(8):
                feed()
                copy_out(qk[:, 2 * j:2 * j + 2, :], "qk", j)
                feed()
            for j in range(4):
                feed()
                copy_out(v1[:, :, j * TOK:(j + 1) * TOK], "v1", j)
                feed()

            def one_tile(t, b):
                return xh[:, t, :], bank(b)[:, 0:TOK]

            def two_tiles(t, b):
                return xh[:, 2 * t:2 * t + 2, :], bank2(b)

            attention(MOBA, CAUSAL, one_tile)
            feed(6)
            squares_late(1, 2)

            def mlp_hidden(i):
                u, first = FILL[f"mlp{i}", "first"]

                def step(it, n, last=False):
                    def f(j, half):
                        high_half(first + j, half, it, 8)
                    b = n % 2
                    f(2 * n + 1 if n else 2, 0)
                    act.wait_ge(s["units_done"], it * 16 + 2 * (first + (2 * n - 1 if n else 0)) + 2)
                    act.activation(sgate[:, b, :], bank(b), ACT.Relu).then_inc(s["gate_silu"], 1)
                    f(2 * n + 1 if n else 2, 1)
                    act.wait_ge(made[b], it * 2 + (u[b] + n // 2 + 1))
                    act.activation(hid_h[:, b, :], sgate[:, b, :], ACT.Copy).then_inc(s["hid_high"], 1)
                    if n and not last:
                        f(2 * n + 2, 0)
                        f(2 * n + 2, 1)

                step(0, 0)
                b = wait_full("norm", 2 * i + 1)
                act.activation(std[:, 0, :], bank(b)[:, 0:TOK], ACT.Sqrt, bias=eps_col[:, 0:1],
                               scale=1.0 / D).then_inc(made[b], 1)
                with act.Fori(0, 3) as it:
                    for n in range(1, 5):
                        step(it, n)
                for n in range(13, FC):
                    step(0, n, n == FC - 1)
                fed[0] += 4 * FC - 4

            mlp_hidden(0)
            squares_late(2, 2)
            feed(2)
            b = wait_full("norm", 2)
            act.activation(std_col[:, 0, :], bank(b)[:, 0:TB], ACT.Sqrt, bias=eps_col[:, 0:1],
                           scale=1.0 / D).then_inc(made[b], 1)
            act.wait_ge(s["col_ready"], 1)
            for g in range(4):
                b = wait_full("poolz", g)
                for tb in range(TB):
                    ins = act.activation(poolz[:, g, tb, :], bank2(b)[:, tb, :], ACT.Copy, scale=std_col[:, 1, tb:tb + 1])
                ins.then_inc(made[b], 1)
                if g == 2:
                    feed()
            squares_late(3, 1)
            mlp_hidden(1)
            feed(2)
            for j in range(KT // 2):
                wait_made("mlp1y", j)
                act.activation(sq[:, 2 * j:2 * j + 2, :], x[:, 2 * j:2 * j + 2, :], ACT.Square).then_inc(s["sq_ready"], 1)
                for k in (2 * j, 2 * j + 1):
                    ins = act.activation(sq_late[:, k, :], x[:, k, :], ACT.Square, scale=col("norm_final", k))
                ins.then_inc(s["sq_ready"], 1)
            feed(2)
            wait_made("norm", 5)
            act.activation(std[:, 2, :], std[:, 2, :], ACT.Sqrt, bias=eps_col[:, 1:2],
                           scale=1.0 / D).then_inc(s["both_ready"], 1)
            norm_parts(5)
            b = wait_full("norm", 4)
            act.wait_ge(s["xn_ready"], XN_NO[5])
            act.activation(std[:, 0, :], bank(b)[:, 0:TOK], ACT.Sqrt, bias=eps_col[:, 0:1],
                           scale=1.0 / D).then_inc(made[b], 1)

            feed()
            act.wait_ge(s["dt_u"], 1)
            copy_out(qa[:, 0, :], "small", 0, view=lambda b: bank2(b)[:, 1, :])
            feed(2)
            copy_out(qa[:, 1:3, :], "small", 1)
            feed(2)
            copy_out(ckv, "small", 2)
            feed()
            copy_out(kpe[64:64 + ROT, :], "small", 3, view=lambda b: bank(b)[64:64 + ROT, 0:TOK])
            act.activation(ssd_par[:, 2:3], ssd_par[:, 1:2], ACT.Exp).then_inc(s["dt_e"], 1)
            act.wait_ge(s["dt_u"], 2)
            act.activation(dtt[:, 0, :], dtt[:, 1, :], ACT.Exp, scale=-1.0).then_inc(s["dt_e"], 1)
            def conv_silu(j):
                wait_made("xbc", j)
                act.activation(xbc[:, 2 * j:2 * j + 2, :], convb[:, 2 * (j % 2):2 * (j % 2) + 2, :],
                               ACT.Silu).then_inc(s["conv_done"], 1)

            def conv_first(j):
                b = wait_full("xbc", j)
                if j >= 2:
                    act.wait_ge(s["conv_done"], j - 1)
                for t in (2 * j, 2 * j + 1):
                    ins = act.activation(convb[:, t % 4, :], bank2(b)[:, t % 2, :], ACT.Identity,
                                         bias=col("conv_b_2", t), scale=col("conv_w_2", 3 * (XBC // P) + t))
                ins.then_inc(s["conv_first"], 1)

            for j in range(12):
                feed()
                conv_first(j)
                if j:
                    conv_silu(j - 1)
                feed()
                if j == 1:
                    norm(6)
                    norm(7)
                if j == 8:
                    act.wait_ge(s["dt_u"], 3)
                    act.activation(dtt[:, 2, 0:P], dta[:, 1, 0:P], ACT.Exp, bias=dta[:, 1, P - 1:P],
                                   scale=-1.0).then_inc(s["dt_e"], 1)
            conv_silu(11)
            copy_out(dtn[:], "dtT", 0, view=lambda b: bank(b)[:, 0:5 * SH].rearrange("p (a h) -> p a h", a=5))
            for j in range(8):
                feed()
                b = wait_full("z", j)
                act.activation(zs[:, 2 * j:2 * j + 2, :], bank2(b), ACT.Silu).then_inc(made[b], 1)
                feed()

            def gate(j):
                b = wait_full("gates", j)
                act.activation(gates[:, 2 * j:2 * j + 2, :], bank2(b), ACT.Sigmoid).then_inc(made[b], 1)
                feed(2 if j < 6 else 0)

            for g in range(NG):
                if g:
                    act.wait_ge(s["m_ready"], HPG * g)
                copy_out(cb_sb[:], "cb", g, view=lambda b: bank(b)[:, 0:TOK])
                copy_out(bn_nat, "bn", g, view=lambda b: bank(b)[:, 0:P])
                for ch in range(TB):
                    copy_out(xs_nat[:, g % 2, ch, :], "xsn", g, ch, view=bank)
                if g:
                    wait_full("y", g - 1, 0)
                    wait_full("y", g - 1, 1)
                for q in range(5):
                    if q < 4:
                        b = wait_full("acum", g, q)
                        act.activation(eac[:, 2 * q:2 * q + 2, :], bank2(b)[:, :, P:TOK],
                                       ACT.Exp).then_inc(s["ea_ready"], 1)
                    if q:
                        wait_made("acum", g, q - 1)
                        act.activation(dec[:, 2 * q - 2:2 * q, :], dec[:, 2 * q - 2:2 * q, :],
                                       ACT.Exp).then_inc(s["dec_ready"], 1)
                copy_out(st0, "state", g, view=bank)
                gate(2 * g)
                norm(10 + g, between=lambda: gate(2 * g + 1))
            for j in range(8):
                if j == 0:
                    act.wait_ge(s["y_ready"], 2 * NG)
                copy_out(qh[0:QK, 2 * j:2 * j + 2, :], "qh", j, view=lambda b: bank2(b)[0:QK])
            for j in range(8):
                copy_out(kh[0:NOPE, 2 * j:2 * j + 2, :], "kh", j, view=lambda b: bank2(b)[0:NOPE])
                if j % 4 == 3:
                    for tb in range(TB):
                        copy_out(vh[:, tb, j // 4 * 512:(j // 4 + 1) * 512], "vh", j // 4 * 2 + tb, view=bank)
            attention(LATENT, CAUSAL, one_tile, lambda i: feed(2 if i in (14, 15) else 0))
            feed(4)
            for j in range(4):
                copy_out(mem[:, 2 * j:2 * j + 2, :], "memT", j)
            norm(8)
            norm(14)
            for j in range(4):
                copy_out(xk[:, 2 * j:2 * j + 2, :], "xk", j)
            for j in range(4):
                copy_out(xv[:, :, j * TOK:(j + 1) * TOK], "xv", j)
            feed(4)
            for j in range(4):
                feed()
                copy_out(xq[:, 2 * j:2 * j + 2, :], "xq", j)
                feed()
            attention(CROSSED, CROSS, two_tiles)
            feed(6)
            norm(15, 2)
            act.wait_ge(s["rt_sub"], 1)
            act.activation(rt("ge"), rt("gs"), ACT.Exp).then_inc(s["rt_exp"], 1)
            act.wait_ge(s["rt_sub"], 2)
            act.activation(rt("de"), rt("ds"), ACT.Exp).then_inc(s["rt_exp"], 1)
            u, first = FILL["moe", "first"]

            def expert(it, n, last=False):
                def f(j, half):
                    high_half(first + j, half, it, 12)
                b = n % 2
                down, gate = (3 * n + 1, 3 * n + 2) if n else (2, 3)
                f(down, 0)
                act.wait_ge(s["units_done"], it * 24 + 2 * (first + (3 * n - 1 if n else 0)) + 2)
                act.activation(sgate[:, b, :], bank(b), ACT.Silu).then_inc(made[b], 1)
                f(down, 1)
                if n == 0:
                    copy_out(combT, "combT", 0, view=lambda b: bank(b)[0:NE, 0:TOK])
                    wait_made("combT", 0)
                    act.dma_start(comb_dram, combT).then_inc(s["comb_out"], 16)
                    act.wait_ge(s["comb_out"], 16)
                    for q in range(4):
                        e0 = q * NE // 4
                        src = comb_dram[e0:e0 + NE // 4, :].rearrange("(o e) t -> o e t", o=1)
                        act.dma_start(comb_b[:, e0:e0 + NE // 4, :],
                                      src.to_broadcast([P, NE // 4, TOK])).then_inc(s["comb_in"], 16)
                f(gate, 0)
                f(gate, 1)
                act.wait_ge(s["hid2"], it * 4 + (n + 1))
                act.activation(hid_h[:, b, :], sgate[:, b, :], ACT.Copy).then_inc(s["hid_high"], 1)
                if n and not last:
                    f(3 * n + 3, 0)
                    f(3 * n + 3, 1)

            expert(0, 0)
            with act.Fori(0, 7) as it:
                for n in range(1, 5):
                    expert(it, n)
            for n in range(29, NE):
                expert(0, n, n == NE - 1)
            norm(16)

        @block.vector
        def _(dve):
            steps, ropes = [0], [0]

            def link(ins):
                steps[0] += 1
                ins.then_inc(s["dve_step"], 1)
                dve.wait_ge(s["dve_step"], steps[0])

            def wait_full(*key):
                b, _, n, by_units = FILL[key]
                dve.wait_ge(s["units_done"] if by_units else full[b], n)
                return b

            def wait_made(*key):
                b, n, _, _ = FILL[key]
                dve.wait_ge(made[b], n)

            fed = [0]

            def low_half(n, half, it=0, body=0):
                _, src, high, low = half_views(n, half)
                dve.wait_ge(s["hi_ready"], it * (2 * body) + (2 * n + half + 1))
                dve.tensor_tensor(low, src, high.bitcast(F32), ALU.subtract).then_inc(s["lo_ready"], 1)

            def feed(halves=1):
                for _ in range(halves):
                    low_half(fed[0] // 2, fed[0] % 2)
                    fed[0] += 1

            def low_part(n, k):
                dve.wait_ge(s["xh_ready"], KT * SPLIT_NORMS.index(n) + k + 1)
                dve.tensor_tensor(xl[:, k, :], sq[:, k, :], xh[:, k, :].bitcast(F32),
                                  ALU.subtract).then_inc(s["xn_ready"], 1)

            def norm_parts(n, gain, inverse):
                for k in range(KT + 1):
                    if k < KT:
                        dve.scalar_tensor_tensor(sq[:, k, :], x[:, k, :], gain(k), inverse,
                                                 ALU.mult, ALU.mult).then_inc(s["xt_ready"], 1)
                    if k:
                        low_part(n, k - 1)

            def norm(n, halves=0, tail=0):
                src, tiles, gain, first, dst, _ = NORM[n]
                feed(halves)
                wait_made("norm", n)
                link(dve.reciprocal(std[:, 1, :], std[:, 0, :]))
                if n not in SPLIT_NORMS:
                    for k in range(tiles):
                        dve.scalar_tensor_tensor(dst[:, k, :], src[:, k, :], col(gain, first + k), std[:, 1, :],
                                                 ALU.mult, ALU.mult).then_inc(s["xn_ready"], 1)
                    return
                norm_parts(n, lambda k: col(gain, first + k), std[:, 1, :])
                feed(tail)

            def gained(n, j):
                gain, first = NORM[n][2:4]
                for k in (2 * j, 2 * j + 1):
                    dve.tensor_scalar(sq[:, k, :], x[:, k, :], col(gain, first + k), None,
                                      ALU.mult).then_inc(s["xt_ready"], 1)

            def add_to_x(stage, j, scale=None):
                b = wait_full(stage, j)
                dve.tensor_tensor(x[:, 2 * j:2 * j + 2, :], bank2(b), x[:, 2 * j:2 * j + 2, :],
                                  ALU.add).then_inc(made[b], 1)

            def pair_bcast(t):
                return t.rearrange("p (o t) -> p o t", o=1).to_broadcast([t.shape[0], 2, TOK])

            def rope(key, t, p0, heads=2):
                r = slice(p0, p0 + ROT)
                b = wait_full(*key)
                if heads == 2:
                    swapped, sin_b, cos_b = bank2(b)[r], pair_bcast(sin_t[r, :]), pair_bcast(cos_t[r, :])
                    ta, tb_ = rope_a[r, :, :], rope_b[r, :, :]
                else:
                    swapped, sin_b, cos_b = bank(b)[r, 0:TOK], sin_t[r, :], cos_t[r, :]
                    ta, tb_ = rope_a[r, 0, :], rope_b[r, 0, :]
                if ropes[0]:
                    dve.wait_ge(s["rope_done"], ropes[0])
                ropes[0] += 1
                dve.tensor_tensor(ta, swapped, sin_b, ALU.mult).then_inc(made[b], 1)
                wait_made(*key)
                link(dve.tensor_tensor(tb_, t, cos_b, ALU.mult))
                dve.tensor_tensor(t, ta, tb_, ALU.add).then_inc(s["rope_done"], 1)

            outputs = [0]

            def attention(at, segments, scale, masked, low, meanwhile=None):
                w = segments[-1][1]
                prob = PROB[at]
                norm_lag = at.t_lag - 1
                for i in range(at.heads + at.o_lag):
                    if i < at.heads:
                        n, buf = at.first + i, i % at.bufs
                        b = wait_full("S", n)
                        if i >= at.bufs:
                            wait_full("T", n - at.bufs)
                        if masked:
                            ins = dve.scalar_tensor_tensor(prob[:, buf, 0:w], bank(b)[:, 0:w], scale, mask3,
                                                           ALU.mult, ALU.add)
                        else:
                            ins = dve.tensor_scalar(prob[:, buf, 0:w], bank(b)[:, 0:w], scale, None, ALU.mult)
                        ins.then_inc(made[b], 1)
                        wait_made("S", n)
                        for e, (c0, c1) in enumerate(segments):
                            dve.tensor_reduce(smax[:, n % 3, e:e + 1], prob[:, buf, c0:c1], AX_X, ALU.max,
                                              negate=True).then_inc(s["att_max"], 1)
                    j = i - norm_lag
                    if 0 <= j < at.heads:
                        n, buf = at.first + j, j % at.bufs
                        dve.wait_ge(s["exp_done"], 2 * (n + 1))
                        link(dve.reciprocal(srec[:, n % 3, :], ssum[:, n % 3, :]))
                        for e, (c0, c1) in enumerate(segments):
                            dve.tensor_scalar(prob[:, buf, c0:c1], prob[:, buf, c0:c1], srec[:, n % 3, e:e + 1],
                                              None, ALU.mult).then_inc(s["p_ready"], 1)
                    if meanwhile is not None:
                        meanwhile(i)
                    n = i - at.o_lag
                    if n >= 0 and n % at.pair == at.pair - 1:
                        b = wait_full("O", at.lead(n))
                        outputs[0] += 1
                        dve.wait_ge(s["o_high"], outputs[0])
                        dst, src, high = low(n // at.pair, b)
                        dve.tensor_tensor(dst, src, high.bitcast(F32), ALU.subtract).then_inc(made[b], 1)

            def one_tile(t, b):
                return xl[:, t, :], bank(b)[:, 0:TOK], xh[:, t, :]

            def two_tiles(t, b):
                return xl[:, 2 * t:2 * t + 2, :], bank2(b), xh[:, 2 * t:2 * t + 2, :]

            CAUSAL = ((0, P), (P, 3 * P))
            CROSS = ((0, TOK), (TOK, 2 * TOK))

            dve.memset(eps_col[:, 0:1], EPS)
            link(dve.memset(eps_col[:, 1:2], EPS * EPS))
            dve.memset(zeros[:], 0.0).then_inc(s["zeros_set"], 1)
            for j in range(4):
                b = wait_full("xT", j)
                dve.tensor_copy(x[:, 2 * j:2 * j + 2, :], bank2(b)).then_inc(made[b], 1)
            b = wait_full("cols", 0)
            link(dve.tensor_copy(cols[:, 0:N_A], bank(b)[:, 0:N_A]))
            dve.tensor_copy(cols[:, P:P + N_B], bank(b)[:, P:P + N_B]).then_inc(made[b], 1)
            wait_made("cols", 0)
            i, j = COL["norm_final"], COL["norm_mix_2"]
            link(dve.tensor_tensor(gain_both[:], cols[:, i:i + KT], cols[:, j:j + KT], ALU.mult))
            feed(4)
            norm(0)

            dve.wait_ge(s["pos_in"], 32)
            dve.wait_ge(s["const_in"], 16)
            ang, turns, red, comp = rope_a[:, 0, :], rope_a[:, 1, :], rope_b[:, 0, :], rope_b[:, 1, :]
            magic = 1.5 * 2.0 ** 23
            c1 = 6.28125
            c2 = float(np.float32(round((2 * math.pi - c1) * 2 ** 20) / 2 ** 20))
            c3 = 2 * math.pi - c1 - c2
            link(dve.tensor_copy(ang, pos_i[:]))
            link(dve.tensor_scalar(ang, ang, consts[:, C_INVF:C_INVF + 1], None, ALU.mult))
            link(dve.tensor_scalar(turns, ang, 1 / (2 * math.pi), magic, ALU.mult, ALU.add))
            link(dve.tensor_scalar(turns, turns, magic, None, ALU.subtract))
            link(dve.scalar_tensor_tensor(red, turns, -c1, ang, ALU.mult, ALU.add))
            link(dve.scalar_tensor_tensor(red, turns, -c2, red, ALU.mult, ALU.add))
            link(dve.scalar_tensor_tensor(red, turns, -c3, red, ALU.mult, ALU.add))
            link(dve.tensor_scalar(red, red, 3.1415925, -3.1415925, ALU.min, ALU.max))
            link(dve.scalar_tensor_tensor(comp, red, -1.0, red, ALU.mult, ALU.max))
            dve.tensor_scalar(comp, comp, -1.0, math.pi / 2, ALU.mult, ALU.add).then_inc(s["angle"], 1)
            dve.wait_ge(s["sines"], 2)

            for j in range(8):
                feed(2)
                rope(("rope1", j), qk[0:ROT, 2 * j:2 * j + 2, :], 0)
            feed(8)
            attention(MOBA, CAUSAL, float(P) ** -0.5, True, one_tile)
            for j in range(4):
                add_to_x("wo1", j)
                wait_made("wo1", j)
                gained(1, j)
                feed(2 if j < 3 else 0)
            feed(2)
            for k in range(KT):
                low_part(1, k)

            scaled = (rope_a[:], rope_b[:])

            def mlp_square(i):
                u, first = FILL[f"mlp{i}", "first"]

                def step(it, n, last=False):
                    def f(j, half):
                        low_half(first + j, half, it, 8)
                    b = n % 2
                    f(2 * n + 1 if n else 2, 0)
                    dve.wait_ge(s["gate_silu"], it * 4 + (FC * i + n + 1))
                    dve.scalar_tensor_tensor(sgate[:, b, :], bank(b), 0.0, sgate[:, b, :], ALU.max,
                                             ALU.mult).then_inc(made[b], 1)
                    f(2 * n + 1 if n else 2, 1)
                    dve.wait_ge(s["hid_high"], it * 4 + (FC * i + n + 1))
                    dve.tensor_tensor(hid_l[:, b, :], sgate[:, b, :], hid_h[:, b, :].bitcast(F32),
                                      ALU.subtract).then_inc(s["hid_ready"], 1)
                    if n and not last:
                        f(2 * n + 2, 0)
                        f(2 * n + 2, 1)

                step(0, 0)
                wait_made("norm", 2 * i + 1)
                link(dve.reciprocal(std[:, 1, :], std[:, 0, :]))
                link(dve.tensor_tensor(std[:, 1, :], std[:, 1, :], std[:, 1, :], ALU.mult))
                with dve.Fori(0, 3) as it:
                    for n in range(1, 5):
                        step(it, n)
                for n in range(13, FC):
                    step(0, n, n == FC - 1)
                fed[0] += 4 * FC - 4
                feed(2)
                for j in range(5):
                    if j < 4:
                        b = wait_full(f"mlp{i}y", j)
                        if j >= 2:
                            wait_made(f"mlp{i}y", j - 2)
                        dve.tensor_tensor(scaled[j % 2], bank2(b), pair_bcast(std[:, 1, :]),
                                          ALU.mult).then_inc(s["y_scaled"], 1)
                    if j:
                        b = FILL[f"mlp{i}y", j - 1][0]
                        dve.wait_ge(s["y_scaled"], 4 * i + j)
                        pair = x[:, 2 * j - 2:2 * j, :]
                        dve.tensor_tensor(pair, pair, scaled[(j - 1) % 2], ALU.add).then_inc(made[b], 1)
                        if i == 0:
                            wait_made(f"mlp{i}y", j - 1)
                            gained(2, j - 1)
                            if j > 1:
                                low_part(2, 2 * j - 4)
                                low_part(2, 2 * j - 3)

            mlp_square(0)
            low_part(2, KT - 2)
            low_part(2, KT - 1)
            feed(2)
            wait_made("norm", 2)
            dve.reciprocal(std_col[:, 1, :], std_col[:, 0, :]).then_inc(s["col_ready"], 1)
            for g in range(4):
                b = wait_full("pooly", g)
                for m in range(2):
                    ins = dve.scalar_tensor_tensor(x[:, 2 * g + m, :], bank2(b)[:, m, :], col("pool_scale", 2 * g + m),
                                                   x[:, 2 * g + m, :], ALU.mult, ALU.add)
                ins.then_inc(made[b], 1)
                wait_made("pooly", g)
                gained(3, g)
                if g == 0:
                    feed()
            feed(1)
            for k in range(KT):
                low_part(3, k)
            mlp_square(1)

            feed(2)
            b = wait_full("norm", 4)
            b = wait_full("norm", 5)
            dve.tensor_copy(std[:, 2, :], bank(b)[:, 0:TOK]).then_inc(s["dve_both"], 1)
            dve.wait_ge(s["dve_both"], 1)
            dve.scalar_tensor_tensor(std[:, 2, :], bank(FILL["norm", 4][0])[:, 0:TOK], EPS, std[:, 2, :], ALU.mult,
                                     ALU.add).then_inc(made[b], 1)
            dve.wait_ge(s["both_ready"], 1)
            link(dve.reciprocal(std[:, 2, :], std[:, 2, :]))
            norm_parts(5, lambda k: gain_both[:, k:k + 1], std[:, 2, :])
            wait_made("norm", 4)
            link(dve.reciprocal(std[:, 1, :], std[:, 0, :]))
            for k in range(KT):
                dve.scalar_tensor_tensor(x[:, k, :], x[:, k, :], col("norm_final", k), std[:, 1, :],
                                         ALU.mult, ALU.mult).then_inc(s["xn_ready"], 1)

            dve.wait_ge(s["par_in"], 48)
            for half in range(2):
                r = slice(64 * half, 64 * half + 64)
                link(dve.tensor_copy(dskip[r, :], dskip_all[r, :].rearrange("p (t h) -> p t h", h=2)[:, :, half]))
            feed()
            b = wait_full("small", 0)
            dve.tensor_scalar(dta[:, 0, :], bank(b)[0:SH, 0:TOK], ssd_par[:, 0:1], None, ALU.add).then_inc(s["dt_u"], 1)
            dve.wait_ge(s["dt_u"], 1)
            dve.scalar_tensor_tensor(dtt[:, 1, :], dta[:, 0, :], -1.0, dta[:, 0, :], ALU.mult,
                                     ALU.max).then_inc(s["dt_u"], 1)
            feed(5)
            e, den, z, z2 = dtt[:, 0, :], dtt[:, 1, :], dtt[:, 2, :], dtt[:, 3, :]
            poly = den

            def series(*odds):
                for k in odds:
                    link(dve.scalar_tensor_tensor(poly, poly, 1 / k, z2, ALU.add, ALU.mult))

            def softplus(part):
                if part == 0:
                    dve.wait_ge(s["dt_e"], 2)
                    link(dve.tensor_scalar(den, e, 2.0, None, ALU.add))
                    link(dve.reciprocal(den, den))
                    link(dve.tensor_tensor(z, e, den, ALU.mult))
                if part == 1:
                    link(dve.tensor_tensor(z2, z, z, ALU.mult))
                    link(dve.tensor_scalar(poly, z2, 1 / 15, None, ALU.mult))
                    series(13)
                if part == 2:
                    series(11, 9, 7)
                if part == 3:
                    series(5, 3)
                    link(dve.scalar_tensor_tensor(poly, poly, 1.0, z, ALU.add, ALU.mult))
                if part == 4:
                    link(dve.tensor_scalar(z, dta[:, 0, :], 0.0, None, ALU.max))
                    link(dve.scalar_tensor_tensor(dta[:, 0, :], poly, 2.0, z, ALU.mult, ALU.add))
                    link(dve.tensor_scalar(dtt[:, 1, :], dta[:, 0, :], ssd_par[:, 2:3], -1.0, ALU.mult, ALU.mult))
                if part == 5:
                    for ch in range(TB):
                        t = slice(ch * P, (ch + 1) * P)
                        ins = dve.tensor_tensor_scan(dta[:, 1, t], consts[0:SH, C_ONE:C_ONE + P], dtt[:, 1, t], 0.0,
                                                     ALU.mult, ALU.add)
                    ins.then_inc(s["dt_u"], 1)

            def conv(j):
                b = wait_full("xbc", j)
                dve.wait_ge(s["conv_first"], j + 1)
                for m in range(2):
                    t = 2 * j + m
                    acc, u = convb[:, t % 4, :], bank2(b)[:, m, :]
                    for tap in (2, 1, 0):
                        sh = CONV - 1 - tap
                        ins = dve.scalar_tensor_tensor(acc[:, sh:], u[:, 0:TOK - sh], col("conv_w_2", tap * (XBC // P) + t),
                                                       acc[:, sh:], ALU.mult, ALU.add)
                        if tap:
                            link(ins)
                    if m == 0:
                        link(ins)
                ins.then_inc(made[b], 1)

            for j in range(12):
                feed()
                conv(j)
                feed()
                if j == 0:
                    rope(("ropek", 0), kpe[64:64 + ROT, :], 64, 1)
                if j == 1:
                    norm(6)
                    norm(7)
                if 2 <= j < 8:
                    softplus(j - 2)
                if j == 9:
                    dve.wait_ge(s["dt_e"], 3)
                    dve.tensor_tensor(dtt[:, 3, 0:P], dtt[:, 2, 0:P], dta[:, 0, 0:P], ALU.mult).then_inc(s["dt_ready"], 1)

            feed(16)

            wait_made("dtT", 0)
            for g in range(NG):
                if g:
                    wait_full("y", g - 1, 0)
                    wait_full("y", g - 1, 1)
                for q in range(4):
                    dve.wait_ge(s["ea_ready"], 4 * g + q + 1)
                    b = wait_full("acum", g, q)
                    for hh in range(2):
                        for ch in range(TB):
                            h = HPG * g + 2 * q + hh
                            ins = dve.scalar_tensor_tensor(dec[:, 2 * q + hh, ch * P:(ch + 1) * P],
                                                           bank2(b)[:, hh, ch * P:(ch + 1) * P], dtn[:, ch, h:h + 1],
                                                           cap, ALU.subtract, ALU.min)
                    ins.then_inc(made[b], 1)
                wait_made("cb", g)
                for h in range(HPG):
                    dve.wait_ge(s["dec_ready"], 4 * g + h // 2 + 1)
                    for ch in range(TB):
                        d = dec[:, h, ch * P:(ch + 1) * P]
                        ins = dve.scalar_tensor_tensor(d, d, dtn[:, 2 + ch, HPG * g + h:HPG * g + h + 1],
                                                       cb_sb[:, ch * P:(ch + 1) * P], ALU.mult, ALU.mult)
                    ins.then_inc(s["m_ready"], 1)
                feed(2 if g < 3 else 0)
                for half in range(2):
                    b = wait_full("y", g, half)
                    for m in range(2):
                        t = 4 * g + 2 * half + m
                        ins = dve.scalar_tensor_tensor(rope_a[:, m, :], xbc[:, t, :], dskip[:, t:t + 1],
                                                       bank2(b)[:, m, :], ALU.mult, ALU.add)
                    ins.then_inc(made[b], 1)
                    wait_made("y", g, half)
                    zt = zs[:, 4 * g + 2 * half:4 * g + 2 * half + 2, :]
                    dve.tensor_tensor(zt, rope_a[:], zt, ALU.mult).then_inc(s["y_ready"], 1)
                    if half == 0:
                        dve.wait_ge(s["y_ready"], 2 * g + 1)
                norm(10 + g, 2 if g < 3 else 0)
            for j in range(8):
                rope(("rope2", j), qh[64:64 + ROT, 2 * j:2 * j + 2, :], 64)
            attention(LATENT, CAUSAL, float(QK) ** -0.5, True, one_tile, lambda i: feed(2 if i in (14, 15) else 0))
            for j in range(4):
                b = wait_full("souty", j)
                dve.tensor_tensor(merged[:, 2 * j:2 * j + 2, :], bank2(b), gates[:, 2 * j:2 * j + 2, :],
                                  ALU.mult).then_inc(made[b], 1)
            for j in range(4):
                feed(2 if j < 2 else 0)
                b = wait_full("mout", j)
                if j:
                    dve.wait_ge(s["y_ready"], 2 * NG + j)
                dve.tensor_tensor(rope_a[:], bank2(b), gates[:, KT + 2 * j:KT + 2 * j + 2, :],
                                  ALU.mult).then_inc(made[b], 1)
                wait_made("mout", j)
                dve.tensor_tensor(merged[:, 2 * j:2 * j + 2, :], merged[:, 2 * j:2 * j + 2, :], rope_a[:],
                                  ALU.add).then_inc(s["y_ready"], 1)
            norm(8)
            for j in range(4):
                add_to_x("wo2", j)
            norm(14)
            feed(12)
            attention(CROSSED, CROSS, float(TOK) ** -0.5, False, two_tiles)
            for j in range(4):
                add_to_x("xo", j)
                feed(2 if j < 3 else 0)
            norm(15, 2)

            def first_of(eq, n, iota, cand, m, onehot):
                link(dve.scalar_tensor_tensor(cand, eq, -float(n), iota, ALU.mult, ALU.add))
                link(dve.tensor_reduce(m, cand, AX_X, ALU.min))
                link(dve.tensor_tensor(onehot, cand, m.to_broadcast([P, TB, n]), ALU.is_equal))

            def spread(t, n):
                return t.to_broadcast([P, TB, n])

            b = wait_full("logits", 0)
            lg = rt("logits")
            bias = router_b[:].rearrange("p (o e) -> p o e", o=1).to_broadcast([P, TB, EG + NE])
            dve.tensor_tensor(lg, bank(b)[:, 0:TB * (EG + NE)].rearrange("p (b e) -> p b e", b=TB), bias,
                              ALU.add).then_inc(made[b], 1)
            wait_made("logits", 0)
            iota = consts[:, C_IOTA:C_IOTA + EPG].rearrange("p (o e) -> p o e", o=1).to_broadcast([P, TB, EPG])
            glog = lg[:, :, 0:EG]
            link(dve.tensor_reduce(rt("gmax"), glog, AX_X, ALU.max))
            dve.tensor_tensor(rt("gs"), glog, spread(rt("gmax"), EG), ALU.subtract).then_inc(s["rt_sub"], 1)
            link(dve.tensor_tensor(rt("geq"), glog, spread(rt("gmax"), EG), ALU.is_equal))
            first_of(rt("geq"), EG, iota[:, :, 0:EG], rt("gcand"), rt("gm"), rt("goh"))
            pick = rt("pick").rearrange("p b (g e) -> p b g e", g=EG)
            goh4 = rt("goh").rearrange("p b (g o) -> p b g o", o=1).to_broadcast([P, TB, EG, EPG])
            link(dve.tensor_tensor(pick, lg[:, :, EG:].rearrange("p b (g e) -> p b g e", g=EG), goh4, ALU.mult))
            link(dve.tensor_reduce(rt("ein"), pick.rearrange("p b g e -> p b e g"), AX_X, ALU.add))
            link(dve.tensor_reduce(rt("v1"), rt("ein"), AX_X, ALU.max))
            link(dve.tensor_tensor(rt("eq1"), rt("ein"), spread(rt("v1"), EPG), ALU.is_equal))
            first_of(rt("eq1"), EPG, iota, rt("cand"), rt("m"), rt("oh1"))
            link(dve.scalar_tensor_tensor(rt("rest"), rt("oh1"), NEG, rt("ein"), ALU.mult, ALU.add))
            link(dve.tensor_reduce(rt("v2"), rt("rest"), AX_X, ALU.max))
            dve.tensor_tensor(rt("ds"), rt("v2"), rt("v1"), ALU.subtract).then_inc(s["rt_sub"], 1)
            link(dve.tensor_tensor(rt("eq2"), rt("rest"), spread(rt("v2"), EPG), ALU.is_equal))
            first_of(rt("eq2"), EPG, iota, rt("cand"), rt("m"), rt("oh2"))
            dve.wait_ge(s["rt_exp"], 2)
            link(dve.tensor_reduce(rt("gsum"), rt("ge"), AX_X, ALU.add))
            link(dve.reciprocal(rt("gw"), rt("gsum")))
            link(dve.tensor_scalar(rt("dsum"), rt("de"), 1.0, None, ALU.add))
            link(dve.reciprocal(rt("w1"), rt("dsum")))
            link(dve.tensor_tensor(rt("w2"), rt("de"), rt("w1"), ALU.mult))
            link(dve.tensor_tensor(rt("oh1"), rt("oh1"), spread(rt("w1"), EPG), ALU.mult))
            link(dve.tensor_tensor(rt("oh2"), rt("oh2"), spread(rt("w2"), EPG), ALU.mult))
            link(dve.tensor_tensor(rt("oh1"), rt("oh1"), rt("oh2"), ALU.add))
            link(dve.tensor_tensor(rt("oh1"), rt("oh1"), spread(rt("gw"), EPG), ALU.mult))
            w_e = rt("oh1").rearrange("p b (o e) -> p b o e", o=1).to_broadcast([P, TB, EG, EPG])
            dve.tensor_tensor(rt("comb").rearrange("p b (g e) -> p b g e", g=EG), goh4, w_e,
                              ALU.mult).then_inc(s["comb_t"], 1)

            u, first = FILL["moe", "first"]

            def expert(it, n, last=False):
                def f(j, half):
                    low_half(first + j, half, it, 12)
                b = n % 2
                down, gate = (3 * n + 1, 3 * n + 2) if n else (2, 3)
                f(down, 0)
                f(down, 1)
                f(gate, 0)
                f(gate, 1)
                dve.wait_ge(made[b], it * 2 + (u[b] + n // 2 + 1))
                dve.wait_ge(s["units_done"], it * 24 + 2 * (first + (3 * n if n else 1)) + 2)
                dve.tensor_tensor(sgate[:, b, :], sgate[:, b, :], bank(2 + b), ALU.mult).then_inc(made[2 + b], 1)
                dve.wait_ge(made[2 + b], it * 2 + (u[2 + b] + n // 2 + 1))
                if n == 0:
                    dve.wait_ge(s["comb_in"], 64)
                cw = comb_b[:, bass.ds(it * 4 + n, 1), :].to_broadcast([P, 2, TOK])
                h2 = sgate[:, b, :].rearrange("p (k t) -> p k t", k=2)
                dve.tensor_tensor(h2, h2, cw, ALU.mult).then_inc(s["hid2"], 1)
                dve.wait_ge(s["hid_high"], it * 4 + (2 * FC + n + 1))
                dve.tensor_tensor(hid_l[:, b, :], sgate[:, b, :], hid_h[:, b, :].bitcast(F32),
                                  ALU.subtract).then_inc(s["hid_ready"], 1)
                if n and not last:
                    f(3 * n + 3, 0)
                    f(3 * n + 3, 1)

            expert(0, 0)
            with dve.Fori(0, 7) as it:
                for n in range(1, 5):
                    expert(it, n)
            for n in range(29, NE):
                expert(0, n, n == NE - 1)
            for j in range(4):
                add_to_x("moey", j)
            norm(16)
            for j in range(4):
                b = wait_full("outT", j)
                dve.tensor_copy(yout[:, j // 2, (j % 2) * 512:(j % 2 + 1) * 512], bank(b)).then_inc(made[b], 1)

        @block.gpsimd
        def _(pool):
            def wait_full(*key):
                b, _, n, _ = FILL[key]
                pool.wait_ge(full[b], n)

            def wait_made(*key):
                b, n, _, _ = FILL[key]
                pool.wait_ge(made[b], n)

            wait_made("dtT", 0)
            for g in range(NG):
                wait_made("xsn", g, 0)
                if g:
                    wait_full("state", g - 1)
                xg = xs_nat[:, g % 2, 0, :].rearrange("p (h c) -> p h c", c=64)
                wg = dtn[:, 4, HPG * g:HPG * (g + 1)].rearrange("p (h o) -> p h o", o=1).to_broadcast([P, HPG, 64])
                pool.tensor_tensor(xw.rearrange("p (h c) -> p h c", c=64), xg, wg, ALU.mult).then_inc(s["xw_ready"], 1)
                pool.wait_ge(s["ea_ready"], 4 * (g + 1))
                cg = xbc[:, ZT + NG + g, P:TOK].rearrange("p (o t) -> p o t", o=1).to_broadcast([P, HPG, P])
                pool.tensor_tensor(eac, eac, cg, ALU.mult).then_inc(s["cs_ready"], 1)
            pool.wait_ge(s["y_ready"], 2 * NG)
            pool.wait_ge(s["rope_done"], 9)
            kb = kpe[64:64 + ROT, :].rearrange("p (o t) -> p o t", o=1).to_broadcast([ROT, MH, TOK])
            pool.tensor_copy(kh[64:64 + ROT, :, :], kb).then_inc(s["kpe_copied"], 1)


_INS = ["x", "positions", "norm_mix", "norm_mlp", "attn_w_qkv", "attn_w_o", "pool_w", "pool_scale",
        "mlp_w_up", "mlp_w_down", "norm_final", "mem_2", "positions_2", "norm_mix_2", "w_in_2", "conv_w_2",
        "conv_b_2", "dt_bias_2", "a_log_2", "d_skip_2", "ssd_norm_2", "w_ssd_out_2", "q_a_norm_2", "w_q_b_2",
        "kv_a_norm_2", "w_kv_b_2", "w_mla_out_2", "w_o_2", "norm_xattn_2", "norm_mem_2", "w_xq_2", "w_xkv_2",
        "w_xo_2", "norm_moe_2", "w_router_group_2", "b_router_group_2", "w_router_expert_2",
        "b_router_expert_2", "w_exp_gate_2", "w_exp_up_2", "w_exp_down_2", "norm_final_2"]


def kernel(**inputs):
    import numpy as _np
    import concourse.bacc as _bacc
    from concourse import mybir as _mybir
    from concourse.bass_utils import run_bass_kernel_spmd as _run

    nc = _bacc.Bacc("TRN2", target_bir_lowering=False, num_devices=1)
    arrays = {f"in_{name}": _np.ascontiguousarray(inputs[name]) for name in _INS}
    arrays["in_consts"] = const_array()
    arrays["in_band"] = band_array()
    args = {name[3:]: nc.dram_tensor(name, v.shape, _mybir.dt.from_np(v.dtype), kind="ExternalInput").ap()
            for name, v in arrays.items()}
    out = nc.dram_tensor("out", (1, TOK, D), _mybir.dt.float32, kind="ExternalOutput").ap()
    build_two_blocks(nc, args, out)
    return _run(nc, [arrays], core_ids=[0]).results[0]["out"]
```

```python
import math
from contextlib import ExitStack

import numpy as np

import concourse.bass as bass
from concourse import mybir

F32 = mybir.dt.float32
F32R = mybir.dt.float32r
BF16 = mybir.dt.bfloat16
I32 = mybir.dt.int32
ALU = mybir.AluOpType
ACT = mybir.ActivationFunctionType
AX_X = mybir.AxisListType.X

P = 128
TOK = 256
TB = TOK // P
D = 1024
KT = D // P
EPS = 1e-6
NEG = -1e30

H1 = 8
ROT = 32
DFF = 4096
FC = DFF // TOK
WINDOWS = (2, 4, 8, 16)

DIN = 2048
ZT = DIN // P
NG, NST = 4, 128
SH = 32
HPG = SH // NG
CONV = 4
XBC = DIN + 2 * NG * NST
MH, QK, NOPE, VH = 16, 96, 64, 64
QLR, KLR = 384, 256
XH = 4
EG, EPG = 4, 8
NE = EG * EPG
DE = 256
O_Z, O_XBC, O_DT = 0, DIN, DIN + XBC
O_QA = O_DT + SH
O_KV = O_QA + QLR
O_KR = O_KV + KLR
O_GS = O_KR + ROT
O_GM = O_GS + D

SLOTS = 4
UNITS = 4
UNIT = 1024
SLOT = 2048

C_ID, C_ONE, C_MASK, C_CAP, C_ROT, C_INVF, C_IOTA, C_N = 0, 128, 256, 640, 768, 800, 801, 812

ROWS_A = [("norm_mix", 16), ("norm_mlp", 16), ("pool_scale", 8), ("norm_final", 8), ("norm_mix_2", 8),
          ("norm_xattn_2", 8), ("norm_mem_2", 8), ("norm_moe_2", 8), ("norm_final_2", 8),
          ("q_a_norm_2", 3), ("kv_a_norm_2", 2), ("ssd_norm_2", 16)]
ROWS_B = [("conv_w_2", CONV * XBC // P), ("conv_b_2", XBC // P)]
COL = {}
for _first, _rows in ((0, ROWS_A), (P, ROWS_B)):
    for _name, _n in _rows:
        COL[_name] = _first
        _first += _n
N_A = sum(n for _, n in ROWS_A)
N_B = sum(n for _, n in ROWS_B)

A_QK, A_V1, A_BAND = 0, 4096, 8192
A_POOLZ = 0
A_ZS, A_XS, A_BC, A_XN, A_GATE = 0, 4096, 8192, 10240, 12288
A_DT = A_GATE + 3072
A_QA, A_KV, A_E, A_XW, A_ST, A_BN = 16384, 17152, 17664, 19712, 20224, 20736
A_CONV = A_E
A_MERGE, A_QH, A_KH, A_VH = 2048, 4096, 8192, 18432
A_XQ, A_XK, A_XV, A_MEM, A_MIN = 0, 2048, 4096, 8192, 10240
A_COMB, A_RT = 0, 8192
A_P = A_QA
A_SG = A_QA
A_LATE = 4096
A_OUT, A_ROWS, A_POS = 12288, 14336, 14592
ARENA = 20864


def const_array():
    c = np.zeros((P, C_N), np.float32)
    c[:, C_ID:C_ID + P] = np.eye(P)
    c[:, C_ONE:C_ONE + P] = 1.0
    i = np.arange(P)
    tri = np.where(i[None, :] <= i[:, None], 0.0, NEG)
    c[:, C_MASK:C_MASK + P] = tri
    c[:, C_MASK + 2 * P:C_MASK + 3 * P] = tri
    c[:, C_CAP:C_CAP + P] = np.where(i[None, :] >= i[:, None], 0.0, NEG)
    h = ROT // 2
    for base in (0, 64):
        for j in range(h):
            c[base + j + h, C_ROT + j] = -1.0
            c[base + j, C_ROT + j + h] = 1.0
    f = np.float32
    f1 = f(500000.0) ** (-np.arange(0, ROT, 2, dtype=f) / f(ROT))
    f2 = f(10000.0) ** (-np.arange(h, dtype=f) / f(h))
    for base, fr in ((0, f1), (64, f2)):
        c[base:base + ROT, C_INVF] = np.tile(fr.astype(f), 2)
    c[:, C_IOTA:C_IOTA + EPG] = np.arange(EPG)
    return c


def band_array():
    b = np.zeros((TOK, len(WINDOWS), TOK), np.float32)
    for g, w in enumerate(WINDOWS):
        for t in range(TOK):
            lo = max(0, t - w + 1)
            b[lo:t + 1, g, t] = np.float32(1.0) / np.float32(t + 1 - lo)
            b[t, g, t] -= np.float32(1.0)
    return b


class Heads:

    def __init__(self, first, heads, pair, s_banks, t_banks, o_banks, t_lag, o_lag, bufs, t_bufs):
        self.first, self.heads, self.pair = first, heads, pair
        self.s_banks, self.t_banks, self.o_banks = s_banks, t_banks, o_banks
        self.t_lag, self.o_lag, self.bufs, self.t_bufs = t_lag, o_lag, bufs, t_bufs

    def lead(self, n):
        return self.first + n - n % self.pair


MOBA = Heads(0, H1, 1, (0, 1), (2, 3), (4, 5), 2, 3, 3, 4)
LATENT = Heads(H1, MH, 2, (0, 1), (2,), (3,), 1, 1, 2, 2)
CROSSED = Heads(H1 + MH, XH, 1, (0, 1), (2, 3), (4, 5), 2, 3, 3, 4)


class Counts:

    def __init__(self):
        self.loads, self.fills, self.split, self.ordinal = {}, {}, [], {}
        self.freed = []
        self.bank_fills = [0] * 8
        self.bank_signals = [0] * 8

    def load(self, key, freed_by=None, kind=None):
        n = len(self.freed)
        self.loads[key] = (n % SLOTS, n // SLOTS + 1, self.freed[n - SLOTS] if n >= SLOTS else None)
        if kind:
            self.ordinal[key] = len(self.split)
            self.split.append((key, kind))
            freed_by = ("lo", 2 * len(self.split))
        self.freed.append(freed_by)

    def fill(self, bank, *key, units=None):
        self.bank_fills[bank] += 1
        if units is None:
            self.bank_signals[bank] += 1
        self.fills[key] = (bank, self.bank_fills[bank], units or self.bank_signals[bank], units is not None)

    def done(self, key, halves=2):
        return 2 * self.ordinal[key] + halves

    def fill_each(self, stage, n, banks, units=None):
        for j in range(n):
            self.fill(banks[j % len(banks)], stage, j, units=units(j) if units else None)

    def attention(self, at):
        for i in range(at.heads + at.o_lag):
            n = i - at.t_lag
            if i < at.heads:
                self.fill(at.s_banks[i % len(at.s_banks)], "S", at.first + i)
            if 0 <= n < at.heads:
                self.fill(at.t_banks[n % len(at.t_banks)], "T", at.first + n)
            n = i - at.o_lag
            if n >= 0 and n % at.pair == 0:
                self.fill(at.o_banks[n // at.pair % len(at.o_banks)], "O", at.first + n)

    def mlp(self, i):
        self.fill(2, "norm", 2 * i + 1)
        stage = f"mlp{i}"
        for n in range(2 * FC):
            self.load((stage, n), kind="cols")
        self.fills[stage, "first"] = (tuple(self.bank_fills[0:2]), self.ordinal[stage, 0])
        for b in range(2):
            self.bank_fills[b] += FC // 2
        last = (stage, 2 * FC - 1)
        self.fill_each(stage + "y", 4, (4, 5, 6, 7), lambda j: self.done(last, 1 + j // 2))

    def moe(self):
        for n in range(3 * NE):
            self.load(("moe", n), kind="cols")
        self.fills["moe", "first"] = (tuple(self.bank_fills[0:4]), self.ordinal["moe", 0])
        for b in range(4):
            self.bank_fills[b] += NE // 2
        self.fill_each("moey", 4, (4, 5, 6, 7), lambda j: self.done(("moe", 3 * NE - 1), 1 + j // 2))


def plan():
    c = Counts()
    c.fill(0, "cols", 0)
    c.fill_each("xT", 4, (1, 2, 3, 4))
    c.fill(4, "norm", 0)
    c.fill(5, "column", 0)
    for j in range(12):
        c.load(("qkv", j), kind="cols" if j < 8 else "k")
    for j in range(8):
        c.fill(j % 2, "qk", j, units=c.done(("qkv", j)))
        c.fill(2 + j % 2, "rope1", j)
    c.fill_each("v1", 4, (0, 1), lambda j: c.done(("qkv", 8 + j)))
    c.attention(MOBA)
    for j in range(4):
        c.load(("wo1", j), kind="cols")
    c.fill_each("wo1", 4, (6, 7), lambda j: c.done(("wo1", j)))
    c.mlp(0)
    c.fill(6, "norm", 2)
    c.load(("pool", 0), kind="k")
    c.fill_each("poolz", 4, (0, 1, 4, 5), lambda g: c.done(("pool", 0), 1 + g // 2))
    c.fill_each("pooly", 4, (2, 3))
    c.mlp(1)
    c.fill(2, "norm", 4)
    c.fill(3, "norm", 5)
    for j in range(32):
        c.load(("win", j), ("small", 3) if j == 3 else None, kind=None if j == 3 else "cols")
    c.fill_each("small", 3, (0, 1), lambda j: c.done(("win", j)))
    c.fill(1, "small", 3)
    c.fill(4, "ropek", 0)
    c.fill_each("xbc", 12, (2, 3), lambda j: c.done(("win", 4 + j)))
    c.fill(0, "norm", 6)
    c.fill(1, "norm", 7)
    c.fill(0, "dtT", 0)
    c.fill_each("z", 8, (4, 5), lambda j: c.done(("win", 16 + j)))
    c.fill_each("gates", 8, (6, 7), lambda j: c.done(("win", 24 + j)))
    for g in range(NG):
        c.fill(0, "cb", g)
        c.fill(1, "bn", g)
        c.fill(2, "xsn", g, 0)
        c.fill(3, "xsn", g, 1)
        for q in range(4):
            c.fill(4 + q % 2, "acum", g, q)
        c.fill(1, "state", g)
        c.fill(2, "y", g, 0)
        c.fill(3, "y", g, 1)
        c.fill(1, "norm", 10 + g)
    for j in range(4):
        c.load(("qb", j), kind="cols")
    for j in range(8):
        c.fill(j % 2, "qh", j, units=c.done(("qb", j // 2), 1 + j % 2))
        c.fill(2 + j % 2, "rope2", j)
    for j in range(2):
        c.load(("kvb", j), kind="cols")
    for j in range(8):
        c.fill(j % 2, "kh", j, units=c.done(("kvb", j // 4), 1 + j % 4 // 2) if j % 2 else None)
    c.fill_each("vh", 4, (4, 5))
    for j in range(8):
        c.load(("sout", j), ("down", j + 1) if j < 7 else ("souty", 3))
    c.fill_each("souty", 4, (4, 5, 6, 7))
    c.attention(LATENT)
    for j in range(4):
        c.load(("mout", j), kind="cols")
    c.fill_each("mout", 4, (6, 7), lambda j: c.done(("mout", j)))
    for j in range(4):
        c.load(("wo2", j), kind="cols")
    c.fill_each("wo2", 4, (4, 5), lambda j: c.done(("wo2", j)))
    c.fill_each("memT", 4, (0, 1, 2, 3))
    c.fill(0, "norm", 8)
    c.fill(0, "norm", 14)
    for j in range(8):
        c.load(("xkv", j), kind="cols" if j < 4 else "k")
    c.fill_each("xk", 4, (3, 4), lambda j: c.done(("xkv", j)))
    c.fill_each("xv", 4, (5, 6), lambda j: c.done(("xkv", 4 + j)))
    for j in range(4):
        c.load(("xq", j), kind="cols")
    c.fill_each("xq", 4, (6, 7), lambda j: c.done(("xq", j)))
    c.attention(CROSSED)
    for j in range(4):
        c.load(("xo", j), kind="cols")
    c.fill_each("xo", 4, (6, 7), lambda j: c.done(("xo", j)))
    c.fill(4, "norm", 15)
    c.fill(3, "column", 1)
    c.fill(1, "logits", 0)
    c.fill(1, "combT", 0)
    c.moe()
    c.fill(0, "norm", 16)
    c.fill_each("outT", 4, (1, 2, 3, 0))
    return c


def build_two_blocks(nc, a, out):
    c = plan()
    W, FILL, SPLIT = c.loads, c.fills, c.split

    with ExitStack() as ctx:
        def sb(name, shape, dt=F32):
            return ctx.enter_context(nc.sbuf_tensor(name, shape, dt))

        def sem(name):
            return ctx.enter_context(nc.semaphore(name))

        ring = sb("ring", [P, SLOTS, SLOT])
        consts = sb("consts_sb", [P, C_N])
        wh = sb("weights_high", [P, UNITS, UNIT], F32R)
        wl = sb("weights_low", [P, UNITS, UNIT], F32R)
        cols = sb("cols", [P, 2 * P])
        dskip = sb("dskip", [P, ZT])
        dskip_all = sb("dskip_all", [P, SH])
        ssd_par = sb("ssd_par", [SH, 4])
        sin_t = sb("sin_t", [P, TOK])
        cos_t = sb("cos_t", [P, TOK])
        x = sb("xres", [P, KT, TOK])
        xh = sb("xnorm_high", [P, KT, TOK], F32R)
        xl = sb("xnorm_low", [P, KT, TOK], F32R)
        hid_h = sb("hidden_high", [P, 2, 512], F32R)
        hid_l = sb("hidden_low", [P, 2, 512], F32R)
        sq = sb("squares", [P, KT, TOK])
        cb_sb = sb("cb_sb", [P, TOK])
        std = sb("std", [P, 3, TOK])
        std_col = sb("std_col", [P, 2, TB])
        gain_both = sb("gain_both", [P, KT])
        smax = sb("smax", [P, 3, 2])
        ssum = sb("ssum", [P, 3, 2])
        srec = sb("srec", [P, 3, 2])
        rope_a = sb("rope_a", [P, 2, TOK])
        rope_b = sb("rope_b", [P, 2, TOK])
        kpe = sb("kpe", [P, TOK])
        dta = sb("dta", [SH, 2, TOK])
        acum_parts = sb("acum_parts", [2 * SH, TOK], F32R)
        unit_pair = sb("unit_pair", [2 * SH, SH], F32R)
        dtn = sb("dtn", [P, 5, SH])
        router_w = sb("router_w", [P, KT, EG + NE])
        router_b = sb("router_b", [P, EG + NE])
        zeros = sb("zeros", [P, 512], BF16)
        eps_col = sb("eps_col", [P, 2])
        arena = sb("arena", [P, ARENA])
        psum = ctx.enter_context(nc.psum_tensor("psum", [P, 8, 512], F32))
        comb_dram = nc.dram_tensor("comb_scratch", (NE, TOK), F32, kind="Internal").ap()

        ident, ones = consts[:, C_ID:C_ID + P], consts[:, C_ONE:C_ONE + P]
        mask3 = consts[:, C_MASK:C_MASK + 3 * P]
        cap = consts[:, C_CAP:C_CAP + P]

        def at(off, *shape):
            n = int(np.prod(shape))
            v = arena[:, off:off + n]
            if len(shape) == 2:
                return v.rearrange("p (a b) -> p a b", a=shape[0])
            if len(shape) == 3:
                return v.rearrange("p (a b c) -> p a b c", a=shape[0], b=shape[1])
            return v

        rows = at(A_ROWS, 2, P)
        pos_i = arena[:, A_POS:A_POS + TOK].bitcast(I32)
        dtt = arena[0:SH, A_DT:A_DT + 4 * TOK].rearrange("p (a t) -> p a t", a=4)
        merged = at(A_MERGE, KT, TOK)
        PROB, PROB_T = {}, {}
        for heads in (MOBA, LATENT, CROSSED):
            PROB[heads] = at(A_P, heads.bufs, 512)
            PROB_T[heads] = at(A_P + 512 * heads.bufs, heads.t_bufs, 512)
        mem = at(A_MEM, KT, TOK)
        qk = at(A_QK, 2 * H1, TOK)
        v1 = at(A_V1, TB, D)
        band = at(A_BAND, TB, 4, TOK)
        poolz = at(A_POOLZ, 4, TB, TOK)
        zs = at(A_ZS, ZT, TOK)
        xbc = at(A_XS, ZT + 2 * NG, TOK)
        xs_nat = at(A_XN, 2, TB, 512)
        gates = at(A_GATE, 2 * KT, TOK)
        qa = at(A_QA, 3, TOK)
        ckv = at(A_KV, 2, TOK)
        convb = at(A_CONV, 4, TOK)
        dec = at(A_E, HPG, TOK)
        eac = sq[:, 4:8, :].rearrange("p k t -> p (k t)").rearrange("p (h l) -> p h l", h=HPG)
        xw = at(A_XW, 512)
        st0 = at(A_ST, 512)
        bn_nat = at(A_BN, P)
        qh = at(A_QH, MH, TOK)
        kh = at(A_KH, MH, TOK)
        vh = at(A_VH, TB, D)
        xq, xk, xv = at(A_XQ, KT, TOK), at(A_XK, KT, TOK), at(A_XV, TB, D)
        comb_b = at(A_COMB, NE, TOK)
        sgate = at(A_SG, 2, 512)
        sq_late = at(A_LATE, KT, TOK)
        xin = at(A_OUT, TB, D)
        mem_in = at(A_MIN, TB, D)
        yout = at(A_OUT, TB, D)

        full = [sem(f"full{b}") for b in range(8)]
        made = [sem(f"made{b}") for b in range(8)]
        w_in = [sem(f"w_in{s}") for s in range(SLOTS)]
        s = {n: sem(n) for n in (
            "const_in", "rows_in", "x_in", "mem_in", "band_in", "pos_in", "par_in", "router_in", "zeros_set",
            "sq_ready", "xn_ready", "dve_step", "att_max", "exp_done", "p_ready", "rope_done", "hid_ready",
            "gate_silu", "down_done", "dt_ready", "conv_done", "xw_ready", "cs_ready", "ea_ready", "dec_ready",
            "m_ready", "y_ready", "kpe_copied", "comb_t", "comb_out", "comb_in", "hid2", "hi_ready",
            "lo_ready", "units_done", "hid_high", "o_high", "both_ready", "latent_high", "latent_low",
            "folded", "fold_step", "acum_high", "acum_low", "row_ready", "silu_ready", "comb_first",
            "conv_first", "col_ready", "y_scaled", "dve_both", "xt_ready", "xh_ready", "out_stored", "rt_sub",
            "rt_exp", "dt_u", "dt_e", "angle", "sines")}

        def bank(b):
            return psum[:, b, :]

        def bank2(b):
            return psum[:, b, :].rearrange("p (m t) -> p m t", m=2)

        def col(name, i=0):
            j = COL[name] + i
            return cols[:, j:j + 1]

        NORM = {
            0: (x, KT, "norm_mix", 0, None, "xT"),
            8: (mem, KT, "norm_mem_2", 0, None, "memT"),
            1: (x, KT, "norm_mlp", 0, None, "wo1"),
            2: (x, KT, "norm_mix", 8, None, "mlp0y"),
            3: (x, KT, "norm_mlp", 8, None, "pooly"),
            4: (x, KT, "norm_final", 0, x, "mlp1y"),
            5: (x, KT, "norm_mix_2", 0, None, None),
            6: (qa, 3, "q_a_norm_2", 0, qa, None),
            7: (ckv, 2, "kv_a_norm_2", 0, ckv, None),
            14: (x, KT, "norm_xattn_2", 0, None, "wo2"),
            15: (x, KT, "norm_moe_2", 0, None, "xo"),
            16: (x, KT, "norm_final_2", 0, x, "moey"),
        }
        SPLIT_NORMS = [0, 1, 2, 3, 5, "merged", 8, 14, 15]
        PLACE = {"merged": merged, 8: mem}
        READ_UNTIL = {"merged": ("mout", 3), 8: ("wo2", 3), 14: ("xkv", 7), 15: ("xo", 3)}
        for g in range(NG):
            NORM[10 + g] = (zs[:, 4 * g:4 * g + 4, :], 4, "ssd_norm_2", 4 * g, zs[:, 4 * g:4 * g + 4, :], None)
        NORM_ORDER = [0, 1, 2, 3, 5, 4, 6, 7, 10, 11, 12, 13, "merged", 8, 14, 15, 16]
        PIECES = {n: [(0, NORM[n][1])] if n in (6, 7) else [(k, k + 2) for k in range(0, NORM[n][1], 2)]
                  for n in NORM_ORDER if n != "merged"}
        SQ_NO, XN_NO, total, pieces = {}, {}, 0, 0
        for n in NORM_ORDER:
            XN_NO[n], SQ_NO[n] = total, pieces
            total += KT if n == "merged" else NORM[n][1]
            pieces += len(PIECES.get(n, ()))

        FOLDED = [1, 3, 8, 14]

        def norms_before(n):
            return [m for m in SPLIT_NORMS if m != "merged"].index(n)

        RT, off = {}, 0
        for name, n in (("logits", EG + NE), ("gmax", 1), ("gs", EG), ("geq", EG), ("gcand", EG), ("gm", 1),
                        ("goh", EG), ("pick", NE), ("ein", EPG), ("v1", 1), ("eq1", EPG), ("cand", EPG), ("m", 1),
                        ("oh1", EPG), ("rest", EPG), ("v2", 1), ("ds", 1), ("eq2", EPG), ("oh2", EPG), ("ge", EG),
                        ("de", 1), ("gsum", 1), ("gw", 1), ("dsum", 1), ("w1", 1), ("w2", 1), ("comb", NE)):
            RT[name] = at(A_RT + off, TB, n)
            off += TB * n
        combT = arena[0:NE, A_RT + off:A_RT + off + TOK]

        def rt(name):
            return RT[name]

        def half_views(n, half):
            key, kind = SPLIT[n]
            slot = W[key][0]
            stage, j = key
            if kind == "k":
                src = ring[:, slot, half * UNIT:(half + 1) * UNIT].rearrange("p (k c) -> p k c", k=4)
            else:
                down = (stage[:3] == "mlp" and (j == 2 * FC - 1 or (j and j % 2 == 0))) or \
                    (stage == "moe" and (j == 3 * NE - 1 or (j > 1 and j % 3 == 1)))
                kt, width = (2, D) if down or stage == "kvb" else (3, 4 * QK) if stage == "qb" else (KT, TOK)
                cut = (0, width // 2, width)
                if key == ("win", 0):
                    width, cut = SH + P, (0, SH, SH + P)
                src = ring[:, slot, 0:kt * width].rearrange("p (k c) -> p k c", k=kt)[:, :, cut[half]:cut[half + 1]]
            kt, width = src.shape[1], src.shape[2]
            unit = (2 * n + half) % UNITS
            high, low = (t[:, unit, 0:kt * width].rearrange("p (k c) -> p k c", k=kt) for t in (wh, wl))
            return W[key], src, high, low

        block = ctx.enter_context(nc.Block())

        @block.sync
        def _(sp):
            def rows_of(w, n):
                return w.rearrange("(k p) n -> p k n", p=P)[:, :, n]

            def wait_free(freed):
                if freed is None:
                    return
                if freed[0] == "lo":
                    sp.wait_ge(s["lo_ready"], freed[1])
                elif freed[0] == "down":
                    sp.wait_ge(s["down_done"], freed[1])
                else:
                    b, _, n, _ = FILL[freed]
                    sp.wait_ge(full[b], n)

            def load(stage, j, src, cols_n):
                slot, n, freed = W[stage, j]
                wait_free(freed)
                k = src.shape[1]
                dst = ring[:, slot, 0:k * cols_n].rearrange("p (k n) -> p k n", k=k)
                sp.dma_start(dst, src).then_inc(w_in[slot], 16)

            sp.dma_start(consts[:], a["consts"]).then_inc(s["const_in"], 16)
            x_rows = a["x"].rearrange("a (b p) d -> p (a b) d", p=P)
            sp.dma_start(xin, x_rows).then_inc(s["x_in"], 16)
            wq = a["attn_w_qkv"][0]
            load("qkv", 0, rows_of(wq, slice(0, TOK)), TOK)
            for tile, table in ((0, ROWS_A), (1, ROWS_B)):
                r = 0
                for name, n in table:
                    v = a[name]
                    flat = {1: "a -> a", 2: "a b -> (a b)", 3: "a b c -> (a b c)"}[len(v.shape)]
                    v = v if len(v.shape) == 1 else v.rearrange(flat)
                    sp.dma_start(rows[r:r + n, tile, :], v.rearrange("(r c) -> r c", c=P)).then_inc(s["rows_in"], 16)
                    r += n
            sp.dma_start(pos_i[0:64, :], a["positions"].to_broadcast([64, TOK])).then_inc(s["pos_in"], 16)
            sp.dma_start(pos_i[64:P, :], a["positions_2"].to_broadcast([64, TOK])).then_inc(s["pos_in"], 16)

            for j in range(1, 12):
                load("qkv", j, rows_of(wq, slice(j * TOK, (j + 1) * TOK)), TOK)
            sp.dma_start(band, a["band"].rearrange("(b p) g t -> p b g t", p=P)).then_inc(s["band_in"], 16)
            sp.dma_start(dskip_all[:], a["d_skip_2"].to_broadcast([P, SH])).then_inc(s["par_in"], 16)
            sp.dma_start(ssd_par[:, 0:1], a["dt_bias_2"].rearrange("a h -> h a")).then_inc(s["par_in"], 16)
            sp.dma_start(ssd_par[:, 1:2], a["a_log_2"].rearrange("a h -> h a")).then_inc(s["par_in"], 16)
            sp.dma_start(router_w[:, :, 0:EG], rows_of(a["w_router_group_2"][0], slice(0, EG))).then_inc(s["router_in"], 16)
            sp.dma_start(router_w[:, :, EG:], rows_of(a["w_router_expert_2"][0], slice(0, NE))).then_inc(s["router_in"], 16)
            sp.dma_start(router_b[:, 0:EG], a["b_router_group_2"].to_broadcast([P, EG])).then_inc(s["router_in"], 16)
            sp.dma_start(router_b[:, EG:], a["b_router_expert_2"].to_broadcast([P, NE])).then_inc(s["router_in"], 16)
            for j in range(4):
                load("wo1", j, rows_of(a["attn_w_o"][0], slice(j * TOK, (j + 1) * TOK)), TOK)

            def mlp_loads(i):
                up = a["mlp_w_up"][i].rearrange("(k p) (c n) -> c p k n", p=P, n=TOK)
                down = a["mlp_w_down"][i].rearrange("(c k p) n -> c p k n", p=P, k=2)
                stage = f"mlp{i}"

                def up_down(it, n, parts=(0, 1), first=False):
                    for half in parts:
                        n0 = (2 * n - 1 + half) if n else 0
                        slot, _, freed = W[stage, n0]
                        if first:
                            wait_free(freed)
                        else:
                            sp.wait_ge(s["lo_ready"], it * 16 + 2 * (c.ordinal[stage, n0] - 3))
                        dst = ring[:, slot, :].rearrange("p (k n) -> p k n", k=(KT, 2)[half])
                        sp.dma_start(dst, (up, down)[half][it * 4 + (n - half)]).then_inc(w_in[slot], 16)

                up_down(0, 0, (0,), True)
                for n in range(1, 5):
                    up_down(0, n, first=True)
                with sp.Fori(1, 3) as it:
                    for n in range(1, 5):
                        up_down(it, n)
                for n in range(13, FC):
                    up_down(0, n, first=True)
                slot, _, freed = W[stage, 2 * FC - 1]
                wait_free(freed)
                sp.dma_start(ring[:, slot, :].rearrange("p (k n) -> p k n", k=2), down[FC - 1]).then_inc(w_in[slot], 16)

            mlp_loads(0)
            pw = a["pool_w"][0].rearrange("g (k p) n -> p (g k) n", p=P)
            load("pool", 0, pw, TOK)
            mlp_loads(1)

            wi = a["w_in_2"][0]
            for j, (c0, n) in enumerate(((O_DT, SH + P), (O_QA + P, 2 * P), (O_KV, KLR), (O_KR, ROT))):
                load("win", j, rows_of(wi, slice(c0, c0 + n)), n)
            for j in range(12):
                load("win", 4 + j, rows_of(wi, slice(O_XBC + j * TOK, O_XBC + (j + 1) * TOK)), TOK)
            for j in range(8):
                load("win", 16 + j, rows_of(wi, slice(O_Z + j * TOK, O_Z + (j + 1) * TOK)), TOK)
            for j in range(8):
                load("win", 24 + j, rows_of(wi, slice(O_GS + j * TOK, O_GS + (j + 1) * TOK)), TOK)
            for j in range(4):
                load("qb", j, rows_of(a["w_q_b_2"][0], slice(j * 4 * QK, (j + 1) * 4 * QK)), 4 * QK)
            for j in range(2):
                load("kvb", j, rows_of(a["w_kv_b_2"][0], slice(j * D, (j + 1) * D)), D)
            so = a["w_ssd_out_2"][0].rearrange("(c k p) n -> c p k n", p=P, k=2)
            for j in range(8):
                load("sout", j, so[j], D)
            for stage, w, n in (("mout", "w_mla_out_2", 4), ("wo2", "w_o_2", 4), ("xkv", "w_xkv_2", 8),
                                ("xq", "w_xq_2", 4), ("xo", "w_xo_2", 4)):
                if stage == "xkv":
                    b, _, n_o, _ = FILL["O", H1 + MH - 2]
                    sp.wait_ge(full[b], n_o)
                    sp.dma_start(mem_in, a["mem_2"].rearrange("a (b p) d -> p (a b) d", p=P)).then_inc(s["mem_in"], 16)
                for j in range(n):
                    load(stage, j, rows_of(a[w][0], slice(j * TOK, (j + 1) * TOK)), TOK)
            wg = a["w_exp_gate_2"][0].rearrange("e (k p) n -> e p k n", p=P)
            wu = a["w_exp_up_2"][0].rearrange("e (k p) n -> e p k n", p=P)
            wd = a["w_exp_down_2"][0].rearrange("e (k p) n -> e p k n", p=P)

            def expert_loads(it, n, parts=(0, 1, 2), first=False):
                for part in parts:
                    i = 3 * n - 1 + part if n else part
                    slot, _, freed = W["moe", i]
                    if first:
                        wait_free(freed)
                    else:
                        sp.wait_ge(s["lo_ready"], it * 24 + 2 * (c.ordinal["moe", i] - 3))
                    dst = ring[:, slot, :].rearrange("p (k n) -> p k n", k=(KT, KT, 2)[part])
                    sp.dma_start(dst, (wg, wu, wd)[part][it * 4 + (n - part // 2)]).then_inc(w_in[slot], 16)

            expert_loads(0, 0, (0, 1), True)
            for n in range(1, 5):
                expert_loads(0, n, first=True)
            with sp.Fori(1, 7) as it:
                for n in range(1, 5):
                    expert_loads(it, n)
            for n in range(29, NE):
                expert_loads(0, n, first=True)
            slot, _, freed = W["moe", 3 * NE - 1]
            wait_free(freed)
            sp.dma_start(ring[:, slot, :].rearrange("p (k n) -> p k n", k=2), wd[NE - 1]).then_inc(w_in[slot], 16)
            o = out.rearrange("a (b p) d -> p (a b) d", p=P)
            for b in range(TB):
                for half in range(2):
                    bk, n, _, _ = FILL["outT", 2 * b + half]
                    sp.wait_ge(made[bk], n)
                sp.dma_start(o[:, b, :], yout[:, b, :]).then_inc(s["out_stored"], 16)
            sp.wait_ge(s["out_stored"], 16 * TB)

        @block.tensor
        def _(pe):
            def open_bank(*key):
                b, n, _, _ = FILL[key]
                if n > 1:
                    pe.wait_ge(made[b], n - 1)
                return b

            def wait_made(*key):
                b, n, _, _ = FILL[key]
                pe.wait_ge(made[b], n)

            def weights(stage, j, k, n):
                slot, no, _ = W[stage, j]
                pe.wait_ge(w_in[slot], 16 * no)
                return ring[:, slot, 0:k * n].rearrange("p (k n) -> p k n", k=k)

            def norm_sum(n, squares=sq):
                tiles = NORM[n][1]
                b = open_bank("norm", n)
                for piece, (k0, k1) in enumerate(PIECES[n]):
                    pe.wait_ge(s["sq_ready"], SQ_NO[n] + piece + 1)
                    for k in range(k0, k1):
                        mm = pe.matmul(bank(b)[:, 0:TOK], ones, squares[:, k, :], start=(k == 0), stop=(k == tiles - 1))
                mm.then_inc(full[b], 1)

            def folded_sum(n, squares):
                b = open_bank("norm", n)
                pe.wait_ge(s["folded"], FOLDED.index(n) + 1)
                pe.matmul(bank(b)[:, 0:TOK], ones, squares[:, 0, :], start=True, stop=True).then_inc(full[b], 1)

            def column_of_row(*key):
                pe.wait_ge(s["row_ready"], key[1] + 1)
                b = open_bank(*key)
                for tb in range(TB):
                    mm = pe.matmul(bank(b)[:, tb:tb + 1], std[0:1, 1, tb * P:(tb + 1) * P], ones[0:1, 0:1],
                                   start=True, stop=True)
                mm.then_inc(full[b], 1)

            def product(b, w, src, kt, parts):
                for m, (p0, c0, width) in enumerate(parts):
                    for k in range(kt):
                        mm = pe.matmul(bank2(b)[p0:p0 + width, m, :], w[:, k, c0:c0 + width], src[:, k, :],
                                       start=(k == 0), stop=(k == kt - 1))
                return mm

            BOTH = ((0, 0, P), (0, P, P))

            def project(stage, j, key, src, parts=BOTH, n=TOK):
                b = open_bank(*key)
                w = weights(stage, j, KT, n)
                product(b, w, src, KT, parts).then_inc(full[b], 1)

            def three(out, lh, ll, rh, rl, start, stop, **more):
                pe.matmul(out, lh, rh, start=start, stop=False, **more)
                pe.matmul(out, lh, rl, start=False, stop=False, **more)
                return pe.matmul(out, ll, rh, start=False, stop=stop, **more)

            def split_half(n, half, shift=0):
                _, _, high, low = half_views(n, half)
                pe.wait_ge(s["lo_ready"], shift + (2 * n + half + 1))
                return high, low

            def project_split(n, b, xn_from=None, shift=0):
                for m in range(2):
                    high, low = split_half(n, m, shift)
                    width = high.shape[2]
                    for k in range(KT):
                        if xn_from is not None and m == 0:
                            pe.wait_ge(s["xn_ready"], xn_from + k + 1)
                        mm = three(bank2(b)[0:width, m, :], high[:, k, :], low[:, k, :], xh[:, k, :], xl[:, k, :],
                                   k == 0, k == KT - 1)
                    mm.then_inc(s["units_done"], 1)

            def project_split_natural(n, b):
                for half in range(2):
                    high, low = split_half(n, half)
                    for tb in range(TB):
                        t = slice(tb * P, (tb + 1) * P)
                        for k in range(4):
                            kk = 4 * half + k
                            mm = three(bank2(b)[:, tb, :], xh[:, kk, t], xl[:, kk, t], high[:, k, :], low[:, k, :],
                                       kk == 0 and tb == 0, kk == KT - 1, skip_group_check=True)
                    mm.then_inc(s["units_done"], 1)

            def rotate(key, src, heads=2):
                b = open_bank(*key)
                p0 = src[1]
                pe.matmul(bank(b)[p0:p0 + ROT, 0:heads * TOK], consts[p0:p0 + ROT, C_ROT:C_ROT + ROT], src[0],
                          start=True, stop=True).then_inc(full[b], 1)

            def attention(at, scores, values, key_blocks, meanwhile=None):
                for i in range(at.heads + at.o_lag):
                    if i < at.heads:
                        b = open_bank("S", at.first + i)
                        scores(i, b).then_inc(full[b], 1)
                    n = i - at.t_lag
                    if 0 <= n < at.heads:
                        b = open_bank("T", at.first + n)
                        pe.wait_ge(s["p_ready"], 2 * (at.first + n + 1))
                        for src, dst in key_blocks:
                            mm = pe.transpose(bank(b)[:, dst:dst + P], PROB[at][:, n % at.bufs, src:src + P], ident)
                        mm.then_inc(full[b], 1)
                    if meanwhile is not None:
                        meanwhile(i)
                    n = i - at.o_lag
                    if n >= 0:
                        lead = at.lead(n)
                        b = open_bank("O", lead) if n % at.pair == 0 else FILL["O", lead][0]
                        wait_made("T", at.first + n)
                        mm = values(n, b, PROB_T[at][:, n % at.t_bufs, :])
                        if n % at.pair == at.pair - 1:
                            mm.then_inc(full[b], 1)

            CAUSAL = ((0, 0), (P, P), (2 * P, 2 * P))
            CROSS = ((0, 0), (P, 2 * P), (2 * P, P), (3 * P, 3 * P))

            def mlp(i):
                stage = f"mlp{i}"
                u, first = FILL[stage, "first"]
                for b in range(4):
                    open_bank(stage + "y", b)

                def up(it, n, xn_from=None):
                    b = n % 2
                    pe.wait_ge(made[b], it * 2 + (u[b] + n // 2))
                    project_split(first + (2 * n - 1 if n else 0), b, xn_from, shift=it * 16)

                def down(it, n, last=False):
                    pe.wait_ge(s["hid_ready"], it * 4 + (FC * i + n + 1))
                    add_down(first + (2 * n + 2 if not last else 2 * n + 1), n % 2, it * 16, last)

                clear_sums()
                up(0, 0, XN_NO[2 * i + 1])
                with pe.Fori(0, 3) as it:
                    for n in range(1, 5):
                        up(it, n)
                        down(it, n - 1)
                folded_sum(2 * i + 1, sq_late)
                for n in range(13, FC):
                    up(0, n)
                    down(0, n - 1)
                down(0, FC - 1, last=True)

            def clear_sums():
                pe.wait_ge(s["zeros_set"], 1)
                for b in range(4, 8):
                    pe.matmul(bank(b), zeros[:, 0:P], zeros[:, :], start=True, stop=False, skip_group_check=True)

            def add_down(n, buf, shift, last):
                hh = hid_h[:, buf, :].rearrange("p (k t) -> p k t", k=2)
                hl = hid_l[:, buf, :].rearrange("p (k t) -> p k t", k=2)
                for half in range(2):
                    high, low = split_half(n, half, shift)
                    for mm_ in range(4):
                        m = 4 * half + mm_
                        cc = slice(mm_ * P, (mm_ + 1) * P)
                        for k in range(2):
                            mm = three(bank2(4 + m // 2)[:, m % 2, :], high[:, k, cc], low[:, k, cc], hh[:, k, :],
                                       hl[:, k, :], False, last and k == 1, skip_group_check=True)
                    mm.then_inc(s["units_done"], 1)

            def add_sums(w, src, ms, last, first):
                for m in ms:
                    for k in range(2):
                        mm = pe.matmul(bank2(4 + m // 2)[:, m % 2, :], w[:, k, m * P:(m + 1) * P], src[:, k, :],
                                       start=(first and k == 0 and m % 2 == 0), stop=(last and k == 1),
                                       skip_group_check=True)
                        if last and m % 2 == 1 and k == 1:
                            mm.then_inc(full[4 + m // 2], 1)
                if not last and m == KT - 1:
                    mm.then_inc(s["down_done"], 1)

            pe.wait_ge(s["const_in"], 16)
            pe.wait_ge(s["x_in"], 16)
            for j in range(4):
                b = open_bank("xT", j)
                for m in range(2):
                    for tb in range(TB):
                        mm = pe.transpose(bank2(b)[:, m, tb * P:(tb + 1) * P],
                                          xin[:, tb, (2 * j + m) * P:(2 * j + m + 1) * P], ident)
                mm.then_inc(full[b], 1)
            pe.wait_ge(s["rows_in"], 16 * (len(ROWS_A) + len(ROWS_B)))
            b = open_bank("cols", 0)
            pe.transpose(bank(b)[:, 0:N_A], rows[0:N_A, 0, :], consts[0:N_A, C_ID:C_ID + N_A])
            pe.transpose(bank(b)[:, P:P + N_B], rows[0:N_B, 1, :], consts[0:N_B, C_ID:C_ID + N_B]).then_inc(full[b], 1)

            def rope1(j):
                wait_made("qk", j)
                rotate(("rope1", j), (qk[0:ROT, 2 * j:2 * j + 2, :], 0))

            for j in range(8):
                project_split(j, open_bank("qk", j), XN_NO[0] if j == 0 else None)
                if j == 0:
                    norm_sum(0, sq_late)
                if j == 4:
                    column_of_row("column", 0)
                if j:
                    rope1(j - 1)
            project_split_natural(8, open_bank("v1", 0))
            rope1(7)
            for j in range(1, 4):
                project_split_natural(8 + j, open_bank("v1", j))

            def scores1(h, b):
                pe.matmul(bank(b)[:, 0:P], qk[:, h, 0:P], qk[:, H1 + h, 0:P], start=True, stop=True)
                return pe.matmul(bank(b)[:, P:3 * P], qk[:, h, P:TOK], qk[:, H1 + h, :], start=True, stop=True)

            def values1(h, b, pt):
                pe.matmul(bank(b)[:, 0:TOK], v1[:, 0, h * P:(h + 1) * P], pt[:, 0:TOK], start=True, stop=False)
                return pe.matmul(bank(b)[:, P:TOK], v1[:, 1, h * P:(h + 1) * P], pt[:, TOK:TOK + P],
                                 start=False, stop=True)

            pe.wait_ge(s["rope_done"], 8)
            for j in range(2, 4):
                wait_made("v1", j)
            attention(MOBA, scores1, values1, CAUSAL)
            for h in range(H1 - 2, H1):
                wait_made("O", h)
            for j in range(4):
                project_split(c.ordinal["wo1", j], open_bank("wo1", j))
            mlp(0)

            for half in range(2):
                high, low = split_half(c.ordinal["pool", 0], half)
                for g in (2 * half, 2 * half + 1):
                    b = open_bank("poolz", g)
                    pe.wait_ge(s["xn_ready"], XN_NO[2] + 2 * g + 2)
                    for tb in range(TB):
                        t = slice(tb * P, (tb + 1) * P)
                        for k in range(2):
                            kk = 2 * (g % 2) + k
                            mm = three(bank2(b)[:, tb, :], xh[:, 2 * g + k, t], xl[:, 2 * g + k, t], high[:, kk, :],
                                       low[:, kk, :], k == 0, k == 1)
                mm.then_inc(s["units_done"], 1)
                if half == 0:
                    pe.wait_ge(s["sq_ready"], SQ_NO[2] + KT // 2)
                    b = open_bank("norm", 2)
                    for tb in range(TB):
                        for k in range(KT):
                            mm = pe.matmul(bank(b)[:, tb:tb + 1], sq_late[:, k, tb * P:(tb + 1) * P], ones[:, 0:1],
                                           start=(k == 0), stop=(k == KT - 1))
                    mm.then_inc(full[b], 1)
            pe.wait_ge(s["band_in"], 16)
            for g in range(4):
                wait_made("poolz", g)
                b = open_bank("pooly", g)
                for m in range(2):
                    pe.matmul(bank2(b)[:, m, :], poolz[:, g, 0, m * P:(m + 1) * P], band[:, 0, g, :],
                              start=True, stop=False)
                    mm = pe.matmul(bank2(b)[:, m, P:TOK], poolz[:, g, 1, m * P:(m + 1) * P], band[:, 1, g, P:TOK],
                                   start=False, stop=True)
                mm.then_inc(full[b], 1)
            mlp(1)

            banks = [open_bank("norm", n) for n in (4, 5)]
            for piece in range(KT // 2):
                for i, squares in enumerate((sq, sq_late)):
                    pe.wait_ge(s["sq_ready"], SQ_NO[5] + 2 * piece + i + 1)
                    for k in (2 * piece, 2 * piece + 1):
                        mm = pe.matmul(bank(banks[i])[:, 0:TOK], ones, squares[:, k, :], start=(k == 0), stop=(k == KT - 1))
                    if piece == KT // 2 - 1:
                        mm.then_inc(full[banks[i]], 1)

            for j in range(3):
                project_split(c.ordinal["win", j], open_bank("small", j), XN_NO[5] if j == 0 else None)
            project("win", 3, ("small", 3), sq, ((64, 0, ROT),), ROT)
            for j in range(12):
                project_split(c.ordinal["win", 4 + j], open_bank("xbc", j))
                if j == 0:
                    wait_made("small", 3)
                    rotate(("ropek", 0), (kpe[64:64 + ROT, :], 64), 1)
                if j == 1:
                    norm_sum(6)
                    norm_sum(7)
            b = open_bank("dtT", 0)
            pe.wait_ge(s["dt_ready"], 1)
            for i, src in enumerate((dta[:, 1, 0:P], dta[:, 1, P:TOK], dta[:, 0, 0:P], dta[:, 0, P:TOK], dtt[:, 3, 0:P])):
                mm = pe.transpose(bank(b)[:, SH * i:SH * (i + 1)], src, consts[0:SH, C_ID:C_ID + SH])
            mm.then_inc(full[b], 1)
            for j in range(8):
                project_split(c.ordinal["win", 16 + j], open_bank("z", j))

            def gate_chunk(j):
                project_split(c.ordinal["win", 24 + j], open_bank("gates", j))

            pe.wait_ge(s["conv_done"], 12)
            pe.wait_ge(s["acum_low"], 1)
            for g in range(NG):
                def decays(q):
                    b = open_bank("acum", g, q)
                    for hh in range(2):
                        h = HPG * g + 2 * q + hh
                        mm = pe.matmul(bank2(b)[:, hh, :], unit_pair[:, h:h + 1].to_broadcast([2 * SH, P]),
                                       acum_parts[:], start=True, stop=True)
                    mm.then_inc(full[b], 1)

                decays(0)
                decays(1)
                b = open_bank("cb", g)
                for ch in range(TB):
                    mm = pe.matmul(bank(b)[:, ch * P:(ch + 1) * P], xbc[:, ZT + g, ch * P:(ch + 1) * P],
                                   xbc[:, ZT + NG + g, ch * P:(ch + 1) * P], start=True, stop=True)
                mm.then_inc(full[b], 1)
                b = open_bank("bn", g)
                pe.transpose(bank(b)[:, 0:P], xbc[:, ZT + g, 0:P], ident).then_inc(full[b], 1)
                for ch in range(TB):
                    b = open_bank("xsn", g, ch)
                    for i in range(4):
                        mm = pe.transpose(bank(b)[:, i * P:(i + 1) * P], xbc[:, 4 * g + i, ch * P:(ch + 1) * P], ident)
                    mm.then_inc(full[b], 1)
                decays(2)
                decays(3)
                wait_made("bn", g)
                pe.wait_ge(s["xw_ready"], g + 1)
                b = open_bank("state", g)
                pe.matmul(bank(b), bn_nat, xw, start=True, stop=True).then_inc(full[b], 1)
                gate_chunk(2 * g)
                wait_made("state", g)
                pe.wait_ge(s["cs_ready"], g + 1)
                wait_made("xsn", g, 0)
                wait_made("xsn", g, 1)
                for half in range(2):
                    b = open_bank("y", g, half)
                    for hp in range(4):
                        h = 4 * half + hp
                        pe.wait_ge(s["m_ready"], HPG * g + h + 1)
                        o = bank2(b)[64 * (h % 2):64 * (h % 2) + 64, (h // 2) % 2, :]
                        hc = slice(h * 64, (h + 1) * 64)
                        pe.matmul(o[:, 0:P], xs_nat[:, g % 2, 0, hc], dec[:, h, 0:P], start=True, stop=True)
                        pe.matmul(o[:, P:TOK], xs_nat[:, g % 2, 1, hc], dec[:, h, P:TOK], start=True, stop=False)
                        mm = pe.matmul(o[:, P:TOK], st0[:, h * 64:(h + 1) * 64], eac[:, h, :], start=False, stop=True)
                    mm.then_inc(full[b], 1)
                gate_chunk(2 * g + 1)
                norm_sum(10 + g)

            def ssd_out(i):
                if i < 16:
                    if i == 0:
                        for b in range(4):
                            open_bank("souty", b)
                    j = i // 2
                    pe.wait_ge(s["xn_ready"], XN_NO[10 + j // 2] + 4)
                    w = weights("sout", j, 2, D)
                    add_sums(w, zs[:, 2 * j:2 * j + 2, :], range(4 * (i % 2), 4 * (i % 2) + 4), last=(j == 7),
                             first=(j == 0))

            def rope2(j):
                wait_made("qh", j)
                rotate(("rope2", j), (qh[64:64 + ROT, 2 * j:2 * j + 2, :], 64))

            pe.wait_ge(s["latent_low"], 1)
            for j in range(8):
                b = open_bank("qh", j)
                high, low = split_half(c.ordinal["qb", j // 2], j % 2)
                for m in range(2):
                    cc = slice(m * QK, (m + 1) * QK)
                    for k in range(3):
                        mm = three(bank2(b)[0:QK, m, :], high[:, k, cc], low[:, k, cc], xh[:, k, :], xl[:, k, :],
                                   k == 0, k == 2)
                mm.then_inc(s["units_done"], 1)
                if j:
                    rope2(j - 1)
            pe.wait_ge(s["latent_low"], 2)
            for part in range(4):
                high, low = split_half(c.ordinal["kvb", part // 2], part % 2)
                vhigh, vlow = (t.rearrange("p k (h c) -> p k h c", c=P)[:, :, :, NOPE:] for t in (high, low))
                for tb in range(TB):
                    t = slice(tb * P, (tb + 1) * P)
                    key = ("vh", part // 2 * 2 + tb)
                    b = FILL[key][0] if part % 2 else open_bank(*key)
                    for k in range(2):
                        mm = three(bank2(b)[:, part % 2, :], xh[:, 3 + k, t], xl[:, 3 + k, t], vhigh[:, k], vlow[:, k],
                                   k == 0, k == 1)
                    if part % 2:
                        mm.then_inc(full[b], 1)
                for j in (2 * part, 2 * part + 1):
                    b = open_bank("kh", j)
                    for m in range(2):
                        cc = slice((2 * (j % 2) + m) * P, (2 * (j % 2) + m) * P + NOPE)
                        for k in range(2):
                            mm = three(bank2(b)[0:NOPE, m, :], high[:, k, cc], low[:, k, cc], xh[:, 3 + k, :],
                                       xl[:, 3 + k, :], k == 0, k == 1)
                    mm.then_inc(s["units_done"] if j % 2 else full[b], 1)
                if part == 0:
                    rope2(7)

            def scores2(h, b):
                pe.matmul(bank(b)[:, 0:P], qh[0:QK, h, 0:P], kh[0:QK, h, 0:P], start=True, stop=True)
                return pe.matmul(bank(b)[:, P:3 * P], qh[0:QK, h, P:TOK], kh[0:QK, h, :], start=True, stop=True)

            def values2(h, b, pt):
                o = bank(b)[64 * (h % 2):64 * (h % 2) + 64, :]
                pe.matmul(o[:, 0:TOK], vh[:, 0, h * VH:(h + 1) * VH], pt[:, 0:TOK], start=True, stop=False,
                          skip_group_check=True)
                return pe.matmul(o[:, P:TOK], vh[:, 1, h * VH:(h + 1) * VH], pt[:, TOK:TOK + P],
                                 start=False, stop=True, skip_group_check=True)

            pe.wait_ge(s["rope_done"], 17)
            pe.wait_ge(s["kpe_copied"], 1)
            for key in (("kh", 6), ("kh", 7), ("vh", 2), ("vh", 3)):
                wait_made(*key)
            attention(LATENT, scores2, values2, CAUSAL, ssd_out)
            wait_made("O", H1 + MH - 2)
            for j in range(4):
                project_split(c.ordinal["mout", j], open_bank("mout", j))
            pe.wait_ge(s["mem_in"], 16)
            for j in range(4):
                b = open_bank("memT", j)
                for m in range(2):
                    for tb in range(TB):
                        mm = pe.transpose(bank2(b)[:, m, tb * P:(tb + 1) * P],
                                          mem_in[:, tb, (2 * j + m) * P:(2 * j + m + 1) * P], ident)
                mm.then_inc(full[b], 1)
            for j in range(4):
                project_split(c.ordinal["wo2", j], open_bank("wo2", j), XN_NO["merged"] if j == 0 else None)
                if j == 1:
                    folded_sum(8, sq)

            for j in range(4):
                project_split(c.ordinal["xkv", j], open_bank("xk", j), XN_NO[8] if j == 0 else None)
                if j == 1:
                    folded_sum(14, sq)
            for j in range(4):
                project_split_natural(c.ordinal["xkv", 4 + j], open_bank("xv", j))

            def queries(j):
                project_split(c.ordinal["xq", j], open_bank("xq", j), XN_NO[14] if j == 0 else None)

            queries(0)
            queries(1)

            def scores3(h, b):
                wait_made("xq", h)
                for qb in range(2):
                    for kk in range(2):
                        mm = pe.matmul(bank2(b)[:, qb, :], xq[:, 2 * h + kk, qb * P:(qb + 1) * P],
                                       xk[:, 2 * h + kk, :], start=(kk == 0), stop=(kk == 1))
                return mm

            def values3(h, b, pt):
                for m in range(2):
                    for kb in range(2):
                        mm = pe.matmul(bank2(b)[:, m, :], xv[:, kb, (2 * h + m) * P:(2 * h + m + 1) * P],
                                       pt[:, kb * TOK:(kb + 1) * TOK], start=(kb == 0), stop=(kb == 1))
                return mm

            for stage in ("xk", "xv"):
                for j in (2, 3):
                    wait_made(stage, j)
            attention(CROSSED, scores3, values3, CROSS, lambda i: queries(i + 2) if i < 2 else None)
            for h in (XH - 2, XH - 1):
                wait_made("O", H1 + MH + h)
            for j in range(4):
                project_split(c.ordinal["xo", j], open_bank("xo", j))

            u, first = FILL["moe", "first"]

            def gate_up(it, n, parts=(0, 1), xn_from=None):
                for part in parts:
                    b = 2 * part + n % 2
                    pe.wait_ge(made[b], it * 2 + (u[b] + n // 2))
                    project_split(first + (3 * n - 1 + part if n else part), b, xn_from, shift=it * 24)

            gate_up(0, 0, (0,), XN_NO[15])
            norm_sum(15, sq_late)

            pe.wait_ge(s["router_in"], 64)
            b = open_bank("logits", 0)
            for tb in range(TB):
                for k in range(KT):
                    mm = pe.matmul(bank(b)[:, tb * (EG + NE):(tb + 1) * (EG + NE)], sq[:, k, tb * P:(tb + 1) * P],
                                   router_w[:, k, :], start=(k == 0), stop=(k == KT - 1))
            mm.then_inc(full[b], 1)

            column_of_row("column", 1)

            def expert_down(it, n, last=False):
                pe.wait_ge(s["hid_ready"], it * 4 + (2 * FC + n + 1))
                add_down(first + (3 * n + 4 if not last else 3 * n + 2), n % 2, it * 24, last)

            gate_up(0, 0, (1,))
            for b in range(4):
                open_bank("moey", b)
            clear_sums()
            b = open_bank("combT", 0)
            pe.wait_ge(s["comb_t"], 1)
            for tb in range(TB):
                mm = pe.transpose(bank(b)[0:NE, tb * P:(tb + 1) * P], rt("comb")[:, tb, :], ident)
            mm.then_inc(full[b], 1)
            with pe.Fori(0, 7) as it:
                for n in range(1, 5):
                    gate_up(it, n)
                    expert_down(it, n - 1)
            for n in range(29, NE):
                gate_up(0, n)
                expert_down(0, n - 1)
            expert_down(0, NE - 1, last=True)

            norm_sum(16)
            for j in range(4):
                b = open_bank("outT", j)
                for i in range(4):
                    k = 4 * (j % 2) + i
                    pe.wait_ge(s["xn_ready"], XN_NO[16] + k + 1)
                    mm = pe.transpose(bank(b)[:, i * P:(i + 1) * P], x[:, k, (j // 2) * P:(j // 2 + 1) * P], ident)
                mm.then_inc(full[b], 1)

        @block.scalar
        def _(act):
            def wait_full(*key):
                b, _, n, by_units = FILL[key]
                act.wait_ge(s["units_done"] if by_units else full[b], n)
                return b

            def wait_made(*key):
                b, n, _, _ = FILL[key]
                act.wait_ge(made[b], n)

            fed = [0]

            def high_half(n, half, it=0, body=0):
                (slot, no, _), src, high, _ = half_views(n, half)
                if half == 0:
                    act.wait_ge(w_in[slot], it * (16 * body // SLOTS) + 16 * no)
                u = 2 * n + half
                if u >= UNITS:
                    act.wait_ge(s["units_done"], it * (2 * body) + (u - UNITS + 1))
                act.activation(high, src, ACT.Copy).then_inc(s["hi_ready"], 1)

            def feed(halves=1):
                for _ in range(halves):
                    high_half(fed[0] // 2, fed[0] % 2)
                    fed[0] += 1

            def copy_out(dst, *key, view=None):
                b = wait_full(*key)
                act.activation(dst, view(b) if view else bank2(b), ACT.Copy).then_inc(made[b], 1)

            def norm_parts(n):
                if n in READ_UNTIL:
                    act.wait_ge(s["units_done"], c.done(READ_UNTIL[n]))
                place = PLACE.get(n, sq)
                for k in range(KT):
                    if n == "merged":
                        act.wait_ge(s["y_ready"], 2 * NG + k // 2 + 1)
                    else:
                        act.wait_ge(s["xt_ready"], KT * norms_before(n) + k + 1)
                    act.activation(xh[:, k, :], place[:, k, :], ACT.Copy).then_inc(s["xh_ready"], 1)

            def column_scaled(dst, *key):
                b = wait_full(*key)
                for tb in range(TB):
                    ins = act.activation(dst[:, tb, :], bank2(b)[:, tb, :], ACT.Copy, scale=std_col[:, 1, tb:tb + 1])
                ins.then_inc(made[b], 1)

            def squares_late(n, halves):
                feed(halves)
                norm_parts(n)
                for j in range(KT // 2):
                    act.activation(sq_late[:, 2 * j:2 * j + 2, :], x[:, 2 * j:2 * j + 2, :],
                                   ACT.Square).then_inc(s["sq_ready"], 1)

            def squares(n):
                src, _, _, _, _, after = NORM[n]
                for j, (k0, k1) in enumerate(PIECES[n]):
                    if after is not None:
                        wait_made(after, j)
                    elif n == 6:
                        wait_made("small", 0)
                        wait_made("small", 1)
                    elif n == 7:
                        wait_made("small", 2)
                    else:
                        act.wait_ge(s["y_ready"], 2 * (n - 10) + j + 1)
                    act.activation(sq[:, k0:k1, :], src[:, k0:k1, :], ACT.Square).then_inc(s["sq_ready"], 1)

            def root(n):
                b = wait_full("norm", n)
                if XN_NO[n]:
                    act.wait_ge(s["xn_ready"], XN_NO[n])
                act.activation(std[:, 0, :], bank(b)[:, 0:TOK], ACT.Sqrt, bias=eps_col[:, 0:1],
                               scale=1.0 / (NORM[n][1] * P)).then_inc(made[b], 1)

            def norm(n, halves=0, tail=0, between=None):
                squares(n)
                feed(halves)
                if between is not None:
                    between()
                root(n)
                if n in SPLIT_NORMS:
                    norm_parts(n)
                feed(tail)

            def attention(at, segments, high, meanwhile=None):
                prob, probT = PROB[at], PROB_T[at]
                for i in range(at.heads + at.o_lag):
                    if i < at.heads:
                        n = at.first + i
                        act.wait_ge(s["att_max"], 2 * (n + 1))
                        for e, (c0, c1) in enumerate(segments):
                            act.activation(prob[:, i % at.bufs, c0:c1], prob[:, i % at.bufs, c0:c1], ACT.Exp,
                                           bias=smax[:, n % 3, e:e + 1],
                                           accum_out=ssum[:, n % 3, e:e + 1]).then_inc(s["exp_done"], 1)
                    n = i - at.t_lag
                    if 0 <= n < at.heads:
                        if n >= at.t_bufs:
                            wait_full("O", at.lead(n - at.t_bufs))
                        w = segments[-1][1]
                        copy_out(probT[:, n % at.t_bufs, 0:w], "T", at.first + n, view=lambda b: bank(b)[:, 0:w])
                    if meanwhile is not None:
                        meanwhile(i)
                    n = i - at.o_lag
                    if n >= 0 and n % at.pair == at.pair - 1:
                        b = wait_full("O", at.lead(n))
                        dst, src = high(n // at.pair, b)
                        act.activation(dst, src, ACT.Copy).then_inc(s["o_high"], 1)

            CAUSAL = ((0, P), (P, 3 * P))
            CROSS = ((0, TOK), (TOK, 2 * TOK))

            act.wait_ge(s["zeros_set"], 1)
            squares_late(0, 2)
            feed(4)
            root(0)
            act.wait_ge(s["angle"], 1)
            act.activation(sin_t[:], rope_b[:, 0, :], ACT.Sin).then_inc(s["sines"], 1)
            act.activation(cos_t[:], rope_b[:, 1, :], ACT.Sin).then_inc(s["sines"], 1)
            feed(14)
            copy_out(std_col[:, 1, :], "column", 0, view=lambda b: bank(b)[:, 0:TB])
            wait_made("column", 0)
            for j in range(4):
                feed()
                column_scaled(v1[:, :, j * TOK:(j + 1) * TOK], "v1", j)
                feed()

            def one_tile(t, b):
                return xh[:, t, :], bank(b)[:, 0:TOK]

            def two_tiles(t, b):
                return xh[:, 2 * t:2 * t + 2, :], bank2(b)

            attention(MOBA, CAUSAL, one_tile)
            feed(6)
            squares_late(1, 2)

            def mlp_hidden(i):
                u, first = FILL[f"mlp{i}", "first"]

                def step(it, n, last=False):
                    def f(j, half):
                        high_half(first + j, half, it, 8)
                    b = n % 2
                    f(2 * n + 1 if n else 2, 0)
                    act.wait_ge(s["units_done"], it * 16 + 2 * (first + (2 * n - 1 if n else 0)) + 2)
                    act.activation(sgate[:, b, :], bank(b), ACT.Relu).then_inc(s["gate_silu"], 1)
                    f(2 * n + 1 if n else 2, 1)
                    act.wait_ge(made[b], it * 2 + (u[b] + n // 2 + 1))
                    act.activation(hid_h[:, b, :], sgate[:, b, :], ACT.Copy).then_inc(s["hid_high"], 1)
                    if n and not last:
                        f(2 * n + 2, 0)
                        f(2 * n + 2, 1)

                step(0, 0)
                with act.Fori(0, 3) as it:
                    for n in range(1, 5):
                        step(it, n)
                root(2 * i + 1)
                for n in range(13, FC):
                    step(0, n, n == FC - 1)
                fed[0] += 4 * FC - 4

            mlp_hidden(0)
            squares_late(2, 2)
            feed(2)
            b = wait_full("norm", 2)
            act.activation(std_col[:, 0, :], bank(b)[:, 0:TB], ACT.Sqrt, bias=eps_col[:, 0:1],
                           scale=1.0 / D).then_inc(made[b], 1)
            act.wait_ge(s["col_ready"], 1)
            for g in range(4):
                column_scaled(poolz[:, g, :, :], "poolz", g)
                if g == 2:
                    feed()
            squares_late(3, 1)
            mlp_hidden(1)
            feed(2)
            for j in range(KT // 2):
                wait_made("mlp1y", j)
                act.activation(sq[:, 2 * j:2 * j + 2, :], x[:, 2 * j:2 * j + 2, :], ACT.Square).then_inc(s["sq_ready"], 1)
                for k in (2 * j, 2 * j + 1):
                    ins = act.activation(sq_late[:, k, :], x[:, k, :], ACT.Square, scale=col("norm_final", k))
                ins.then_inc(s["sq_ready"], 1)
            feed(2)
            wait_made("norm", 5)
            act.activation(std[:, 2, :], std[:, 2, :], ACT.Sqrt, bias=eps_col[:, 1:2],
                           scale=1.0 / D).then_inc(s["both_ready"], 1)
            norm_parts(5)
            b = wait_full("norm", 4)
            act.wait_ge(s["xn_ready"], XN_NO[5])
            act.activation(std[:, 0, :], bank(b)[:, 0:TOK], ACT.Sqrt, bias=eps_col[:, 0:1],
                           scale=1.0 / D).then_inc(made[b], 1)

            feed()
            act.wait_ge(s["dt_u"], 1)
            copy_out(qa[:, 0, :], "small", 0, view=lambda b: bank2(b)[:, 1, :])
            feed(2)
            copy_out(qa[:, 1:3, :], "small", 1)
            feed(2)
            copy_out(ckv, "small", 2)
            feed()
            copy_out(kpe[64:64 + ROT, :], "small", 3, view=lambda b: bank(b)[64:64 + ROT, 0:TOK])
            act.activation(ssd_par[:, 2:3], ssd_par[:, 1:2], ACT.Exp).then_inc(s["dt_e"], 1)
            act.wait_ge(s["dt_u"], 2)
            act.activation(dtt[:, 0, :], dtt[:, 1, :], ACT.Exp, scale=-1.0).then_inc(s["dt_e"], 1)
            def conv_silu(j):
                wait_made("xbc", j)
                act.activation(xbc[:, 2 * j:2 * j + 2, :], convb[:, 2 * (j % 2):2 * (j % 2) + 2, :],
                               ACT.Silu).then_inc(s["conv_done"], 1)

            def conv_first(j):
                b = wait_full("xbc", j)
                if j >= 2:
                    act.wait_ge(s["conv_done"], j - 1)
                for t in (2 * j, 2 * j + 1):
                    ins = act.activation(convb[:, t % 4, :], bank2(b)[:, t % 2, :], ACT.Identity,
                                         bias=col("conv_b_2", t), scale=col("conv_w_2", 3 * (XBC // P) + t))
                ins.then_inc(s["conv_first"], 1)

            for j in range(12):
                feed()
                conv_first(j)
                if j:
                    conv_silu(j - 1)
                feed()
                if j == 1:
                    norm(6)
                    norm(7)
                if j == 8:
                    act.wait_ge(s["dt_u"], 3)
                    act.activation(dtt[:, 2, 0:P], dta[:, 1, 0:P], ACT.Exp, bias=dta[:, 1, P - 1:P],
                                   scale=-1.0).then_inc(s["dt_e"], 1)
                    for i in range(2):
                        act.activation(unit_pair[SH * i:SH * (i + 1), :],
                                       consts[SH * i:SH * (i + 1), C_ID + SH * i:C_ID + SH * (i + 1)], ACT.Copy)
                    act.activation(acum_parts[0:SH, :], dta[:, 1, :], ACT.Copy).then_inc(s["acum_high"], 1)
            conv_silu(11)
            copy_out(dtn[:], "dtT", 0, view=lambda b: bank(b)[:, 0:5 * SH].rearrange("p (a h) -> p a h", a=5))
            for j in range(8):
                feed()
                b = wait_full("z", j)
                act.activation(zs[:, 2 * j:2 * j + 2, :], bank2(b), ACT.Silu).then_inc(made[b], 1)
                feed()

            def gate(j):
                b = wait_full("gates", j)
                act.activation(gates[:, 2 * j:2 * j + 2, :], bank2(b), ACT.Sigmoid).then_inc(made[b], 1)
                feed(2)

            for g in range(NG):
                if g:
                    act.wait_ge(s["m_ready"], HPG * g)
                    wait_full("y", g - 1, 0)
                    wait_full("y", g - 1, 1)

                def decay_since_start(q):
                    b = wait_full("acum", g, q)
                    act.activation(eac[:, 2 * q:2 * q + 2, :], bank2(b)[:, :, P:TOK],
                                   ACT.Exp).then_inc(s["ea_ready"], 1)

                decay_since_start(0)
                decay_since_start(1)
                copy_out(cb_sb[:], "cb", g, view=lambda b: bank(b)[:, 0:TOK])
                copy_out(bn_nat, "bn", g, view=lambda b: bank(b)[:, 0:P])
                for ch in range(TB):
                    copy_out(xs_nat[:, g % 2, ch, :], "xsn", g, ch, view=bank)
                for q in range(1, 5):
                    if q < 3:
                        decay_since_start(q + 1)
                    wait_made("acum", g, q - 1)
                    act.activation(dec[:, 2 * q - 2:2 * q, :], dec[:, 2 * q - 2:2 * q, :],
                                   ACT.Exp).then_inc(s["dec_ready"], 1)
                copy_out(st0, "state", g, view=bank)
                gate(2 * g)

                def last_gates():
                    gate(2 * g + 1)
                    if g == NG - 1:
                        act.activation(xh[:, 0:3, :], qa, ACT.Copy).then_inc(s["latent_high"], 1)
                        act.activation(xh[:, 3:5, :], ckv, ACT.Copy).then_inc(s["latent_high"], 1)

                norm(10 + g, between=last_gates)
            for j in range(8):
                if j == 0:
                    act.wait_ge(s["y_ready"], 2 * NG)
                copy_out(qh[0:QK, 2 * j:2 * j + 2, :], "qh", j, view=lambda b: bank2(b)[0:QK])
                feed(2 if j % 2 else 0)
            for j in range(8):
                copy_out(kh[0:NOPE, 2 * j:2 * j + 2, :], "kh", j, view=lambda b: bank2(b)[0:NOPE])
                if j % 4 == 3:
                    for tb in range(TB):
                        copy_out(vh[:, tb, j // 4 * 512:(j // 4 + 1) * 512], "vh", j // 4 * 2 + tb, view=bank)
            attention(LATENT, CAUSAL, one_tile, lambda i: feed(2 if i in (14, 15) else 0))
            feed(6)
            norm_parts("merged")
            feed(2)
            for j in range(4):
                copy_out(mem[:, 2 * j:2 * j + 2, :], "memT", j)
            squares(8)
            feed(2)
            root(8)
            feed(4)
            norm_parts(8)
            feed(2)
            squares(14)
            for j in range(4):
                copy_out(xk[:, 2 * j:2 * j + 2, :], "xk", j)
                feed(2)
                if j == 1:
                    root(14)
            for j in range(4):
                if j == 3:
                    norm_parts(14)
                copy_out(xv[:, :, j * TOK:(j + 1) * TOK], "xv", j)
                feed(2)

            def queries(j):
                copy_out(xq[:, 2 * j:2 * j + 2, :], "xq", j)
                feed(2)

            queries(0)
            queries(1)
            attention(CROSSED, CROSS, two_tiles, lambda i: queries(i + 2) if i < 2 else None)
            feed(6)
            squares_late(15, 0)
            feed(2)
            u, first = FILL["moe", "first"]
            high_half(first + 2, 0)
            high_half(first + 2, 1)
            root(15)
            act.wait_ge(s["rt_sub"], 1)
            act.activation(rt("ge"), rt("gs"), ACT.Exp).then_inc(s["rt_exp"], 1)
            act.wait_ge(s["rt_sub"], 2)
            act.activation(rt("de"), rt("ds"), ACT.Exp).then_inc(s["rt_exp"], 1)

            def expert(it, n, last=False):
                def f(j, half):
                    high_half(first + j, half, it, 12)
                b = n % 2
                down, gate = (3 * n + 1, 3 * n + 2) if n else (2, 3)
                if n:
                    f(down, 0)
                act.wait_ge(made[b], it * 2 + (u[b] + n // 2 + 1))
                act.activation(sgate[:, b, :], sgate[:, b, :], ACT.Silu).then_inc(s["silu_ready"], 1)
                if n:
                    f(down, 1)
                if n == 0:
                    copy_out(combT, "combT", 0, view=lambda b: bank(b)[0:NE, 0:TOK])
                    wait_made("combT", 0)
                    act.dma_start(comb_dram, combT).then_inc(s["comb_out"], 16)
                    act.wait_ge(s["comb_out"], 16)
                    for e0, e1 in ((0, 1), (1, 8), (8, 16), (16, 24), (24, NE)):
                        src = comb_dram[e0:e1, :].rearrange("(o e) t -> o e t", o=1)
                        act.dma_start(comb_b[:, e0:e1, :], src.to_broadcast([P, e1 - e0, TOK])).then_inc(
                            s["comb_in" if e0 else "comb_first"], 16)
                f(gate, 0)
                f(gate, 1)
                act.wait_ge(s["hid2"], it * 4 + (n + 1))
                act.activation(hid_h[:, b, :], sgate[:, b, :], ACT.Copy).then_inc(s["hid_high"], 1)
                if n and not last:
                    f(3 * n + 3, 0)
                    f(3 * n + 3, 1)

            expert(0, 0)
            with act.Fori(0, 7) as it:
                for n in range(1, 5):
                    expert(it, n)
            for n in range(29, NE):
                expert(0, n, n == NE - 1)
            norm(16)

        @block.vector
        def _(dve):
            steps, ropes = [0], [0]

            def link(ins):
                steps[0] += 1
                ins.then_inc(s["dve_step"], 1)
                dve.wait_ge(s["dve_step"], steps[0])

            def wait_full(*key):
                b, _, n, by_units = FILL[key]
                dve.wait_ge(s["units_done"] if by_units else full[b], n)
                return b

            def wait_made(*key):
                b, n, _, _ = FILL[key]
                dve.wait_ge(made[b], n)

            fed = [0]

            def low_half(n, half, it=0, body=0):
                _, src, high, low = half_views(n, half)
                dve.wait_ge(s["hi_ready"], it * (2 * body) + (2 * n + half + 1))
                dve.tensor_tensor(low, src, high.bitcast(F32), ALU.subtract).then_inc(s["lo_ready"], 1)

            def feed(halves=1):
                for _ in range(halves):
                    low_half(fed[0] // 2, fed[0] % 2)
                    fed[0] += 1

            def low_part(n, k):
                dve.wait_ge(s["xh_ready"], KT * SPLIT_NORMS.index(n) + k + 1)
                dve.tensor_tensor(xl[:, k, :], PLACE.get(n, sq)[:, k, :], xh[:, k, :].bitcast(F32),
                                  ALU.subtract).then_inc(s["xn_ready"], 1)

            def low_parts(n):
                for k in range(KT):
                    low_part(n, k)

            def scaled_norm(n):
                src, tiles, gain, first, _, _ = NORM[n]
                wait_made("norm", n)
                link(dve.reciprocal(std[:, 1, :], std[:, 0, :]))
                for k in range(tiles):
                    dve.scalar_tensor_tensor(PLACE.get(n, sq)[:, k, :], src[:, k, :], col(gain, first + k),
                                             std[:, 1, :], ALU.mult, ALU.mult).then_inc(s["xt_ready"], 1)

            def norm_parts(n, gain, inverse):
                for k in range(KT + 1):
                    if k < KT:
                        dve.scalar_tensor_tensor(sq[:, k, :], x[:, k, :], gain(k), inverse,
                                                 ALU.mult, ALU.mult).then_inc(s["xt_ready"], 1)
                    if k:
                        low_part(n, k - 1)

            def norm(n, halves=0, tail=0):
                src, tiles, gain, first, dst, _ = NORM[n]
                feed(halves)
                wait_made("norm", n)
                link(dve.reciprocal(std[:, 1, :], std[:, 0, :]))
                if n not in SPLIT_NORMS:
                    for k in range(tiles):
                        dve.scalar_tensor_tensor(dst[:, k, :], src[:, k, :], col(gain, first + k), std[:, 1, :],
                                                 ALU.mult, ALU.mult).then_inc(s["xn_ready"], 1)
                    return
                norm_parts(n, lambda k: col(gain, first + k), std[:, 1, :])
                feed(tail)

            def gained(n, j):
                gain, first = NORM[n][2:4]
                for k in (2 * j, 2 * j + 1):
                    dve.tensor_scalar(sq[:, k, :], x[:, k, :], col(gain, first + k), None,
                                      ALU.mult).then_inc(s["xt_ready"], 1)

            def add_to_x(stage, j):
                b = wait_full(stage, j)
                dve.tensor_tensor(x[:, 2 * j:2 * j + 2, :], bank2(b), x[:, 2 * j:2 * j + 2, :],
                                  ALU.add).then_inc(made[b], 1)

            def pair_bcast(t):
                return t.rearrange("p (o t) -> p o t", o=1).to_broadcast([t.shape[0], 2, TOK])

            def rope(key, t, p0, heads=2):
                r = slice(p0, p0 + ROT)
                b = wait_full(*key)
                if heads == 2:
                    swapped, sin_b, cos_b = bank2(b)[r], pair_bcast(sin_t[r, :]), pair_bcast(cos_t[r, :])
                    ta, tb_ = rope_a[r, :, :], rope_b[r, :, :]
                else:
                    swapped, sin_b, cos_b = bank(b)[r, 0:TOK], sin_t[r, :], cos_t[r, :]
                    ta, tb_ = rope_a[r, 0, :], rope_b[r, 0, :]
                if ropes[0]:
                    dve.wait_ge(s["rope_done"], ropes[0])
                ropes[0] += 1
                dve.tensor_tensor(ta, swapped, sin_b, ALU.mult).then_inc(made[b], 1)
                wait_made(*key)
                link(dve.tensor_tensor(tb_, t, cos_b, ALU.mult))
                dve.tensor_tensor(t, ta, tb_, ALU.add).then_inc(s["rope_done"], 1)

            outputs = [0]

            def attention(at, segments, scale, masked, low, meanwhile=None):
                w = segments[-1][1]
                prob = PROB[at]
                norm_lag = at.t_lag - 1
                for i in range(at.heads + at.o_lag):
                    if i < at.heads:
                        n, buf = at.first + i, i % at.bufs
                        b = wait_full("S", n)
                        if i >= at.bufs:
                            wait_full("T", n - at.bufs)
                        if masked:
                            ins = dve.scalar_tensor_tensor(prob[:, buf, 0:w], bank(b)[:, 0:w], scale, mask3,
                                                           ALU.mult, ALU.add)
                        else:
                            ins = dve.tensor_scalar(prob[:, buf, 0:w], bank(b)[:, 0:w], scale, None, ALU.mult)
                        ins.then_inc(made[b], 1)
                        wait_made("S", n)
                        for e, (c0, c1) in enumerate(segments):
                            dve.tensor_reduce(smax[:, n % 3, e:e + 1], prob[:, buf, c0:c1], AX_X, ALU.max,
                                              negate=True).then_inc(s["att_max"], 1)
                    j = i - norm_lag
                    if 0 <= j < at.heads:
                        n, buf = at.first + j, j % at.bufs
                        dve.wait_ge(s["exp_done"], 2 * (n + 1))
                        link(dve.reciprocal(srec[:, n % 3, :], ssum[:, n % 3, :]))
                        for e, (c0, c1) in enumerate(segments):
                            dve.tensor_scalar(prob[:, buf, c0:c1], prob[:, buf, c0:c1], srec[:, n % 3, e:e + 1],
                                              None, ALU.mult).then_inc(s["p_ready"], 1)
                    if meanwhile is not None:
                        meanwhile(i)
                    n = i - at.o_lag
                    if n >= 0 and n % at.pair == at.pair - 1:
                        b = wait_full("O", at.lead(n))
                        outputs[0] += 1
                        dve.wait_ge(s["o_high"], outputs[0])
                        dst, src, high = low(n // at.pair, b)
                        dve.tensor_tensor(dst, src, high.bitcast(F32), ALU.subtract).then_inc(made[b], 1)

            def one_tile(t, b):
                return xl[:, t, :], bank(b)[:, 0:TOK], xh[:, t, :]

            def two_tiles(t, b):
                return xl[:, 2 * t:2 * t + 2, :], bank2(b), xh[:, 2 * t:2 * t + 2, :]

            CAUSAL = ((0, P), (P, 3 * P))
            CROSS = ((0, TOK), (TOK, 2 * TOK))

            dve.memset(eps_col[:, 0:1], EPS)
            link(dve.memset(eps_col[:, 1:2], EPS * EPS))
            dve.memset(zeros[:], 0.0).then_inc(s["zeros_set"], 1)
            for j in range(4):
                b = wait_full("xT", j)
                dve.tensor_copy(x[:, 2 * j:2 * j + 2, :], bank2(b)).then_inc(made[b], 1)
            feed(2)
            b = wait_full("cols", 0)
            link(dve.tensor_copy(cols[:, 0:N_A], bank(b)[:, 0:N_A]))
            dve.tensor_copy(cols[:, P:P + N_B], bank(b)[:, P:P + N_B]).then_inc(made[b], 1)
            wait_made("cols", 0)
            i, j = COL["norm_final"], COL["norm_mix_2"]
            link(dve.tensor_tensor(gain_both[:], cols[:, i:i + KT], cols[:, j:j + KT], ALU.mult))
            for j in range(4):
                gained(0, j)
            low_parts(0)
            feed(4)

            dve.wait_ge(s["pos_in"], 32)
            dve.wait_ge(s["const_in"], 16)
            ang, turns, red, comp = rope_a[:, 0, :], rope_a[:, 1, :], rope_b[:, 0, :], rope_b[:, 1, :]
            magic = 1.5 * 2.0 ** 23
            c1 = 6.28125
            c2 = float(np.float32(round((2 * math.pi - c1) * 2 ** 20) / 2 ** 20))
            c3 = 2 * math.pi - c1 - c2
            link(dve.tensor_copy(ang, pos_i[:]))
            link(dve.tensor_scalar(ang, ang, consts[:, C_INVF:C_INVF + 1], None, ALU.mult))
            link(dve.tensor_scalar(turns, ang, 1 / (2 * math.pi), magic, ALU.mult, ALU.add))
            link(dve.tensor_scalar(turns, turns, magic, None, ALU.subtract))
            link(dve.scalar_tensor_tensor(red, turns, -c1, ang, ALU.mult, ALU.add))
            link(dve.scalar_tensor_tensor(red, turns, -c2, red, ALU.mult, ALU.add))
            link(dve.scalar_tensor_tensor(red, turns, -c3, red, ALU.mult, ALU.add))
            link(dve.tensor_scalar(red, red, 3.1415925, -3.1415925, ALU.min, ALU.max))
            link(dve.scalar_tensor_tensor(comp, red, -1.0, red, ALU.mult, ALU.max))
            dve.tensor_scalar(comp, comp, -1.0, math.pi / 2, ALU.mult, ALU.add).then_inc(s["angle"], 1)
            wait_made("norm", 0)
            dve.reciprocal(std[:, 1, :], std[:, 0, :]).then_inc(s["row_ready"], 1)
            dve.wait_ge(s["row_ready"], 1)
            dve.wait_ge(s["sines"], 2)

            for j in range(9):
                if j < 8:
                    b = wait_full("qk", j)
                    dve.tensor_tensor(qk[:, 2 * j:2 * j + 2, :], bank2(b), pair_bcast(std[:, 1, :]),
                                      ALU.mult).then_inc(made[b], 1)
                if j < 7:
                    feed(2)
                if j:
                    rope(("rope1", j - 1), qk[0:ROT, 2 * j - 2:2 * j, :], 0)
            feed(8)
            attention(MOBA, CAUSAL, float(P) ** -0.5, True, one_tile)
            for j in range(4):
                add_to_x("wo1", j)
                wait_made("wo1", j)
                gained(1, j)
                feed(2 if j < 3 else 0)
            feed(2)
            low_parts(1)

            scaled = (rope_a[:], rope_b[:])

            def mlp_square(i):
                u, first = FILL[f"mlp{i}", "first"]

                def step(it, n, last=False):
                    def f(j, half):
                        low_half(first + j, half, it, 8)
                    b = n % 2
                    f(2 * n + 1 if n else 2, 0)
                    dve.wait_ge(s["gate_silu"], it * 4 + (FC * i + n + 1))
                    dve.scalar_tensor_tensor(sgate[:, b, :], bank(b), 0.0, sgate[:, b, :], ALU.max,
                                             ALU.mult).then_inc(made[b], 1)
                    f(2 * n + 1 if n else 2, 1)
                    dve.wait_ge(s["hid_high"], it * 4 + (FC * i + n + 1))
                    dve.tensor_tensor(hid_l[:, b, :], sgate[:, b, :], hid_h[:, b, :].bitcast(F32),
                                      ALU.subtract).then_inc(s["hid_ready"], 1)
                    if n and not last:
                        f(2 * n + 2, 0)
                        f(2 * n + 2, 1)

                step(0, 0)
                with dve.Fori(0, 3) as it:
                    for n in range(1, 5):
                        step(it, n)
                wait_made("norm", 2 * i + 1)
                link(dve.reciprocal(std[:, 1, :], std[:, 0, :]))
                link(dve.tensor_tensor(std[:, 1, :], std[:, 1, :], std[:, 1, :], ALU.mult))
                for n in range(13, FC):
                    step(0, n, n == FC - 1)
                fed[0] += 4 * FC - 4
                feed(2)
                for j in range(5):
                    if j < 4:
                        b = wait_full(f"mlp{i}y", j)
                        if j >= 2:
                            wait_made(f"mlp{i}y", j - 2)
                        dve.tensor_tensor(scaled[j % 2], bank2(b), pair_bcast(std[:, 1, :]),
                                          ALU.mult).then_inc(s["y_scaled"], 1)
                    if j:
                        b = FILL[f"mlp{i}y", j - 1][0]
                        dve.wait_ge(s["y_scaled"], 4 * i + j)
                        pair = x[:, 2 * j - 2:2 * j, :]
                        dve.tensor_tensor(pair, pair, scaled[(j - 1) % 2], ALU.add).then_inc(made[b], 1)
                        if i == 0:
                            wait_made(f"mlp{i}y", j - 1)
                            gained(2, j - 1)
                            if j > 1:
                                low_part(2, 2 * j - 4)
                                low_part(2, 2 * j - 3)

            mlp_square(0)
            low_part(2, KT - 2)
            low_part(2, KT - 1)
            feed(2)
            wait_made("norm", 2)
            dve.reciprocal(std_col[:, 1, :], std_col[:, 0, :]).then_inc(s["col_ready"], 1)
            for g in range(4):
                b = wait_full("pooly", g)
                for m in range(2):
                    ins = dve.scalar_tensor_tensor(x[:, 2 * g + m, :], bank2(b)[:, m, :], col("pool_scale", 2 * g + m),
                                                   x[:, 2 * g + m, :], ALU.mult, ALU.add)
                ins.then_inc(made[b], 1)
                wait_made("pooly", g)
                gained(3, g)
                if g == 0:
                    feed()
            feed(1)
            low_parts(3)
            mlp_square(1)

            feed(2)
            wait_full("norm", 4)
            b = wait_full("norm", 5)
            dve.tensor_copy(std[:, 2, :], bank(b)[:, 0:TOK]).then_inc(s["dve_both"], 1)
            dve.wait_ge(s["dve_both"], 1)
            dve.scalar_tensor_tensor(std[:, 2, :], bank(FILL["norm", 4][0])[:, 0:TOK], EPS, std[:, 2, :], ALU.mult,
                                     ALU.add).then_inc(made[b], 1)
            dve.wait_ge(s["both_ready"], 1)
            link(dve.reciprocal(std[:, 2, :], std[:, 2, :]))
            norm_parts(5, lambda k: gain_both[:, k:k + 1], std[:, 2, :])
            wait_made("norm", 4)
            link(dve.reciprocal(std[:, 1, :], std[:, 0, :]))
            for k in range(KT):
                dve.scalar_tensor_tensor(x[:, k, :], x[:, k, :], col("norm_final", k), std[:, 1, :],
                                         ALU.mult, ALU.mult).then_inc(s["xn_ready"], 1)

            dve.wait_ge(s["par_in"], 48)
            for half in range(2):
                r = slice(64 * half, 64 * half + 64)
                link(dve.tensor_copy(dskip[r, :], dskip_all[r, :].rearrange("p (t h) -> p t h", h=2)[:, :, half]))
            feed()
            b = wait_full("small", 0)
            dve.tensor_scalar(dta[:, 0, :], bank(b)[0:SH, 0:TOK], ssd_par[:, 0:1], None, ALU.add).then_inc(s["dt_u"], 1)
            dve.wait_ge(s["dt_u"], 1)
            dve.scalar_tensor_tensor(dtt[:, 1, :], dta[:, 0, :], -1.0, dta[:, 0, :], ALU.mult,
                                     ALU.max).then_inc(s["dt_u"], 1)
            feed(5)
            e, den, z, z2 = dtt[:, 0, :], dtt[:, 1, :], dtt[:, 2, :], dtt[:, 3, :]
            poly = den

            def series(*odds):
                for k in odds:
                    link(dve.scalar_tensor_tensor(poly, poly, 1 / k, z2, ALU.add, ALU.mult))

            def softplus(part):
                if part == 0:
                    dve.wait_ge(s["dt_e"], 2)
                    link(dve.tensor_scalar(den, e, 2.0, None, ALU.add))
                    link(dve.reciprocal(den, den))
                    link(dve.tensor_tensor(z, e, den, ALU.mult))
                if part == 1:
                    link(dve.tensor_tensor(z2, z, z, ALU.mult))
                    link(dve.tensor_scalar(poly, z2, 1 / 15, None, ALU.mult))
                    series(13)
                if part == 2:
                    series(11, 9, 7)
                if part == 3:
                    series(5, 3)
                    link(dve.scalar_tensor_tensor(poly, poly, 1.0, z, ALU.add, ALU.mult))
                if part == 4:
                    link(dve.tensor_scalar(z, dta[:, 0, :], 0.0, None, ALU.max))
                    link(dve.scalar_tensor_tensor(dta[:, 0, :], poly, 2.0, z, ALU.mult, ALU.add))
                    link(dve.tensor_scalar(dtt[:, 1, :], dta[:, 0, :], ssd_par[:, 2:3], -1.0, ALU.mult, ALU.mult))
                if part == 5:
                    for ch in range(TB):
                        t = slice(ch * P, (ch + 1) * P)
                        ins = dve.tensor_tensor_scan(dta[:, 1, t], consts[0:SH, C_ONE:C_ONE + P], dtt[:, 1, t], 0.0,
                                                     ALU.mult, ALU.add)
                    ins.then_inc(s["dt_u"], 1)

            def conv(j):
                b = wait_full("xbc", j)
                dve.wait_ge(s["conv_first"], j + 1)
                for m in range(2):
                    t = 2 * j + m
                    acc, u = convb[:, t % 4, :], bank2(b)[:, m, :]
                    for tap in (2, 1, 0):
                        sh = CONV - 1 - tap
                        ins = dve.scalar_tensor_tensor(acc[:, sh:], u[:, 0:TOK - sh], col("conv_w_2", tap * (XBC // P) + t),
                                                       acc[:, sh:], ALU.mult, ALU.add)
                        if tap:
                            link(ins)
                    if m == 0:
                        link(ins)
                ins.then_inc(made[b], 1)

            for j in range(12):
                feed()
                conv(j)
                feed()
                if j == 0:
                    rope(("ropek", 0), kpe[64:64 + ROT, :], 64, 1)
                if j == 1:
                    norm(6)
                    norm(7)
                if 2 <= j < 8:
                    softplus(j - 2)
                if j == 9:
                    dve.wait_ge(s["acum_high"], 1)
                    dve.tensor_tensor(acum_parts[SH:2 * SH, :], dta[:, 1, :], acum_parts[0:SH, :].bitcast(F32),
                                      ALU.subtract).then_inc(s["acum_low"], 1)
                    dve.wait_ge(s["dt_e"], 3)
                    dve.tensor_tensor(dtt[:, 3, 0:P], dtt[:, 2, 0:P], dta[:, 0, 0:P], ALU.mult).then_inc(s["dt_ready"], 1)

            feed(16)

            wait_made("dtT", 0)
            for g in range(NG):
                if g:
                    wait_full("y", g - 1, 0)
                    wait_full("y", g - 1, 1)
                for q in range(4):
                    dve.wait_ge(s["ea_ready"], 4 * g + q + 1)
                    b = wait_full("acum", g, q)
                    for hh in range(2):
                        for ch in range(TB):
                            h = HPG * g + 2 * q + hh
                            ins = dve.scalar_tensor_tensor(dec[:, 2 * q + hh, ch * P:(ch + 1) * P],
                                                           bank2(b)[:, hh, ch * P:(ch + 1) * P], dtn[:, ch, h:h + 1],
                                                           cap, ALU.subtract, ALU.min)
                    ins.then_inc(made[b], 1)
                wait_made("cb", g)
                for h in range(HPG):
                    dve.wait_ge(s["dec_ready"], 4 * g + h // 2 + 1)
                    for ch in range(TB):
                        d = dec[:, h, ch * P:(ch + 1) * P]
                        ins = dve.scalar_tensor_tensor(d, d, dtn[:, 2 + ch, HPG * g + h:HPG * g + h + 1],
                                                       cb_sb[:, ch * P:(ch + 1) * P], ALU.mult, ALU.mult)
                    ins.then_inc(s["m_ready"], 1)
                feed(2)
                for half in range(2):
                    b = wait_full("y", g, half)
                    for m in range(2):
                        t = 4 * g + 2 * half + m
                        ins = dve.scalar_tensor_tensor(rope_a[:, m, :], xbc[:, t, :], dskip[:, t:t + 1],
                                                       bank2(b)[:, m, :], ALU.mult, ALU.add)
                    ins.then_inc(made[b], 1)
                    wait_made("y", g, half)
                    zt = zs[:, 4 * g + 2 * half:4 * g + 2 * half + 2, :]
                    dve.tensor_tensor(zt, rope_a[:], zt, ALU.mult).then_inc(s["y_ready"], 1)
                    if half == 0:
                        dve.wait_ge(s["y_ready"], 2 * g + 1)
                feed(2)
                if g == NG - 1:
                    for i, (k0, k1, src) in enumerate(((0, 3, qa), (3, 5, ckv))):
                        dve.wait_ge(s["latent_high"], i + 1)
                        dve.tensor_tensor(xl[:, k0:k1, :], src, xh[:, k0:k1, :].bitcast(F32),
                                          ALU.subtract).then_inc(s["latent_low"], 1)
                norm(10 + g)
            for j in range(8):
                feed(2 if j % 2 else 0)
                rope(("rope2", j), qh[64:64 + ROT, 2 * j:2 * j + 2, :], 64)
            attention(LATENT, CAUSAL, float(QK) ** -0.5, True, one_tile, lambda i: feed(2 if i in (14, 15) else 0))
            for j in range(4):
                b = wait_full("souty", j)
                dve.tensor_tensor(merged[:, 2 * j:2 * j + 2, :], bank2(b), gates[:, 2 * j:2 * j + 2, :],
                                  ALU.mult).then_inc(made[b], 1)
            for j in range(4):
                feed(2 if j < 3 else 0)
                b = wait_full("mout", j)
                if j:
                    dve.wait_ge(s["y_ready"], 2 * NG + j)
                dve.tensor_tensor(rope_a[:], bank2(b), gates[:, KT + 2 * j:KT + 2 * j + 2, :],
                                  ALU.mult).then_inc(made[b], 1)
                wait_made("mout", j)
                dve.tensor_tensor(merged[:, 2 * j:2 * j + 2, :], merged[:, 2 * j:2 * j + 2, :], rope_a[:],
                                  ALU.add).then_inc(s["y_ready"], 1)
            low_parts("merged")
            feed(4)
            for j in range(4):
                add_to_x("wo2", j)
                if j == 1:
                    scaled_norm(8)
                feed(2 if j < 2 else 0)
            low_parts(8)
            feed(6)
            scaled_norm(14)
            feed(10)
            low_parts(14)
            feed(6)
            attention(CROSSED, CROSS, float(TOK) ** -0.5, False, two_tiles, lambda i: feed(2 if i < 2 else 0))
            for j in range(4):
                add_to_x("xo", j)
                wait_made("xo", j)
                gained(15, j)
                feed(2 if j < 3 else 0)
            low_parts(15)
            feed(2)
            u, first = FILL["moe", "first"]
            low_half(first + 2, 0)
            low_half(first + 2, 1)
            wait_made("norm", 15)
            dve.reciprocal(std[:, 1, :], std[:, 0, :]).then_inc(s["row_ready"], 1)
            b = wait_full("column", 1)
            dve.tensor_copy(std_col[:, 1, :], bank(b)[:, 0:TB]).then_inc(made[b], 1)
            wait_made("column", 1)

            def first_of(eq, n, iota, cand, m, onehot):
                link(dve.scalar_tensor_tensor(cand, eq, -float(n), iota, ALU.mult, ALU.add))
                link(dve.tensor_reduce(m, cand, AX_X, ALU.min))
                link(dve.tensor_tensor(onehot, cand, m.to_broadcast([P, TB, n]), ALU.is_equal))

            def spread(t, n):
                return t.to_broadcast([P, TB, n])

            b = wait_full("logits", 0)
            lg = rt("logits")
            for tb in range(TB):
                ins = dve.scalar_tensor_tensor(lg[:, tb, :], bank(b)[:, tb * (EG + NE):(tb + 1) * (EG + NE)],
                                               std_col[:, 1, tb:tb + 1], router_b[:], ALU.mult, ALU.add)
            ins.then_inc(made[b], 1)
            wait_made("logits", 0)
            iota = consts[:, C_IOTA:C_IOTA + EPG].rearrange("p (o e) -> p o e", o=1).to_broadcast([P, TB, EPG])
            glog = lg[:, :, 0:EG]
            link(dve.tensor_reduce(rt("gmax"), glog, AX_X, ALU.max))
            dve.tensor_tensor(rt("gs"), glog, spread(rt("gmax"), EG), ALU.subtract).then_inc(s["rt_sub"], 1)
            link(dve.tensor_tensor(rt("geq"), glog, spread(rt("gmax"), EG), ALU.is_equal))
            first_of(rt("geq"), EG, iota[:, :, 0:EG], rt("gcand"), rt("gm"), rt("goh"))
            pick = rt("pick").rearrange("p b (g e) -> p b g e", g=EG)
            goh4 = rt("goh").rearrange("p b (g o) -> p b g o", o=1).to_broadcast([P, TB, EG, EPG])
            link(dve.tensor_tensor(pick, lg[:, :, EG:].rearrange("p b (g e) -> p b g e", g=EG), goh4, ALU.mult))
            link(dve.tensor_reduce(rt("ein"), pick.rearrange("p b g e -> p b e g"), AX_X, ALU.add))
            link(dve.tensor_reduce(rt("v1"), rt("ein"), AX_X, ALU.max))
            link(dve.tensor_tensor(rt("eq1"), rt("ein"), spread(rt("v1"), EPG), ALU.is_equal))
            first_of(rt("eq1"), EPG, iota, rt("cand"), rt("m"), rt("oh1"))
            link(dve.scalar_tensor_tensor(rt("rest"), rt("oh1"), NEG, rt("ein"), ALU.mult, ALU.add))
            link(dve.tensor_reduce(rt("v2"), rt("rest"), AX_X, ALU.max))
            dve.tensor_tensor(rt("ds"), rt("v2"), rt("v1"), ALU.subtract).then_inc(s["rt_sub"], 1)
            link(dve.tensor_tensor(rt("eq2"), rt("rest"), spread(rt("v2"), EPG), ALU.is_equal))
            first_of(rt("eq2"), EPG, iota, rt("cand"), rt("m"), rt("oh2"))
            dve.wait_ge(s["rt_exp"], 2)
            link(dve.tensor_reduce(rt("gsum"), rt("ge"), AX_X, ALU.add))
            link(dve.reciprocal(rt("gw"), rt("gsum")))
            link(dve.tensor_tensor(rt("gw"), rt("gw"), std_col[:, 1, :].rearrange("p (b o) -> p b o", o=1), ALU.mult))
            link(dve.tensor_scalar(rt("dsum"), rt("de"), 1.0, None, ALU.add))
            link(dve.reciprocal(rt("w1"), rt("dsum")))
            link(dve.tensor_tensor(rt("w2"), rt("de"), rt("w1"), ALU.mult))
            link(dve.tensor_tensor(rt("oh1"), rt("oh1"), spread(rt("w1"), EPG), ALU.mult))
            link(dve.tensor_tensor(rt("oh2"), rt("oh2"), spread(rt("w2"), EPG), ALU.mult))
            link(dve.tensor_tensor(rt("oh1"), rt("oh1"), rt("oh2"), ALU.add))
            link(dve.tensor_tensor(rt("oh1"), rt("oh1"), spread(rt("gw"), EPG), ALU.mult))
            w_e = rt("oh1").rearrange("p b (o e) -> p b o e", o=1).to_broadcast([P, TB, EG, EPG])
            dve.tensor_tensor(rt("comb").rearrange("p b (g e) -> p b g e", g=EG), goh4, w_e,
                              ALU.mult).then_inc(s["comb_t"], 1)

            def expert(it, n, last=False):
                def f(j, half):
                    low_half(first + j, half, it, 12)
                b = n % 2
                down, gate = (3 * n + 1, 3 * n + 2) if n else (2, 3)
                if n:
                    f(down, 0)
                dve.wait_ge(s["units_done"], it * 24 + 2 * (first + (3 * n - 1 if n else 0)) + 2)
                dve.tensor_tensor(sgate[:, b, :].rearrange("p (k t) -> p k t", k=2), bank2(b), pair_bcast(std[:, 1, :]),
                                  ALU.mult).then_inc(made[b], 1)
                if n:
                    f(down, 1)
                f(gate, 0)
                f(gate, 1)
                dve.wait_ge(s["silu_ready"], it * 4 + (n + 1))
                dve.wait_ge(s["units_done"], it * 24 + 2 * (first + (3 * n if n else 1)) + 2)
                dve.tensor_tensor(sgate[:, b, :], sgate[:, b, :], bank(2 + b), ALU.mult).then_inc(made[2 + b], 1)
                dve.wait_ge(made[2 + b], it * 2 + (u[2 + b] + n // 2 + 1))
                if n < 2:
                    dve.wait_ge(s["comb_in" if n else "comb_first"], 64 if n else 16)
                cw = comb_b[:, bass.ds(it * 4 + n, 1), :].to_broadcast([P, 2, TOK])
                h2 = sgate[:, b, :].rearrange("p (k t) -> p k t", k=2)
                dve.tensor_tensor(h2, h2, cw, ALU.mult).then_inc(s["hid2"], 1)
                dve.wait_ge(s["hid_high"], it * 4 + (2 * FC + n + 1))
                dve.tensor_tensor(hid_l[:, b, :], sgate[:, b, :], hid_h[:, b, :].bitcast(F32),
                                  ALU.subtract).then_inc(s["hid_ready"], 1)
                if n and not last:
                    f(3 * n + 3, 0)
                    f(3 * n + 3, 1)

            expert(0, 0)
            with dve.Fori(0, 7) as it:
                for n in range(1, 5):
                    expert(it, n)
            for n in range(29, NE):
                expert(0, n, n == NE - 1)
            for j in range(4):
                add_to_x("moey", j)
            norm(16)
            for j in range(4):
                b = wait_full("outT", j)
                dve.tensor_copy(yout[:, j // 2, (j % 2) * 512:(j % 2 + 1) * 512], bank(b)).then_inc(made[b], 1)

        @block.gpsimd
        def _(pool):
            def wait_full(*key):
                b, _, n, _ = FILL[key]
                pool.wait_ge(full[b], n)

            def wait_made(*key):
                b, n, _, _ = FILL[key]
                pool.wait_ge(made[b], n)

            folds = [0]

            def fold(n, squares):
                pool.wait_ge(s["sq_ready"], SQ_NO[n] + KT // 2)
                for half in (4, 2, 1):
                    ins = pool.tensor_tensor(squares[:, 0:half, :], squares[:, 0:half, :],
                                             squares[:, half:2 * half, :], ALU.add)
                    if half > 1:
                        folds[0] += 1
                        ins.then_inc(s["fold_step"], 1)
                        pool.wait_ge(s["fold_step"], folds[0])
                ins.then_inc(s["folded"], 1)

            fold(1, sq_late)
            fold(3, sq_late)
            wait_made("dtT", 0)
            for g in range(NG):
                wait_made("xsn", g, 0)
                if g:
                    wait_full("state", g - 1)
                xg = xs_nat[:, g % 2, 0, :].rearrange("p (h c) -> p h c", c=64)
                wg = dtn[:, 4, HPG * g:HPG * (g + 1)].rearrange("p (h o) -> p h o", o=1).to_broadcast([P, HPG, 64])
                pool.tensor_tensor(xw.rearrange("p (h c) -> p h c", c=64), xg, wg, ALU.mult).then_inc(s["xw_ready"], 1)
                pool.wait_ge(s["ea_ready"], 4 * (g + 1))
                cg = xbc[:, ZT + NG + g, P:TOK].rearrange("p (o t) -> p o t", o=1).to_broadcast([P, HPG, P])
                pool.tensor_tensor(eac, eac, cg, ALU.mult).then_inc(s["cs_ready"], 1)
            pool.wait_ge(s["y_ready"], 2 * NG)
            pool.wait_ge(s["rope_done"], 9)
            kb = kpe[64:64 + ROT, :].rearrange("p (o t) -> p o t", o=1).to_broadcast([ROT, MH, TOK])
            pool.tensor_copy(kh[64:64 + ROT, :, :], kb).then_inc(s["kpe_copied"], 1)
            fold(8, sq)
            fold(14, sq)


_INS = ["x", "positions", "norm_mix", "norm_mlp", "attn_w_qkv", "attn_w_o", "pool_w", "pool_scale",
        "mlp_w_up", "mlp_w_down", "norm_final", "mem_2", "positions_2", "norm_mix_2", "w_in_2", "conv_w_2",
        "conv_b_2", "dt_bias_2", "a_log_2", "d_skip_2", "ssd_norm_2", "w_ssd_out_2", "q_a_norm_2", "w_q_b_2",
        "kv_a_norm_2", "w_kv_b_2", "w_mla_out_2", "w_o_2", "norm_xattn_2", "norm_mem_2", "w_xq_2", "w_xkv_2",
        "w_xo_2", "norm_moe_2", "w_router_group_2", "b_router_group_2", "w_router_expert_2",
        "b_router_expert_2", "w_exp_gate_2", "w_exp_up_2", "w_exp_down_2", "norm_final_2"]


def kernel(**inputs):
    import numpy as _np
    import concourse.bacc as _bacc
    from concourse import mybir as _mybir
    from concourse.bass_utils import run_bass_kernel_spmd as _run

    nc = _bacc.Bacc("TRN2", target_bir_lowering=False, num_devices=1)
    arrays = {f"in_{name}": _np.ascontiguousarray(inputs[name]) for name in _INS}
    arrays["in_consts"] = const_array()
    arrays["in_band"] = band_array()
    args = {name[3:]: nc.dram_tensor(name, v.shape, _mybir.dt.from_np(v.dtype), kind="ExternalInput").ap()
            for name, v in arrays.items()}
    out = nc.dram_tensor("out", (1, TOK, D), _mybir.dt.float32, kind="ExternalOutput").ap()
    build_two_blocks(nc, args, out)
    return _run(nc, [arrays], core_ids=[0]).results[0]["out"]
```
